# Optimizing a Trainium2 kernel written in Bass

```python
import math
import jax
import jax.numpy as jnp
from jax import lax
import numpy as np

D_MODEL = 1024
BATCH = 1
SEQ = 512
DEPTH = 2
DEC_BATCH = 8
DEC_SEQ = 8
PAST_LEN = 4096
PAGE_SIZE = 128

N_EVEN = (DEPTH + 1) // 2
N_ODD = DEPTH // 2
HALF = D_MODEL // 2
MLSTM_HEADS = 4
MLSTM_HD = HALF // MLSTM_HEADS
RWKV_HD = 64
RWKV_HEADS = HALF // RWKV_HD
RWKV_W_LORA = 64
RWKV_A_LORA = 64
RWKV_G_LORA = 128
GLA_HEADS = 4
GLA_DK = HALF // 2 // GLA_HEADS
GLA_DV = HALF // GLA_HEADS
GLA_QK = GLA_HEADS * GLA_DK
GLA_GATE_RANK = 16
GLA_TAU = 16.0
S5_CH = HALF
S5_GROUP = 16
S5_GROUPS = S5_CH // S5_GROUP
S5_P = 64
D_FF = ((8 * D_MODEL // 3 + 255) // 256) * 256
CONV_W = 3
CHUNK = 64
EPS = 1e-6
RWKV_LN_EPS = 64e-5
M_INIT = -1e30
MLSTM_COLS = 4 * HALF + 2 * MLSTM_HEADS
RWKV_COLS = 3 * HALF + RWKV_W_LORA + RWKV_A_LORA + RWKV_G_LORA
EVEN_COLS = MLSTM_COLS + RWKV_COLS
GLA_COLS = 2 * GLA_QK + 2 * HALF + GLA_GATE_RANK
ODD_COLS = GLA_COLS + S5_CH

kernel_name = 'hybrid_mlstm_rwkv7_gla_s5_step'

def rms_norm(x, g):
    xf = x.astype(jnp.float32)
    y = xf * lax.rsqrt(jnp.mean(xf * xf, -1, keepdims=True) + EPS)
    return (y * g.astype(jnp.float32)).astype(x.dtype)

def head_layer_norm(x, g, b, eps):
    mu = jnp.mean(x, -1, keepdims=True)
    xc = x - mu
    y = xc * lax.rsqrt(jnp.mean(xc * xc, -1, keepdims=True) + eps)
    y = y * g.astype(jnp.float32).reshape(x.shape[-2:])
    if b is not None:
        y = y + b.astype(jnp.float32).reshape(x.shape[-2:])
    return y

def head_rms_norm(x, g):
    y = x * lax.rsqrt(jnp.mean(x * x, -1, keepdims=True) + EPS)
    return y * g.astype(jnp.float32).reshape(x.shape[-2:])

def to_heads(t, n_heads):
    b, s, _ = t.shape
    return t.reshape(b, s, n_heads, -1).transpose(0, 2, 1, 3)

def to_chunks(a, L):
    s = a.shape
    a = a.reshape(s[:2] + (s[2] // L, L) + s[3:])
    return jnp.moveaxis(a, 2, 0)

def from_chunks(a):
    a = jnp.moveaxis(a, 0, 2)
    s = a.shape
    return a.reshape(s[:2] + (s[2] * s[3],) + s[4:])

def mlstm_chunked(q, k, v, i_log, f_log, C0, n0, m0):
    T = q.shape[2]
    L = math.gcd(T, CHUNK)
    causal = jnp.tril(jnp.ones((L, L), dtype=bool))

    def step(carry, xs):
        C, n, m = carry
        qc, kc, vc, ic, fc = xs
        b = jnp.cumsum(fc, -1)
        dlog = jnp.where(causal, b[..., :, None] - b[..., None, :] + ic[..., None, :], -jnp.inf)
        inter = b + m[..., None]
        m_t = jnp.maximum(inter, jnp.max(dlog, -1))
        w = jnp.exp(dlog - m_t[..., None])
        s_inter = jnp.exp(inter - m_t)
        qk = jnp.einsum('bhtd,bhsd->bhts', qc, kc) * w
        num = s_inter[..., None] * jnp.einsum('bhvd,bhtd->bhtv', C, qc) + jnp.einsum('bhts,bhsv->bhtv', qk, vc)
        den = s_inter * jnp.einsum('bhd,bhtd->bht', n, qc) + jnp.sum(qk, -1)
        h = num / jnp.maximum(jnp.abs(den), jnp.exp(-m_t))[..., None]
        m_new = m_t[..., -1]
        wl = jnp.exp(b[..., -1:] - b + ic - m_new[..., None])
        dec = jnp.exp(b[..., -1] + m - m_new)
        C_new = dec[..., None, None] * C + jnp.einsum('bhs,bhsv,bhsd->bhvd', wl, vc, kc)
        n_new = dec[..., None] * n + jnp.einsum('bhs,bhsd->bhd', wl, kc)
        return (C_new, n_new, m_new), h

    xs = (to_chunks(q, L), to_chunks(k, L), to_chunks(v, L), to_chunks(i_log, L), to_chunks(f_log, L))
    (C, n, m), h = lax.scan(step, (C0, n0, m0), xs)
    return from_chunks(h), C, n, m

def rwkv7_recurrence(r, w, k, v, kk, a, S0):
    def step(S, xs):
        rt, wt, kt, vt, kkt, at = xs
        sa = jnp.einsum('bhvk,bhk->bhv', S, -kkt)
        S = S * wt[:, :, None, :] + sa[..., None] * (kkt * at)[:, :, None, :] + vt[..., None] * kt[:, :, None, :]
        return S, jnp.einsum('bhvk,bhk->bhv', S, rt)

    xs = (jnp.moveaxis(r, 1, 0), jnp.moveaxis(w, 1, 0), jnp.moveaxis(k, 1, 0),
          jnp.moveaxis(v, 1, 0), jnp.moveaxis(kk, 1, 0), jnp.moveaxis(a, 1, 0))
    S, y = lax.scan(step, S0, xs)
    return jnp.moveaxis(y, 0, 1), S

def gla_chunked(q, k, v, la, S0):
    T = q.shape[2]
    L = math.gcd(T, CHUNK)
    causal = jnp.tril(jnp.ones((L, L), dtype=bool))[:, :, None]

    def step(S, xs):
        qc, kc, vc, lc = xs
        bc = jnp.cumsum(lc, axis=2)
        inter = jnp.einsum('bhtd,bhdv->bhtv', qc * jnp.exp(bc), S)
        diff = jnp.where(causal, bc[:, :, :, None, :] - bc[:, :, None, :, :], -jnp.inf)
        att = jnp.einsum('bhtd,bhsd,bhtsd->bhts', qc, kc, jnp.exp(diff))
        o = inter + jnp.einsum('bhts,bhsv->bhtv', att, vc)
        bl = bc[:, :, -1]
        S = jnp.exp(bl)[..., None] * S + jnp.einsum('bhsd,bhsv->bhdv', kc * jnp.exp(bl[:, :, None] - bc), vc)
        return S, o

    S, o = lax.scan(step, S0, (to_chunks(q, L), to_chunks(k, L), to_chunks(v, L), to_chunks(la, L)))
    return from_chunks(o), S

def s5_scan(u, lam_re, lam_im, log_step, b_re, b_im, c_re, c_im, d_skip, x_re0, x_im0):
    f32 = jnp.float32
    bsz, T, _ = u.shape
    ug = u.reshape(bsz, T, S5_GROUPS, S5_GROUP).astype(jnp.complex64)
    lam = lax.complex(lam_re.astype(f32), lam_im.astype(f32))
    lam_bar = jnp.exp(lam * jnp.exp(log_step.astype(f32))[:, None])
    b_bar = ((lam_bar - 1.0) / lam)[..., None] * lax.complex(b_re.astype(f32), b_im.astype(f32))
    bu = jnp.einsum('gpc,btgc->btgp', b_bar, ug)
    x0 = lax.complex(x_re0.astype(f32), x_im0.astype(f32))
    bu = bu.at[:, 0].add(lam_bar * x0)
    a = jnp.broadcast_to(lam_bar, bu.shape)

    def combine(e1, e2):
        a1, b1 = e1
        a2, b2 = e2
        return a1 * a2, a2 * b1 + b2

    _, xs = lax.associative_scan(combine, (a, bu), axis=1)
    cmat = lax.complex(c_re.astype(f32), c_im.astype(f32))
    y = jnp.real(jnp.einsum('gcp,btgp->btgc', cmat, xs)).reshape(bsz, T, S5_CH) + d_skip.astype(f32) * u
    x_last = xs[:, -1]
    return y, jnp.real(x_last), jnp.imag(x_last)

def even_mixer(h, state, p):
    C0, n0, m0, S0, shift0 = state
    (w_in, b_if, mu, w0, w_up, a0, a_up, g_up, k_k, k_a, r_k, ln_m_g, ln_r_g, ln_r_b, w_out) = p
    f32 = jnp.float32
    bsz, T, _ = h.shape
    z = jnp.matmul(h, w_in).astype(f32)
    zm, zr = z[..., :MLSTM_COLS], z[..., MLSTM_COLS:]
    q = to_heads(zm[..., :HALF], MLSTM_HEADS)
    k = to_heads(zm[..., HALF:2 * HALF], MLSTM_HEADS) * (MLSTM_HD ** -0.5)
    v = to_heads(zm[..., 2 * HALF:3 * HALF], MLSTM_HEADS)
    o_gate = jax.nn.sigmoid(zm[..., 3 * HALF:4 * HALF])
    gates = zm[..., 4 * HALF:] + b_if.astype(f32)
    i_log = jnp.swapaxes(gates[..., :MLSTM_HEADS], 1, 2)
    f_log = jnp.swapaxes(jax.nn.log_sigmoid(gates[..., MLSTM_HEADS:]), 1, 2)
    hm, C, n, m = mlstm_chunked(q, k, v, i_log, f_log, C0.astype(f32), n0.astype(f32), m0.astype(f32))
    hm = head_layer_norm(jnp.swapaxes(hm, 1, 2), ln_m_g, None, EPS)
    y_m = o_gate * hm.reshape(bsz, T, HALF)
    prev = jnp.concatenate([shift0.astype(f32)[:, None], zr[:, :-1]], axis=1)
    zs = zr + (prev - zr) * mu.astype(f32)
    new_shift = zr[:, -1]
    o1 = 3 * HALF
    o2 = o1 + RWKV_W_LORA
    o3 = o2 + RWKV_A_LORA
    r = zs[..., :HALF]
    kr = zs[..., HALF:2 * HALF]
    vr = zs[..., 2 * HALF:3 * HALF]
    w_log = -jax.nn.softplus(-(w0 + jnp.matmul(jnp.tanh(zs[..., o1:o2]), w_up))) - 0.5
    decay = jnp.exp(-jnp.exp(w_log))
    a = jax.nn.sigmoid(a0 + jnp.matmul(zs[..., o2:o3], a_up))
    g = jnp.matmul(jax.nn.sigmoid(zs[..., o3:]), g_up)
    kk = (kr * k_k).reshape(bsz, T, RWKV_HEADS, RWKV_HD)
    kk = kk * lax.rsqrt(jnp.maximum(jnp.sum(kk * kk, -1, keepdims=True), 1e-24))
    kr = kr * (1.0 + (a - 1.0) * k_a)
    shp = (bsz, T, RWKV_HEADS, RWKV_HD)
    r4, k4, v4 = r.reshape(shp), kr.reshape(shp), vr.reshape(shp)
    yr, S = rwkv7_recurrence(r4, decay.reshape(shp), k4, v4, kk, a.reshape(shp), S0.astype(f32))
    yr = head_layer_norm(yr, ln_r_g, ln_r_b, RWKV_LN_EPS)
    yr = yr + jnp.sum(r4 * k4 * r_k.astype(f32).reshape(RWKV_HEADS, RWKV_HD), -1, keepdims=True) * v4
    y_r = yr.reshape(bsz, T, HALF) * g
    y = jnp.matmul(jnp.concatenate([y_m, y_r], -1), w_out)
    return y, (C, n, m, S, new_shift)

def odd_mixer(h, state, p):
    S0, x_re0, x_im0 = state
    (w_in, a_up, a_b, ln_g, lam_re, lam_im, log_step, b_re, b_im, c_re, c_im, d_skip, w_glu, w_out) = p
    f32 = jnp.float32
    bsz, T, _ = h.shape
    z = jnp.matmul(h, w_in).astype(f32)
    q = to_heads(z[..., :GLA_QK], GLA_HEADS) * (GLA_DK ** -0.5)
    k = to_heads(z[..., GLA_QK:2 * GLA_QK], GLA_HEADS)
    v = to_heads(z[..., 2 * GLA_QK:2 * GLA_QK + HALF], GLA_HEADS)
    g = z[..., 2 * GLA_QK + HALF:2 * GLA_QK + 2 * HALF]
    a_down = z[..., 2 * GLA_QK + 2 * HALF:GLA_COLS]
    la = to_heads(jax.nn.log_sigmoid(jnp.matmul(a_down, a_up) + a_b) / GLA_TAU, GLA_HEADS)
    o, S = gla_chunked(q, k, v, la, S0.astype(f32))
    y_g = head_rms_norm(jnp.swapaxes(o, 1, 2), ln_g).reshape(bsz, T, HALF) * jax.nn.silu(g)
    u = z[..., GLA_COLS:]
    ys, x_re, x_im = s5_scan(u, lam_re, lam_im, log_step, b_re, b_im, c_re, c_im, d_skip, x_re0, x_im0)
    ys = jax.nn.gelu(ys)
    y_s = ys * jax.nn.sigmoid(jnp.matmul(ys, w_glu))
    y = jnp.matmul(jnp.concatenate([y_g, y_s], -1), w_out)
    return y, (S, x_re, x_im)

def conv_ffn(h, conv0, w_up, conv_w, conv_b, w_down):
    T = h.shape[1]
    u = jnp.matmul(h, w_up)
    ext = jnp.concatenate([conv0.astype(u.dtype), u], axis=1)
    c = conv_b + sum(conv_w[j] * ext[:, j:j + T] for j in range(CONV_W))
    val, gate = c[..., :D_FF], c[..., D_FF:]
    return jnp.matmul(val * jax.nn.silu(gate), w_down), ext[:, T:]

def trunk(x, st, prm):
    (st_C, st_n, st_m, st_S, st_shift, st_gla, st_re, st_im, st_conv) = st
    (norm_mix, norm_ffn, norm_final,
     e_w_in, e_b_if, e_mu, e_w0, e_w_up, e_a0, e_a_up, e_g_up, e_k_k, e_k_a, e_r_k, e_ln_m_g, e_ln_r_g, e_ln_r_b, e_w_out,
     o_w_in, o_a_up, o_a_b, o_ln_g, o_lam_re, o_lam_im, o_log_step, o_b_re, o_b_im, o_c_re, o_c_im, o_d, o_w_glu, o_w_out,
     f_w_up, f_conv_w, f_conv_b, f_w_down) = prm
    ev, od, cv = [], [], []
    for l in range(DEPTH):
        i = l // 2
        h = rms_norm(x, norm_mix[l])
        if l % 2 == 0:
            y, s = even_mixer(h, (st_C[i], st_n[i], st_m[i], st_S[i], st_shift[i]),
                              (e_w_in[i], e_b_if[i], e_mu[i], e_w0[i], e_w_up[i], e_a0[i], e_a_up[i], e_g_up[i],
                               e_k_k[i], e_k_a[i], e_r_k[i], e_ln_m_g[i], e_ln_r_g[i], e_ln_r_b[i], e_w_out[i]))
            ev.append(s)
        else:
            y, s = odd_mixer(h, (st_gla[i], st_re[i], st_im[i]),
                             (o_w_in[i], o_a_up[i], o_a_b[i], o_ln_g[i], o_lam_re[i], o_lam_im[i], o_log_step[i],
                              o_b_re[i], o_b_im[i], o_c_re[i], o_c_im[i], o_d[i], o_w_glu[i], o_w_out[i]))
            od.append(s)
        x = x + y.astype(x.dtype)
        h = rms_norm(x, norm_ffn[l])
        y, c = conv_ffn(h, st_conv[l], f_w_up[l], f_conv_w[l], f_conv_b[l], f_w_down[l])
        x = x + y.astype(x.dtype)
        cv.append(c)
    out = rms_norm(x, norm_final)
    new_state = (jnp.stack([s[0] for s in ev]), jnp.stack([s[1] for s in ev]), jnp.stack([s[2] for s in ev]),
                 jnp.stack([s[3] for s in ev]), jnp.stack([s[4] for s in ev]),
                 jnp.stack([s[0] for s in od]), jnp.stack([s[1] for s in od]), jnp.stack([s[2] for s in od]),
                 jnp.stack(cv))
    return out, new_state

def setup_inputs(seed: int = 0) -> dict:
    key = jax.random.key(seed)
    keys = jax.random.split(key, 96)
    counter = [0]

    def nk():
        counter[0] += 1
        return keys[counter[0] - 1]

    def nrm(shape, scale):
        return scale * jax.random.normal(nk(), shape, jnp.float32)

    def unif(shape, lo, hi):
        return jax.random.uniform(nk(), shape, jnp.float32, lo, hi)

    f2 = 2 * D_FF
    inp = {}
    inp['x_prompt'] = nrm((BATCH, SEQ, D_MODEL), 1.0)
    inp['x_sample'] = nrm((DEC_BATCH, DEC_SEQ, D_MODEL), 1.0)
    inp['state_mlstm_C'] = nrm((N_EVEN, DEC_BATCH, MLSTM_HEADS, MLSTM_HD, MLSTM_HD), 0.05)
    inp['state_mlstm_n'] = nrm((N_EVEN, DEC_BATCH, MLSTM_HEADS, MLSTM_HD), 0.1)
    inp['state_mlstm_m'] = nrm((N_EVEN, DEC_BATCH, MLSTM_HEADS), 1.0)
    inp['state_rwkv_S'] = nrm((N_EVEN, DEC_BATCH, RWKV_HEADS, RWKV_HD, RWKV_HD), 0.1)
    inp['state_rwkv_shift'] = nrm((N_EVEN, DEC_BATCH, RWKV_COLS), 1.0)
    inp['state_gla_S'] = nrm((N_ODD, DEC_BATCH, GLA_HEADS, GLA_DK, GLA_DV), 0.1)
    inp['state_s5_re'] = nrm((N_ODD, DEC_BATCH, S5_GROUPS, S5_P), 0.1)
    inp['state_s5_im'] = nrm((N_ODD, DEC_BATCH, S5_GROUPS, S5_P), 0.1)
    inp['state_ffn_conv'] = nrm((DEPTH, DEC_BATCH, CONV_W - 1, f2), 1.0)
    inp['norm_mix'] = 1.0 + nrm((DEPTH, D_MODEL), 0.02)
    inp['norm_ffn'] = 1.0 + nrm((DEPTH, D_MODEL), 0.02)
    inp['norm_final'] = 1.0 + nrm((D_MODEL,), 0.02)
    inp['e_w_in'] = nrm((N_EVEN, D_MODEL, EVEN_COLS), D_MODEL ** -0.5)
    inp['e_b_if'] = jnp.concatenate([nrm((N_EVEN, MLSTM_HEADS), 0.1),
                                     jnp.linspace(3.0, 6.0, MLSTM_HEADS, dtype=jnp.float32)[None] + nrm((N_EVEN, MLSTM_HEADS), 0.1)], axis=-1)
    inp['e_mu'] = unif((N_EVEN, RWKV_COLS), 0.0, 1.0)
    inp['e_w0'] = unif((N_EVEN, HALF), -6.0, -1.0)
    inp['e_w_up'] = nrm((N_EVEN, RWKV_W_LORA, HALF), 0.1)
    inp['e_a0'] = nrm((N_EVEN, HALF), 0.1)
    inp['e_a_up'] = nrm((N_EVEN, RWKV_A_LORA, HALF), RWKV_A_LORA ** -0.5)
    inp['e_g_up'] = nrm((N_EVEN, RWKV_G_LORA, HALF), RWKV_G_LORA ** -0.5)
    inp['e_k_k'] = 0.85 + nrm((N_EVEN, HALF), 0.05)
    inp['e_k_a'] = 1.0 + nrm((N_EVEN, HALF), 0.05)
    inp['e_r_k'] = nrm((N_EVEN, HALF), 0.1)
    inp['e_ln_m_g'] = 1.0 + nrm((N_EVEN, HALF), 0.02)
    inp['e_ln_r_g'] = 1.0 + nrm((N_EVEN, HALF), 0.02)
    inp['e_ln_r_b'] = nrm((N_EVEN, HALF), 0.02)
    inp['e_w_out'] = nrm((N_EVEN, 2 * HALF, D_MODEL), (2 * HALF) ** -0.5)
    inp['o_w_in'] = nrm((N_ODD, D_MODEL, ODD_COLS), D_MODEL ** -0.5)
    inp['o_a_up'] = nrm((N_ODD, GLA_GATE_RANK, GLA_QK), GLA_GATE_RANK ** -0.5)
    inp['o_a_b'] = nrm((N_ODD, GLA_QK), 0.1)
    inp['o_ln_g'] = 1.0 + nrm((N_ODD, HALF), 0.02)
    inp['o_lam_re'] = -0.5 + nrm((N_ODD, S5_GROUPS, S5_P), 0.01)
    inp['o_lam_im'] = math.pi * jnp.arange(S5_P, dtype=jnp.float32) + nrm((N_ODD, S5_GROUPS, S5_P), 0.01)
    inp['o_log_step'] = unif((N_ODD, S5_GROUPS), math.log(1e-3), math.log(1e-1))
    inp['o_b_re'] = nrm((N_ODD, S5_GROUPS, S5_P, S5_GROUP), (2 * S5_GROUP) ** -0.5)
    inp['o_b_im'] = nrm((N_ODD, S5_GROUPS, S5_P, S5_GROUP), (2 * S5_GROUP) ** -0.5)
    inp['o_c_re'] = nrm((N_ODD, S5_GROUPS, S5_GROUP, S5_P), 0.5)
    inp['o_c_im'] = nrm((N_ODD, S5_GROUPS, S5_GROUP, S5_P), 0.5)
    inp['o_d'] = nrm((N_ODD, S5_CH), 1.0)
    inp['o_w_glu'] = nrm((N_ODD, S5_CH, S5_CH), S5_CH ** -0.5)
    inp['o_w_out'] = nrm((N_ODD, 2 * HALF, D_MODEL), (2 * HALF) ** -0.5)
    inp['f_w_up'] = nrm((DEPTH, D_MODEL, f2), D_MODEL ** -0.5)
    inp['f_conv_w'] = nrm((DEPTH, CONV_W, f2), CONV_W ** -0.5)
    inp['f_conv_b'] = nrm((DEPTH, f2), 0.02)
    inp['f_w_down'] = nrm((DEPTH, D_FF, D_MODEL), D_FF ** -0.5)
    return inp

def reference(x_prompt, x_sample, state_mlstm_C, state_mlstm_n, state_mlstm_m, state_rwkv_S, state_rwkv_shift,
              state_gla_S, state_s5_re, state_s5_im, state_ffn_conv,
              norm_mix, norm_ffn, norm_final,
              e_w_in, e_b_if, e_mu, e_w0, e_w_up, e_a0, e_a_up, e_g_up, e_k_k, e_k_a, e_r_k,
              e_ln_m_g, e_ln_r_g, e_ln_r_b, e_w_out,
              o_w_in, o_a_up, o_a_b, o_ln_g, o_lam_re, o_lam_im, o_log_step, o_b_re, o_b_im, o_c_re, o_c_im,
              o_d, o_w_glu, o_w_out,
              f_w_up, f_conv_w, f_conv_b, f_w_down):
    params = (norm_mix, norm_ffn, norm_final,
              e_w_in, e_b_if, e_mu, e_w0, e_w_up, e_a0, e_a_up, e_g_up, e_k_k, e_k_a, e_r_k,
              e_ln_m_g, e_ln_r_g, e_ln_r_b, e_w_out,
              o_w_in, o_a_up, o_a_b, o_ln_g, o_lam_re, o_lam_im, o_log_step, o_b_re, o_b_im, o_c_re, o_c_im,
              o_d, o_w_glu, o_w_out,
              f_w_up, f_conv_w, f_conv_b, f_w_down)
    f32 = jnp.float32
    bp = x_prompt.shape[0]
    init = (jnp.zeros((N_EVEN, bp, MLSTM_HEADS, MLSTM_HD, MLSTM_HD), f32),
            jnp.zeros((N_EVEN, bp, MLSTM_HEADS, MLSTM_HD), f32),
            jnp.full((N_EVEN, bp, MLSTM_HEADS), M_INIT, f32),
            jnp.zeros((N_EVEN, bp, RWKV_HEADS, RWKV_HD, RWKV_HD), f32),
            jnp.zeros((N_EVEN, bp, RWKV_COLS), f32),
            jnp.zeros((N_ODD, bp, GLA_HEADS, GLA_DK, GLA_DV), f32),
            jnp.zeros((N_ODD, bp, S5_GROUPS, S5_P), f32),
            jnp.zeros((N_ODD, bp, S5_GROUPS, S5_P), f32),
            jnp.zeros((DEPTH, bp, CONV_W - 1, 2 * D_FF), x_prompt.dtype))
    y_prompt, (p_C, p_n, p_m, p_S, p_shift, p_gla, p_re, p_im, p_conv) = trunk(x_prompt, init, params)
    past = (state_mlstm_C, state_mlstm_n, state_mlstm_m, state_rwkv_S, state_rwkv_shift,
            state_gla_S, state_s5_re, state_s5_im, state_ffn_conv)
    y_sample, (s_C, s_n, s_m, s_S, s_shift, s_gla, s_re, s_im, s_conv) = trunk(x_sample, past, params)
    return (y_prompt, y_sample, p_C, p_n, p_m, p_S, p_shift, p_gla, p_re, p_im, p_conv,
            s_C, s_n, s_m, s_S, s_shift, s_gla, s_re, s_im, s_conv)


_drawn_inputs = setup_inputs


def setup_inputs(seed=0):
    import zlib

    import numpy as np

    out = dict(_drawn_inputs(seed))
    spreads = {}
    factors = {'norm_final': 7.526,
     'e_ln_m_g': 5.591,
     'e_ln_r_g': 5.792,
     'e_ln_r_b': 11.097,
     'o_ln_g': 31.305,
     'o_lam_re': 17.52,
     'norm_ffn': 2.781,
     'o_c_re': 2.964,
     'o_c_im': 3.007,
     'o_w_glu': 3.013,
     'f_conv_b': 5.061}
    for name, (base, spread) in spreads.items():
        noise = np.random.default_rng([zlib.crc32(name.encode()), seed]).standard_normal(out[name].shape)
        drawn = base * np.exp(spread * noise) if base else spread * noise
        out[name] = jnp.asarray(drawn.astype(out[name].dtype))
    for name, factor in factors.items():
        out[name] = (out[name] * factor).astype(out[name].dtype)
    return out
```

```python
from contextlib import ExitStack

import numpy as np

import concourse.bass as bass
from concourse import mybir
from concourse.alu_op_type import AluOpType as ALU

F32 = mybir.dt.float32
ACT = mybir.ActivationFunctionType
AX = mybir.AxisListType

P = 128
D_MODEL, SEQ, DEC_BATCH, DEC_SEQ = 1024, 512, 8, 8
HALF = D_MODEL // 2
NSAMP = DEC_BATCH * DEC_SEQ
T = SEQ + NSAMP
TH = T // 2
KT = D_MODEL // P
D_FF = ((8 * D_MODEL // 3 + 255) // 256) * 256
FT = D_FF // P
NSEQ = 1 + DEC_BATCH
MH, MHD = 4, 128
RP, RHD = 4, 64
GH, GDK, GDV = 4, 64, 128
L = 128
LR = 64
NCH = SEQ // L
NCR = SEQ // LR
SG, SC, SP = 32, 16, 64
BL = 8
NB = T // BL
NBP = SEQ // BL
GRANK, GLA_TAU = 16, 16.0
EPS = 1e-6
RWKV_EPS = 64e-5
M_INIT = -1e30
NEG = -1e30
TWO_PI = 6.283185307179586
HN = {"mn": 0, "rn": 4, "gn": 8}
ROUND = 12582912.0

E_TILES = 30
O_TILES = 16
ADDS = ("e_out", "down0", "o_out", "down1")
RUNS = {"e_in": (0, E_TILES), "e_out": (30, 8), "ffn0": (38, 2 * FT),
        "o_in": (38 + 2 * FT, O_TILES), "o_out": (54 + 2 * FT, 8), "ffn1": (62 + 2 * FT, 2 * FT)}
W_TILES = 62 + 4 * FT
USE = {}
_u = 0
for _name, _n in (("e_in", E_TILES), ("e_out", 8), ("ffn0", 2 * FT), ("down0", 8),
                  ("o_in", O_TILES), ("o_out", 8), ("ffn1", 2 * FT), ("down1", 8)):
    USE[_name] = _u
    _u += _n

VEC = {}
_c = 0
for _name, _n in (("norm_mix", 16), ("norm_ffn", 16), ("norm_final", 8), ("mu", 14), ("w0", 4), ("a0", 4),
                  ("k_k", 4), ("k_a", 4), ("r_k", 4), ("ln_m_g", 4), ("ln_r_g", 4), ("ln_r_b", 4),
                  ("a_b", 2), ("o_ln_g", 4), ("o_d", 4), ("sgn", 1), ("b_if", 1)):
    VEC[_name] = _c
    _c += _n
NVEC = _c
CONVC = 4 * 2 * FT

CONST = {}
_c = 0
GLEV = 8
for _name, _n in (("ident", 128), ("ones", 128), ("headones", 128), ("scan128", T), ("scan64", T),
                  ("mneg", 128), ("mneg_s", 64), ("gla", GLEV * 128), ("gla_s", 4 * 64),
                  ("rk", 5 * 64), ("rk_s", 5 * 64), ("seq", 8), ("idpair", 64), ("sel", 4 * 128)):
    CONST[_name] = _c
    _c += _n
NCONST = _c


def shape_constants():
    c = np.zeros((P, NCONST), np.float32)

    def put(name, a):
        c[:a.shape[0], CONST[name]:CONST[name] + a.shape[1]] = a

    i = np.arange(P)
    put("ident", np.eye(P))
    put("ones", np.ones((P, P)))
    put("headones", (i[:, None] // 64 == i[None] // 64) * 1.0)
    t = np.arange(T)
    for name, n in (("scan128", L), ("scan64", LR)):
        start = np.where(t < SEQ, t % n == 0, (t - SEQ) % DEC_SEQ == 0)
        put(name, np.broadcast_to(1.0 - start, (P, T)))
    s, tt = i[:, None], i[None]
    put("mneg", np.where(s <= tt, 0.0, NEG))
    s8, t8 = s[:64], tt[:, :64]
    same = s8 // 8 == t8 // 8
    put("mneg_s", np.where(same & (s8 <= t8), 0.0, NEG))
    lev = [((s // (2 * h) == tt // (2 * h)) & (s % (2 * h) < h) & (tt % (2 * h) >= h)) * 1.0
           for h in (64, 32, 16, 8, 4, 2, 1)] + [np.eye(P)]
    put("gla", np.concatenate(lev, 1))
    put("gla_s", np.concatenate([m[:64, :64] for m in lev[4:]], 1))
    s2 = (i % 64)[:, None]
    t2 = np.arange(64)[None]
    for name, ok in (("rk", np.ones((P, 64), bool)), ("rk_s", s2 // 8 == t2 // 8)):
        up, upi, low = (s2 < t2) & ok, (s2 <= t2) & ok, (s2 > t2) & ok
        put(name, np.concatenate([up, upi, up, upi, low], 1) * 1.0)
    put("idpair", (s2 == t2) * 1.0)
    put("seq", (s2 // 8 == np.arange(8)[None]) * 1.0)
    sel = np.zeros((4, 4, 128))
    sel[np.arange(4), np.arange(4)] = 1.0
    put("sel", sel.reshape(4, 512))
    return c


class Chain:

    def __init__(self, eng, sem):
        self.eng, self.sem, self.n, self.i, self.per = eng, sem, 0, None, 0

    def __call__(self, ins):
        ins.then_inc(self.sem, 1)
        self.n += 1
        if self.i is None:
            self.eng.wait_ge(self.sem, self.n)
        else:
            self.eng.wait_ge(self.sem, self.i * self.per + self.n)

    def loop(self, i, per):
        self.i, self.per, self.start = i, per, self.n

    def end_loop(self, times):
        assert self.n - self.start == self.per, (self.n - self.start, self.per)
        self.n = self.start + self.per * times
        self.i = None


def program(nc, d, o, stages):
    ctx = ExitStack()
    with ctx:
        def sb(name, *shape):
            return ctx.enter_context(nc.sbuf_tensor(name, list(shape), F32))

        def sem(name):
            return ctx.enter_context(nc.semaphore(name))

        class Sems:

            def __init__(self):
                self.made = {}

            def __call__(self, name):
                if name not in self.made:
                    self.made[name] = sem(name)
                return self.made[name]

        S = Sems()

        xT = sb("xT", P, KT, T)
        hT = sb("hT", P, KT, T)
        w_ring = sb("w_ring", P, 2, KT * P)
        down_ring = sb("down_ring", P, 2, FT * P)
        cst = sb("cst", P, NCONST)
        vec = sb("vec", P, NVEC)
        convp = sb("convp", P, 2, CONVC)
        ext = sb("ext", P, 2, 2 + SEQ + 10 * DEC_BATCH)
        rstd = sb("rstd", P, T)
        sq = sb("sq", P, 2, T)
        NA = 28600
        arena = sb("arena", P, NA)
        PP = [ctx.enter_context(nc.psum_tensor(f"PP{i}", [P, 2, 512], F32)) for i in range(4)]

        def bank(b, n=512):
            return PP[b // 2][:, b % 2, 0:n]

        def pair(i):
            return PP[i][:, :, 0:TH]

        def at(off, *shape):
            n = int(np.prod(shape))
            assert off + n <= NA, (off, n)
            v = arena[:, off:off + n]
            if len(shape) == 1:
                return v
            names = [f"a{i}" for i in range(len(shape))]
            return v.rearrange(f"p ({' '.join(names)}) -> p {' '.join(names)}", **dict(zip(names[1:], shape[1:])))

        def halves(v):
            return v.rearrange("p (a n) -> p a n", a=2)

        def c_(name, n, rows=P, r0=0):
            return cst[r0:r0 + rows, CONST[name]:CONST[name] + n]

        def v_(name, k=0, rows=P, r0=0):
            return vec[r0:r0 + rows, VEC[name] + k:VEC[name] + k + 1]

        ident, ones, headones = c_("ident", 128), c_("ones", 128), c_("headones", 128)
        sel = c_("sel", 512, 4).rearrange("p (h n) -> p h n", h=4)
        seqmask = c_("seq", 8)

        def tt(eng, out, a, b, op):
            return eng.tensor_tensor(out, a, b, op)

        def stt(out, a, s, b, op0, op1):
            return nc.vector.scalar_tensor_tensor(out=out, in0=a, scalar=s, in1=b, op0=op0, op1=op1)

        def bc(v, axis, n):
            v = v.unsqueeze(axis)
            shape = list(v.shape)
            shape[axis] = n
            return v.to_broadcast(shape)

        def mm(out, lhsT, rhs, start=True, stop=True):
            return nc.tensor.matmul(out, lhsT, rhs, start=start, stop=stop)

        zm = at(0, 16, T)
        zr = at(9216, 14, T)
        W0 = 9216 + 14 * T
        lora = at(W0, 2, 512)
        wif = at(W0 + 1024, KT, 36)
        shin = at(W0 + 1312, 14, DEC_BATCH)
        shout = at(W0 + 1424, 14, NSEQ)
        W1 = W0 + 1552
        rows = at(W1, 8, T)
        r_f, r_i, r_B, r_m, r_a, r_s, r_w, r_e = (rows[0:4, k, :] for k in range(8))
        W2 = W1 + 8 * T
        qh = at(W2, 4, T)
        W3 = W2 + 4 * T
        sqf = sq[:, :, :].rearrange("p a b -> p (a b)")
        qn = sqf[:, 0:512].rearrange("p (h n) -> p h n", h=4)
        att = sqf[:, 512:1024].rearrange("p (h n) -> p h n", h=4)
        Dm = at(W3, 4, L)
        vaug = at(W3 + 512, 4, 129)
        ktok = at(W3 + 1028, 4, L)
        PL = at(W3 + 1540, 4, 16)
        omka = at(W3 + 1604, 4)
        W4 = W3 + 1612
        Cst = at(W4 + 160, 4, 129)
        wlc = at(W4, 5, 4)
        decb = at(W4 + 20, 4, 12)
        rsm = at(W4 + 68, 5, 12)
        wlm = at(W4 + 128, 4, 8)
        r_mp, r_rl, r_dec, r_m0, r_mo = (rsm[0:4, k, :] for k in range(5))
        Cs = hT[:, :, :].rearrange("p a b -> p (a b)")[:, 0:4128].rearrange("p (h j n) -> p h j n", h=4, j=8)
        Csf = hT[:, :, :].rearrange("p a b -> p (a b)")[:, 0:4128].rearrange("p (g n) -> p g n", n=129)
        dring = down_ring[:, :, :].rearrange("p a b -> p (a b)")
        Km = dring[0:64, 0:4096].rearrange("p (h j n) -> p h j n", h=4, j=8)

        AR = at(0, 4, 2, T)
        BK = at(4608, 4, 2, T)
        rkp = at(W1, 4, T)
        yr = at(W1 + 2304, 4, T)
        X0 = W1 + 4608
        prep = at(W1 + 2304, 5, 2, T)
        XPA = at(X0, 2, 2, 2, 3, 64)
        PF = at(X0 + 1536, 2, 4, 64)
        tok = at(X0 + 2048, 2, 4, 3, 64)
        R1 = sqf[:, 0:256].rearrange("p (a b) -> p a b", a=4)
        U = sqf[:, 256:512].rearrange("p (a b) -> p a b", a=4)
        Sr = at(W4 + 932, 4, 64)
        QT = at(W4 + 676, 4, 64)
        Gs = at(9216, 2, 4, 320)
        SS = at(9216 + 2560, 4, 8, 64)
        UVm = dring[:, 0:4096].rearrange("p (a q j n) -> p a q j n", a=2, q=4, j=8)

        actv = at(0, FT, T)
        cv = at(12672, 3, T)
        convin = at(14400, 2 * FT, 16)
        convout = at(15104, 2 * FT, 18)

        block = ctx.enter_context(nc.Block())
        do_odd = stages > 1

        WL = [S("w_landed0"), S("w_landed1")]
        DL = [S("down_landed0"), S("down_landed1")]
        FREE = [S("psum_free0"), S("psum_free1")]
        runs = ["e_in", "e_out", "ffn0"] + (["o_in", "o_out", "ffn1"] if do_odd else [])
        last_tile = RUNS[runs[-1]][0] + RUNS[runs[-1]][1]

        def all_free(eng, name, n):
            for s in range(2):
                eng.wait_ge(FREE[s], (USE[name] + n) // 2 + 1)

        zo = at(0, 16, T)
        adown = at(9216, T)[0:GRANK]
        aup = at(9792, 256)[0:GRANK]
        wad = at(10048, KT, GRANK)
        LA = at(10176, 2, T)
        BC = at(11328, 2, T)
        QG = at(12480, 2, T)
        KG = at(13632, 2, T)
        XL = at(14784, 2, 7, T)
        attg = at(22848, 4, 128)
        attw = at(23360, 2, 1024)
        vt = at(25408, 4, 128)
        kgt = at(25920, 2, 128)
        Sg = at(26176, 2, 128)
        ebl = at(26432, 2, 12)
        E1 = at(26456, 2, T)
        hflat = hT[:, :, :].rearrange("p a b -> p (a b)")
        SSg = hflat[:, 0:2048].rearrange("p (t j n) -> p t j n", t=2, j=8)
        Vm = dring[0:64, 0:4096].rearrange("p (h j n) -> p h j n", h=4, j=8)
        Gy = at(0, SG, BL + 1, SC)
        Ub = at(4608, SG, NB)
        FZT = at(9216, SG, P)
        Mt = at(13312, SG, P)
        FZ = at(17408, SG, BL, SC)
        Yb = at(17408, SG, NB)
        Yf = at(19712, 4, BL, NB)
        ZZ = at(21504, 2, SG, NB)
        Kb = at(21504, SG, P)[0:SC]
        fsw = at(21504, 2, SG, SC)
        gsw = at(22528, 2, SG, SC)
        ft = at(23552, SG, SC)
        gt = at(24064, SG, SC)
        XX = at(26112, SG, NB + 1)
        BC4 = at(26112, 4, SG, SC)
        up = dring[:, 0:4 * T].rearrange("p (a s b) -> p a s b", a=4, s=BL)
        wglu = dring[:, 2304:4352].rearrange("p (k n) -> p k n", k=4)
        LAX = at(14784, 4, T)
        Yf_tok = at(0, 4, T)
        sgl = at(2304, 4, T)
        x0st = dring[:, 0:256].rearrange("p (g j) -> p g j", g=SG)
        x0sw = dring[:, 4352:4608].rearrange("p (g j) -> p g j", g=SG)
        SO = dring[:, 4608:4896].rearrange("p (g j) -> p g j", g=SG)
        st1 = dring[:, 4896:5152].rearrange("p (g j) -> p g j", g=SG)
        st2 = dring[:, 5152:5408].rearrange("p (g j) -> p g j", g=SG)
        tab = sqf[:, 0:768].rearrange("p (k g) -> p k g", g=SG)
        cur = sqf[:, 768:960].rearrange("p (a k g) -> p a k g", a=2, k=3)
        sc1 = sqf[:, 960:1024].rearrange("p (k g) -> p k g", k=2)
        sc2 = sqf[:, 1024:1088].rearrange("p (k g) -> p k g", k=2)
        (l_re, l_im, l_st, t_a, t_b, t_er, t_s, t_c, t_n, lr, li, lis, wr, wi, wis, t_d,
         lr8, li8) = (tab[:, k, :] for k in range(18))
        li2 = tab[:, 18:20, :]
        lis8 = li2[:, 0, :]
        t_e, t_f = tab[:, 20, :], tab[:, 21, :]
        u_scr = nc.dram_tensor("u_scratch", (4 * P, BL, NB), F32, kind="Internal").ap()
        y_scr = nc.dram_tensor("y_scratch", (4 * P, BL, NB), F32, kind="Internal").ap()

        def odd_sp(sp, stream, out):
            sp.wait_ge(S("proj_done"), USE["down0"] + 8)
            sp.dma_start(wad, d["w_ad"]).then_inc(S("o_small_in"), 16)
            sp.dma_start(aup, d["a_up"]).then_inc(S("o_small_in"), 16)
            stream("o_in")
            sp.wait_ge(S("proj_done"), USE["o_in"] + O_TILES)
            sp.dma_start(SSg, d["gS"]).then_inc(S("gS_in"), 16)
            sp.wait_ge(S("gl_st"), NCH + 1)
            out("pG", Sg)
            sp.wait_ge(S("gs_st"), 2)
            sp.dma_start(o["sG"], SSg).then_inc(S("sG_written"), 16)
            sp.wait_ge(S("ycat"), 12)
            sp.wait_ge(S("out_written"), 16 * 6)
            sp.dma_start(tab[:, 0:3, :], d["s5_lam"]).then_inc(S("s5_in"), 16)
            sp.dma_start(BC4, d["s5_bc"]).then_inc(S("s5_in"), 16)
            sp.dma_start(wglu, d["w_glu"]).then_inc(S("glu_in"), 16)
            sp.dma_start(x0sw, d["s5_x0"][:, 1]).then_inc(S("x0_in"), 16)
            sp.wait_ge(S("s5_up"), 1)
            sp.dma_start(u_scr.rearrange("(a p) s b -> p a (s b)", p=P),
                         up.rearrange("p a s b -> p a (s b)")).then_inc(S("u_scratched"), 16)
            sp.wait_ge(S("u_scratched"), 16)
            sp.dma_start(x0st, d["s5_x0"][:, 0]).then_inc(S("x0_in"), 16)
            uv = u_scr.rearrange("(g c) s b -> s c g b", c=SC)
            for s in range(BL):
                sp.dma_start(Ub[SC * s:SC * s + SC], uv[s]).then_inc(S("U_in"), 16)
            sp.wait_ge(S("s5_mzero"), 1)
            sp.wait_ge(S("s5_kc"), 8)
            for s in range(BL):
                sp.dma_start(Mt[SC * s:SC * s + SC, :, SC * s:P], Kb[:, :, 0:P - SC * s]).then_inc(S("M_in"), 16)
            sp.wait_ge(S("s5_zc"), 8)
            for r in range(2):
                sp.dma_start(ZZ[64 * r:64 * r + 64, 1], ZZ[64 - 64 * r:128 - 64 * r, 0]).then_inc(S("zsw_in"), 16)
            sp.wait_ge(S("s5_yc"), 8)
            yv = y_scr.rearrange("(g c) t b -> t c g b", c=SC)
            for t in range(BL):
                sp.dma_start(yv[t], Yb[SC * t:SC * t + SC]).then_inc(S("y_scratched"), 16)
            sp.wait_ge(S("y_scratched"), 16 * BL)
            sp.dma_start(Yf.rearrange("p a s b -> p a (s b)"),
                         y_scr.rearrange("(a p) s b -> p a (s b)", p=P)).then_inc(S("Y_in"), 16)
            sp.wait_ge(S("s5_so"), 1)
            out("s5", SO)
            stream("o_out")
            stream("ffn1")
            for s in range(2):
                sp.wait_ge(S(f"ext_free{s}"), 1 + 7 + 2 * FT)
            out("conv1", convout)
            sp.wait_ge(S("h_ready"), 40)
            out("y", hT[:])

        def odd_pool(pool):
            chain = Chain(pool, S("pool_chain"))
            G = nc.gpsimd
            pool.wait_ge(S("ycat"), 12)
            G.memset(Mt.rearrange("p a b -> p (a b)"), 0.0).then_inc(S("s5_mzero"), 1)
            pool.wait_ge(S("s5_lam"), 1)
            neg = v_("sgn")
            chain(G.tensor_scalar(Gy[:, :, 0, :], BC4[:, 2], neg, -1.0, ALU.mult, ALU.mult))
            chain(G.tensor_scalar(gsw[:, 0], BC4[:, 3], neg, None, ALU.mult))
            for k in range(BL):
                g, sw, nsw = Gy[:, :, k, :], gsw[:, k % 2], gsw[:, (k + 1) % 2]
                r, i = bc(lr, 2, SC), bc(lis, 2, SC)
                chain(tt(G, Gy[:, :, k + 1, :], g, r, ALU.mult))
                chain(tt(G, gt, sw, i, ALU.mult))
                chain(tt(G, Gy[:, :, k + 1, :], Gy[:, :, k + 1, :], gt, ALU.subtract))
                chain(tt(G, nsw, sw, r, ALU.mult))
                chain(tt(G, gt, g, i, ALU.mult))
                tt(G, nsw, nsw, gt, ALU.add).then_inc(S("s5_g"), 1)
                pool.wait_ge(S("s5_g"), k + 1)

        def odd_pe(pe, norm, project, head_norm):
            norm(2)
            pe.wait_ge(S("h_ready"), 24)
            pe.wait_ge(S("o_small_in"), 32)
            for a in range(2):
                for k in range(KT):
                    last = mm(PP[2][0:GRANK, a, 0:TH], wad[:, k, :], hT[:, k, a * TH:(a + 1) * TH], k == 0,
                              k == KT - 1)
            last.then_inc(S("ad_done"), 1)
            project("o_in", hT)
            pe.wait_ge(S("ad_copied"), 1)
            for t in range(2):
                for a in range(2):
                    last = mm(PP[2 + t][:, a, 0:TH], aup[:, t * P:(t + 1) * P], adown[:, a * TH:(a + 1) * TH])
                last.then_inc(S("gl_up"), 1)
            pe.wait_ge(S("gl_qk"), 2)
            pe.wait_ge(S("gl_x"), 14)
            all_free(pe, "o_in", O_TILES)
            for c in range(NCH + 1):
                n, c0 = (L, L * c) if c < NCH else (NSAMP, SEQ)
                cols = slice(c0, c0 + n)
                if c:
                    pe.wait_ge(S("gl_tokc"), c)
                    pe.wait_ge(S("gl_st"), c + 1)
                for h in range(GH):
                    nc.tensor.transpose(bank(4)[0:n, h * P:(h + 1) * P], zo[:, 4 + h, cols], ident)
                for t in range(2):
                    last = nc.tensor.transpose(bank(5)[0:n, t * P:(t + 1) * P], KG[:, t, cols], ident)
                last.then_inc(S("gl_tok"), 1)
                for h in range(GH):
                    t, r = h // 2, slice(64 * (h % 2), 64 * (h % 2) + 64)
                    if 4 * c + h >= 2:
                        pe.wait_ge(S("gl_am"), 4 * c + h - 1)
                    lev = range(8) if c < NCH else range(4, 8)
                    for e, v in enumerate(lev):
                        out = PP[h % 2][0:n, (e * n) // 512, (e * n) % 512:(e * n) % 512 + n]
                        lhs, rhs = ((XL[r, t, v, cols], XL[r, t, v, cols]) if v < 7
                                    else (zo[r, 2 + t, cols], zo[r, t, cols]))
                        last = mm(out, lhs, rhs)
                    last.then_inc(S("gl_sc"), 1)
                pe.wait_ge(S("gl_tokc"), c + 1)
                pe.wait_ge(S("gl_st"), c + 1)
                if c == NCH:
                    pe.wait_ge(S("gS_in"), 16)
                if c:
                    pe.wait_ge(S("gl_oc"), c)
                for h in range(GH):
                    t, r = h // 2, slice(64 * (h % 2), 64 * (h % 2) + 64)
                    out = bank(6 + h % 2)[:, t * n:(t + 1) * n]
                    pe.wait_ge(S("gl_at"), 4 * c + h + 1)
                    mm(out, vt[:, h, :], attg[:, h, 0:n], True, False)
                    if c < NCH:
                        last = mm(out, Sg[r, t, :], QG[r, t, cols], False, True)
                    else:
                        for j in range(8):
                            last = mm(out[:, 8 * j:8 * j + 8], SSg[r, t, j, :], QG[r, t, c0 + 8 * j:c0 + 8 * j + 8],
                                      False, j == 7)
                last.then_inc(S("gl_o"), 1)
                if c < NCH:
                    for h in range(GH):
                        t, r = h // 2, slice(64 * (h % 2), 64 * (h % 2) + 64)
                        last = mm(bank(5)[r, 256 + t * P:256 + (t + 1) * P], kgt[0:n, t, r], vt[0:n, h, :])
                    last.then_inc(S("gl_s"), 1)
                else:
                    pe.wait_ge(S("gs_vm"), 1)
                    pe.wait_ge(S("gl_am"), 20)
                    for t in range(2):
                        for h in (2 * t, 2 * t + 1):
                            r = slice(64 * (h % 2), 64 * (h % 2) + 64)
                            for a in range(2):
                                last = mm(PP[t][r, a, :], kgt[0:n, t, r], Vm[:, h, 4 * a:4 * a + 4, :])
                        last.then_inc(S("gs_s"), 1)
            pe.wait_ge(S("gs_st"), 2)
            head_norm("gn", zo[:, 0:4, :], LAX, ones, mean=False)

            pe.wait_ge(S("ycat"), 12)
            pe.wait_ge(S("s5_f"), 8)
            for b in range(8):
                if b >= 2:
                    pe.wait_ge(S("s5_ftc"), b - 1)
                for e in range(4):
                    last = nc.tensor.transpose(bank(b % 2)[:, e * P:(e + 1) * P],
                                               FZ[:, 4 * b + e, :, :].rearrange("p s c -> p (s c)"), ident)
                last.then_inc(S("s5_ft"), 1)
            pe.wait_ge(S("s5_g"), 8)
            for b in range(8):
                if b >= 2:
                    pe.wait_ge(S("s5_kc"), b - 1)
                for e in range(4):
                    g = 4 * b + e
                    last = mm(bank(2 + b % 2)[0:SC, e * P:(e + 1) * P], FZ[:, g, BL - 1, :],
                              Gy[:, g, 0:BL, :].rearrange("p s c -> p (s c)"))
                last.then_inc(S("s5_k"), 1)
            pe.wait_ge(S("U_in"), 16 * BL)
            pe.wait_ge(S("s5_ftc"), 8)
            for b in range(8):
                if b >= 2:
                    pe.wait_ge(S("s5_zc"), b - 1)
                for e in range(4):
                    last = mm(bank(4 + b % 2)[:, e * NB:(e + 1) * NB], FZT[:, 4 * b + e, :], Ub[:, 4 * b + e, :])
                last.then_inc(S("s5_z"), 1)
            pe.wait_ge(S("M_in"), 16 * BL)
            pe.wait_ge(S("s5_scan"), 1)
            for b in range(8):
                if b >= 2:
                    pe.wait_ge(S("s5_yc"), b - 1)
                for e in range(4):
                    g = 4 * b + e
                    out = bank(6 + b % 2)[:, e * NB:(e + 1) * NB]
                    mm(out, Mt[:, g, :], Ub[:, g, :], True, False)
                    last = mm(out, Gy[:, g, 1:BL + 1, :].rearrange("p s c -> p (s c)"), XX[:, g, 0:NB], False, True)
                last.then_inc(S("s5_y"), 1)
            pe.wait_ge(S("s5_gelu"), 4)
            pe.wait_ge(S("glu_in"), 16)
            for m in range(4):
                for a in range(2):
                    for k in range(4):
                        last = mm(PP[m][:, a, 0:TH], wglu[:, k, m * P:(m + 1) * P], Yf_tok[:, k, a * TH:(a + 1) * TH],
                                  k == 0, k == 3)
                last.then_inc(S("s5_glu"), 1)
            pe.wait_ge(S("ycat"), 16)
            project("o_out", hT)

        def odd_act(act, A, chain, norm, evac, head_norm):
            norm(2)
            act.wait_ge(S("ad_done"), 1)
            A(halves(adown), PP[2][0:GRANK, :, 0:TH], ACT.Copy).then_inc(S("ad_copied"), 1)
            evac("o_in", 0, 2, ACT.Copy, zo[:, 0:2, :], GDK ** -0.5)
            evac("o_in", 2, 6, ACT.Copy, zo[:, 2:8, :])
            evac("o_in", 8, 4, ACT.Silu, zo[:, 8:12, :])
            evac("o_in", 12, 4, ACT.Copy, zo[:, 12:16, :])
            for t in range(2):
                act.wait_ge(S("gl_up"), t + 1)
                chain(A(halves(LA[:, t, :]), pair(2 + t), ACT.Identity, bias=v_("a_b", t)))
                chain(A(BC[:, t, :], LA[:, t, :], ACT.Abs))
            for t in range(2):
                chain(A(BC[:, t, :], BC[:, t, :], ACT.Exp, scale=-1.0))
                A(BC[:, t, :], BC[:, t, :], ACT.Ln, bias=1.0).then_inc(S("gl_sp"), 1)
            for t in range(2):
                act.wait_ge(S("gl_kd"), t + 1)
                A(E1[:, t, :], BC[:, t, :], ACT.Exp)
                A(KG[:, t, :], KG[:, t, :], ACT.Exp).then_inc(S("gl_e1"), 1)
            for k in range(14):
                t, v = k // 7, k % 7
                n = SEQ if v < 4 else T
                act.wait_ge(S("gl_d"), k + 1)
                A(XL[:, t, v, 0:n], XL[:, t, v, 0:n], ACT.Exp).then_inc(S("gl_e"), 1)
            for c in range(NCH + 1):
                n, c0 = (L, L * c) if c < NCH else (NSAMP, SEQ)
                act.wait_ge(S("gl_tok"), c + 1)
                A(vt[0:n].rearrange("p a b -> p (a b)"), bank(4)[0:n, :], ACT.Copy)
                A(kgt[0:n].rearrange("p a b -> p (a b)"), bank(5)[0:n, 0:256], ACT.Copy).then_inc(S("gl_tokc"), 1)
                act.wait_ge(S("gl_o"), c + 1)
                for a in range(2):
                    last = A(zo[:, a:4:2, c0:c0 + n], bank(6 + a)[:, 0:2 * n].rearrange("p (h n) -> p h n", h=2),
                             ACT.Copy)
                last.then_inc(S("gl_oc"), 1)
            act.wait_ge(S("gl_oc"), NCH + 1)
            for h in range(4):
                act.sem_inc(S("hn_src"), 1)
            head_norm("gn", zo[:, 0:4, :], LAX, GDV, EPS, mean=False)

            act.wait_ge(S("ycat"), 12)
            act.wait_ge(S("s5_in"), 32)
            A(t_s, l_st, ACT.Exp).then_inc(S("s5_step"), 1)
            act.wait_ge(S("s5_ab"), 1)
            A(t_er, t_a, ACT.Exp)
            A(t_s, t_s, ACT.Sin)
            A(t_c, t_c, ACT.Sin).then_inc(S("s5_trig"), 1)
            for b in range(8):
                act.wait_ge(S("s5_ft"), b + 1)
                A(FZT[:, 4 * b:4 * b + 4, :].rearrange("p a b -> p (a b)"), bank(b % 2), ACT.Copy).then_inc(
                    S("s5_ftc"), 1)
            for b in range(8):
                act.wait_ge(S("s5_k"), b + 1)
                A(Kb[:, 4 * b:4 * b + 4, :].rearrange("p a b -> p (a b)"), bank(2 + b % 2)[0:SC, :],
                  ACT.Copy).then_inc(S("s5_kc"), 1)
            act.wait_ge(S("M_in"), 16 * BL)
            for b in range(8):
                act.wait_ge(S("s5_z"), b + 1)
                A(ZZ[:, 0, 4 * b:4 * b + 4, :].rearrange("p a b -> p (a b)"), bank(4 + b % 2)[:, 0:4 * NB],
                  ACT.Copy).then_inc(S("s5_zc"), 1)
            for b in range(8):
                act.wait_ge(S("s5_y"), b + 1)
                A(Yb[:, 4 * b:4 * b + 4, :].rearrange("p a b -> p (a b)"), bank(6 + b % 2)[:, 0:4 * NB],
                  ACT.Copy).then_inc(S("s5_yc"), 1)
            for k in range(4):
                act.wait_ge(S("s5_ys"), k + 1)
                A(Yf_tok[:, k, :], Yf_tok[:, k, :], ACT.Gelu_apprx_tanh).then_inc(S("s5_gelu"), 1)
            for m in range(4):
                act.wait_ge(S("s5_glu"), m + 1)
                A(halves(sgl[:, m, :]), pair(m), ACT.Sigmoid).then_inc(S("s5_sig"), 1)

        def odd_dve(dve, V, chain, norm, residual, head_norm):
            norm(2, "norm_mix", 8)
            dve.wait_ge(S("out_written"), 16 * 5)
            for t in range(2):
                dve.wait_ge(S("gl_sp"), t + 1)
                la, b_ = LA[:, t, :], BC[:, t, :]
                chain(stt(la, la, 0.0, b_, ALU.min, ALU.subtract))
                chain(V.tensor_scalar(la, la, 1.0 / GLA_TAU, None, ALU.mult))
                chain(V.tensor_tensor_scan(b_, c_("scan128", T), la, 0.0, ALU.mult, ALU.add))
                kd = KG[:, t, :]
                for c0, m, n in ((0, NCH, L), (SEQ, 8, 8)):
                    b3, k3 = (x[:, c0:c0 + m * n].rearrange("p (c n) -> p c n", n=n) for x in (b_, kd))
                    last = tt(V, k3, bc(b3[:, :, n - 1], 2, n), b3, ALU.subtract)
                last.then_inc(S("gl_kd"), 1)
            for t in range(2):
                dve.wait_ge(S("gl_e1"), t + 1)
                e1 = E1[:, t, :]
                V.tensor_copy(ebl[:, t, 0:4], e1[:, 0:SEQ].rearrange("p (c n) -> p c n", n=L)[:, :, L - 1])
                V.tensor_copy(ebl[:, t, 4:12], e1[:, SEQ:T].rearrange("p (c n) -> p c n", n=8)[:, :, 7])
                tt(V, QG[:, t, :], zo[:, t, :], e1, ALU.mult)
                tt(V, KG[:, t, :], zo[:, 2 + t, :], KG[:, t, :], ALU.mult).then_inc(S("gl_qk"), 1)

            def parts(x, v):
                h = 64 >> v
                n = SEQ if v < 4 else T
                b = x[:, 0:n].rearrange("p (b a h) -> p b a h", a=2, h=h)
                return b[:, :, 0, :], b[:, :, 1, :], h

            def diffs(k):
                t, v = k // 7, k % 7
                low, high, h = parts(XL[:, t, v, :], v)
                bl, bh, _ = parts(BC[:, t, :], v)
                ref = bc(bl[:, :, h - 1], 2, h)
                tt(V, low, ref, bl, ALU.subtract)
                tt(V, high, bh, ref, ALU.subtract).then_inc(S("gl_d"), 1)

            def scales(k):
                t, v = k // 7, k % 7
                dve.wait_ge(S("gl_e"), k + 1)
                low, high, _ = parts(XL[:, t, v, :], v)
                kl, _, _ = parts(zo[:, 2 + t, :], v)
                _, qh_, _ = parts(zo[:, t, :], v)
                tt(V, low, low, kl, ALU.mult)
                tt(V, high, high, qh_, ALU.mult).then_inc(S("gl_x"), 1)

            diffs(0)
            diffs(1)
            for k in range(14):
                if k < 12:
                    diffs(k + 2)
                scales(k)
            V.memset(Sg, 0.0).then_inc(S("gl_st"), 1)
            for c in range(NCH + 1):
                n = L if c < NCH else NSAMP
                nl = 8 if c < NCH else 4
                m = c_("gla", 1024) if c < NCH else c_("gla_s", 256, 64)
                for h in range(GH):
                    w = attw[0:n, h % 2, 0:nl * n]
                    dve.wait_ge(S("gl_sc"), 4 * c + h + 1)
                    if c == NCH and h == 0:
                        V.memset(attg[NSAMP:P, :, 0:NSAMP], 0.0)
                    if c < NCH:
                        tt(V, w.rearrange("p (a b) -> p a b", a=2), PP[h % 2][:, :, :],
                           m.rearrange("p (a b) -> p a b", a=2), ALU.mult).then_inc(S("gl_am"), 1)
                    else:
                        tt(V, w, PP[h % 2][0:n, 0, 0:256], m, ALU.mult).then_inc(S("gl_am"), 1)
                    dve.wait_ge(S("gl_am"), 4 * c + h + 1)
                    V.tensor_reduce(attg[0:n, h, 0:n], w.rearrange("p (v n) -> p n v", v=nl), AX.X,
                                    ALU.add).then_inc(S("gl_at"), 1)
                if c < NCH:
                    dve.wait_ge(S("gl_s"), c + 1)
                    for t in range(2):
                        last = stt(Sg[:, t, :], Sg[:, t, :], ebl[:, t, c:c + 1], bank(5)[:, 256 + t * P:256 + (t + 1) * P],
                                   ALU.mult, ALU.add)
                    last.then_inc(S("gl_st"), 1)
                    dve.wait_ge(S("gl_st"), c + 2)
            dve.wait_ge(S("gl_tokc"), NCH + 1)
            for h in range(GH):
                last = tt(V, Vm[:, h], bc(vt[0:64, h, :], 1, 8), bc(seqmask[0:64, :], 2, P), ALU.mult)
            last.then_inc(S("gs_vm"), 1)
            dve.wait_ge(S("gl_o"), NCH + 1)
            dve.wait_ge(S("gS_in"), 16)
            for t in range(2):
                chain(tt(V, SSg[:, t], SSg[:, t], bc(ebl[:, t, 4:12], 2, P), ALU.mult))
                dve.wait_ge(S("gs_s"), t + 1)
                s4 = SSg[:, t].rearrange("p (a j) n -> p a (j n)", a=2)
                tt(V, s4, s4, PP[t][:, :, :], ALU.add).then_inc(S("gs_st"), 1)
            head_norm("gn", zo[:, 0:4, :], LAX, GDV, mean=False)
            dve.wait_ge(S("sG_written"), 16)
            for h in range(4):
                stt(hT[:, h, :], zo[:, h, :], v_("o_ln_g", h), zo[:, 8 + h, :], ALU.mult,
                    ALU.mult).then_inc(S("ycat"), 1)

            dve.wait_ge(S("ycat"), 12)
            for k in range(4):
                last = V.tensor_copy(up[:, k], zo[:, 12 + k, :].rearrange("p (b s) -> p s b", s=BL))
            last.then_inc(S("s5_up"), 1)
            dve.wait_ge(S("s5_step"), 1)
            chain(tt(V, t_a, l_re, t_s, ALU.mult))
            chain(tt(V, t_b, l_im, t_s, ALU.mult))
            for out, shift in ((t_s, 0.0), (t_c, np.pi / 2)):
                chain(V.tensor_scalar(t_n, t_b, 1.0 / TWO_PI, shift / TWO_PI, ALU.mult, ALU.add))
                chain(V.tensor_scalar(t_n, t_n, ROUND, None, ALU.add))
                chain(V.tensor_scalar(t_n, t_n, -ROUND, None, ALU.add))
                chain(stt(out, t_n, -6.28125, t_b, ALU.mult, ALU.add))
                chain(stt(out, t_n, -(TWO_PI - 6.28125), out, ALU.mult, ALU.add))
                chain(V.tensor_scalar(out, out, float(shift), 3.1415925, ALU.add, ALU.min))
                ins = V.tensor_scalar(out, out, -3.1415925, None, ALU.max)
                if shift:
                    ins.then_inc(S("s5_ab"), 1)
                else:
                    chain(ins)
            dve.wait_ge(S("s5_trig"), 1)
            chain(tt(V, lr, t_er, t_c, ALU.mult))
            chain(tt(V, li, t_er, t_s, ALU.mult))
            V.tensor_scalar(lis, li, v_("sgn"), None, ALU.mult).then_inc(S("s5_lam"), 1)
            dve.wait_ge(S("s5_lam"), 1)
            chain(tt(V, t_d, l_re, l_re, ALU.mult))
            chain(tt(V, t_e, l_im, l_im, ALU.mult))
            chain(tt(V, t_d, t_d, t_e, ALU.add))
            chain(V.reciprocal(t_d, t_d))
            chain(V.tensor_scalar(t_f, lr, -1.0, None, ALU.add))
            for out, x, y, op in ((wr, l_re, l_im, ALU.add), (wi, l_im, l_re, ALU.subtract)):
                chain(tt(V, out, t_f, x, ALU.mult))
                chain(tt(V, t_e, li, y, ALU.mult))
                if op == ALU.add:
                    chain(tt(V, out, out, t_e, ALU.add))
                else:
                    chain(tt(V, out, t_e, out, ALU.subtract))
                chain(tt(V, out, out, t_d, ALU.mult))
            chain(V.tensor_scalar(wis, wi, v_("sgn"), None, ALU.mult))

            def turn(out, osw, x, xsw, r, i, done=None):
                r, i = bc(r, 2, SC), bc(i, 2, SC)
                chain(tt(V, out, x, r, ALU.mult))
                chain(tt(V, ft, xsw, i, ALU.mult))
                chain(tt(V, out, out, ft, ALU.add))
                chain(tt(V, osw, xsw, r, ALU.mult))
                chain(tt(V, ft, x, i, ALU.mult))
                tt(V, osw, osw, ft, ALU.subtract).then_inc(S("s5_f"), 1)
                dve.wait_ge(S("s5_f"), done)

            turn(FZ[:, :, BL - 1, :], fsw[:, 0], BC4[:, 0], BC4[:, 1], wr, wis, 1)
            for k in range(1, BL):
                s = BL - 1 - k
                turn(FZ[:, :, s, :], fsw[:, k % 2], FZ[:, :, s + 1, :], fsw[:, (k + 1) % 2], lr, lis, k + 1)
            chain(V.tensor_copy(lr8, lr))
            chain(V.tensor_copy(li8, li))
            for _ in range(3):
                chain(tt(V, t_d, lr8, lr8, ALU.mult))
                chain(tt(V, t_e, li8, li8, ALU.mult))
                chain(tt(V, li8, lr8, li8, ALU.mult))
                chain(V.tensor_scalar(li8, li8, 2.0, None, ALU.mult))
                chain(tt(V, lr8, t_d, t_e, ALU.subtract))
            chain(V.tensor_scalar(lis8, li8, v_("sgn"), None, ALU.mult))
            chain(V.tensor_scalar(li2[:, 1, :], lis8, -1.0, None, ALU.mult))
            chain(V.memset(cur[:, 0].rearrange("p a b -> p (a b)"), 0.0))
            dve.wait_ge(S("s5_g"), 8)
            dve.wait_ge(S("s5_kc"), 8)
            chain(V.memset(XX[:, :, 0:1], 0.0))
            dve.wait_ge(S("zsw_in"), 32)
            r2 = bc(lr8, 1, 2)

            def step(x, y, z, dst):
                tt(V, sc1, x[:, 0:2, :], r2, ALU.mult)
                chain(tt(V, sc2, x[:, 1:3, :], li2, ALU.mult))
                chain(tt(V, sc1, sc1, sc2, ALU.add))
                chain(tt(V, y[:, 0:2, :], sc1, z, ALU.add))
                V.tensor_copy(dst, y[:, 0, :])
                chain(V.tensor_copy(y[:, 2, :], y[:, 0, :]))

            with dve.Fori(0, NBP // 2) as i:
                chain.loop(i, 8)
                for e in range(2):
                    z = ZZ[:, :, :, bass.ds(2 * i + e, 1)].rearrange("p k g a -> p k (g a)")
                    dst = XX[:, :, bass.ds(2 * i + e + 1, 1)].rearrange("p g a -> p (g a)")
                    step(cur[:, e], cur[:, 1 - e], z, dst)
                chain.end_loop(NBP // 2)
            V.tensor_copy(SO[:, :, 0], cur[:, 0, 0, :]).then_inc(S("s5_end"), 1)
            dve.wait_ge(S("x0_in"), 32)
            x0 = x0st
            tt(V, st1, x0, bc(lr8, 2, 8), ALU.mult)
            chain(tt(V, st2, x0sw, bc(lis8, 2, 8), ALU.mult))
            chain(tt(V, st1, st1, st2, ALU.add))
            tt(V, SO[:, :, 1:9], st1, ZZ[:, 0, :, NBP:NB], ALU.add).then_inc(S("s5_so"), 1)
            V.tensor_copy(XX[:, :, NBP:NB], x0).then_inc(S("s5_scan"), 1)
            dve.wait_ge(S("Y_in"), 16)
            dve.wait_ge(S("s5_y"), 8)
            for k in range(4):
                stt(Yf_tok[:, k, :].rearrange("p (b s) -> p b s", s=BL),
                    zo[:, 12 + k, :].rearrange("p (b s) -> p b s", s=BL), v_("o_d", k),
                    Yf[:, k].rearrange("p s b -> p b s"), ALU.mult, ALU.add).then_inc(S("s5_ys"), 1)
            for m in range(4):
                dve.wait_ge(S("s5_sig"), m + 1)
                tt(V, hT[:, 4 + m, :], Yf_tok[:, m, :], sgl[:, m, :], ALU.mult).then_inc(S("ycat"), 1)
            residual("o_out")

        @block.sync
        def _(sp):
            def stream(name):
                t0, n = RUNS[name]
                n = min(n, last_tile - t0 - 2)
                if n <= 0:
                    return
                with sp.Fori(0, n // 2) as i:
                    for s in range(2):
                        sp.wait_ge(S("proj_done"), 2 * i + (USE[name] + s + 1))
                        sp.dma_start(w_ring[:, s, :], d["w"][bass.ds(2 * i + (t0 + 2 + s), 1)].rearrange(
                            "a p n -> p (a n)")).then_inc(WL[s], 16)

            nout = [0]

            def out(name, src):
                nout[0] += 16
                sp.dma_start(o[name], src).then_inc(S("out_written"), 16)

            sp.dma_start(cst[:], d["consts"]).then_inc(S("consts_in"), 16)
            for k in range(KT):
                sp.dma_start(xT[:, k, :], d["x"][:, k, :]).then_inc(S("x_in"), 16)
            sp.dma_start(vec[:], d["vec"]).then_inc(S("vec_in"), 16)
            sp.dma_start(wif, d["w_if"]).then_inc(S("e_small_in"), 16)
            for s in range(2):
                sp.dma_start(w_ring[:, s, :], d["w"][s]).then_inc(WL[s], 16)
            sp.dma_start(shin, d["shift"]).then_inc(S("e_small_in"), 16)
            sp.dma_start(lora, d["lora"]).then_inc(S("e_small_in"), 16)
            sp.dma_start(r_m0[:, 0:8], d["m0"]).then_inc(S("e_small_in"), 16)
            sp.dma_start(convp[:], d["convp"]).then_inc(S("e_small_in"), 16)
            stream("e_in")
            sp.wait_ge(S("proj_done"), E_TILES)
            sp.dma_start(Csf, d["C"]).then_inc(S("C_in"), 16)
            for s in range(2):
                sp.wait_ge(S(f"ext_free{s}"), 1 + 7)
            out("shift", shout)
            sp.wait_ge(S("ml_m_out"), 1)
            out("m", r_mo[:, 0:NSEQ])
            sp.wait_ge(S("ml_state"), 4)
            out("pC", Cst)
            sp.wait_ge(S("ml_sst"), 11)
            sp.dma_start(o["sC"], Csf).then_inc(S("sC_written"), 16)
            sp.wait_ge(S("rw_prep"), 4)
            sp.dma_start(SS, d["rS"]).then_inc(S("rS_in"), 16)
            sp.wait_ge(S("rk_st"), NCR + 1)
            out("pS", Sr)
            sp.wait_ge(S("rs_st"), 1)
            sp.dma_start(o["sS"], SS).then_inc(S("sS_written"), 16)
            stream("e_out")
            sp.wait_ge(S("sS_written"), 16)
            stream("ffn0")
            for s in range(2):
                sp.wait_ge(S(f"ext_free{s}"), 1 + 7 + FT)
            out("conv0", convout)
            if do_odd:
                odd_sp(sp, stream, out)
            if not do_odd:
                all_free(sp, "down0", 8)
                out("y", xT[:])
            sp.wait_ge(S("sC_written"), 16)
            sp.wait_ge(S("out_written"), nout[0])

        @block.gpsimd
        def _(pool):
            def down(l):
                pool.wait_ge(S("proj_done"), USE["e_out" if l == 0 else "o_out"] + 8)
                if l == 1:
                    pool.wait_ge(S("out_written"), 16 * 7)
                pool.dma_start(convin, d["conv_state"][l]).then_inc(S("convin_in"), 16)
                for s in range(2):
                    pool.dma_start(down_ring[:, s, :], d["w_down"][8 * l + s]).then_inc(DL[s], 16)
                with pool.Fori(0, 3) as i:
                    for s in range(2):
                        pool.wait_ge(S("proj_done"), 2 * i + (USE[f"down{l}"] + s + 1))
                        pool.dma_start(down_ring[:, s, :], d["w_down"][bass.ds(2 * i + (8 * l + 2 + s), 1)].rearrange(
                            "a p n -> p (a n)")).then_inc(DL[s], 16)

            down(0)
            if do_odd:
                odd_pool(pool)
                down(1)

        @block.tensor
        def _(pe):
            def norm(n):
                for k in range(KT):
                    pe.wait_ge(S("sq_ready"), 8 * n + k + 1)
                    for a in range(2):
                        last = mm(PP[3][:, a, 0:TH], ones, sq[:, k % 2, a * TH:(a + 1) * TH], k == 0, k == KT - 1)
                    last.then_inc(S("sq_used"), 1)

            def project(name, rhs):
                t0, n = RUNS[name]
                with pe.Fori(0, n // 2) as i:
                    for s in range(2):
                        pe.wait_ge(WL[s], 16 * i + 16 * (t0 // 2 + 1))
                        pe.wait_ge(FREE[s], i + (USE[name] // 2 + 1))
                        for a in range(2):
                            for k in range(KT):
                                last = mm(PP[s][:, a, 0:TH], w_ring[:, s, k * P:(k + 1) * P],
                                          rhs[:, k, a * TH:(a + 1) * TH], k == 0, k == KT - 1)
                        last.then_inc(S("proj_done"), 1)

            def down(l):
                pe.wait_ge(S("act_ready"), FT * (l + 1))
                with pe.Fori(0, 4) as i:
                    for s in range(2):
                        pe.wait_ge(DL[s], 16 * i + 16 * (4 * l + 1))
                        pe.wait_ge(FREE[s], i + (USE[f"down{l}"] // 2 + 1))
                        for a in range(2):
                            for k in range(FT):
                                last = mm(PP[s][:, a, 0:TH], down_ring[:, s, k * P:(k + 1) * P],
                                          actv[:, k, a * TH:(a + 1) * TH], k == 0, k == FT - 1)
                        last.then_inc(S("proj_done"), 1)

            def head_norm(nm, src, sqs, avg, mean=True):
                if mean:
                    for h in range(4):
                        pe.wait_ge(S("hn_src"), HN[nm] + h + 1)
                        for a in range(2):
                            last = mm(PP[h][:, a, 0:TH], avg, src[:, h, a * TH:(a + 1) * TH])
                        last.then_inc(S("hn_mean"), 1)
                for h in range(4):
                    pe.wait_ge(S("hn_sq"), HN[nm] + h + 1)
                    for a in range(2):
                        last = mm(PP[h][:, a, 0:TH], avg, sqs[:, h, a * TH:(a + 1) * TH])
                    last.then_inc(S("hn_var"), 1)

            def mlstm():
                pe.wait_ge(S("ml_exps"), 4)
                pe.wait_ge(FREE[0], USE["e_out"] // 2 + 1)
                pe.wait_ge(FREE[1], USE["e_out"] // 2 + 1)
                for h in range(MH):
                    if h >= 2:
                        pe.wait_ge(S("ml_qh"), h - 1)
                    for a in range(2):
                        last = mm(PP[h % 2][:, a, 0:TH], sel[:, h, :], r_s[:, a * TH:(a + 1) * TH])
                    last.then_inc(S("ml_bcast"), 1)
                for h in range(MH):
                    mm(bank(4)[:, 12 * h:12 * h + 12], sel[:, h, :], r_dec[:, 0:12])
                for c in range(NCH + 1):
                    n = L if c < NCH else NSAMP
                    last = mm(bank(4)[0:n, 48 + 4 * c:52 + 4 * c], r_w[:, L * c:L * c + n], ident[0:4, 0:4])
                last.then_inc(S("ml_small"), 1)
                pe.wait_ge(S("ml_qh"), 4)
                for c in range(NCH + 1):
                    n, c0 = (L, L * c) if c < NCH else (NSAMP, SEQ)
                    cols = slice(c0, c0 + n)
                    if c:
                        pe.wait_ge(S("ml_att"), c)
                    for h in range(MH):
                        mm(bank(0)[0:n, h * n:(h + 1) * n], zm[:, 4 + h, cols], zm[:, h, cols])
                    for h in range(MH):
                        mm(bank(1)[0:n, h * n:(h + 1) * n], sel[:, h, 0:n], r_a[:, cols], True, False)
                        last = mm(bank(1)[0:n, h * n:(h + 1) * n], r_i[:, cols], sel[:, h, 0:n], False, True)
                    last.then_inc(S("ml_scores"), 1)
                    if c:
                        pe.wait_ge(S("ml_tokc"), c)
                    for h in range(MH):
                        nc.tensor.transpose(bank(2)[0:n, h * P:(h + 1) * P], zm[:, 8 + h, cols], ident)
                    for h in range(MH):
                        last = nc.tensor.transpose(bank(3)[0:n, h * P:(h + 1) * P], zm[:, 4 + h, cols], ident)
                    last.then_inc(S("ml_tok"), 1)
                    pe.wait_ge(S("ml_att"), c + 1)
                    pe.wait_ge(S("ml_tokc"), c + 1)
                    pe.wait_ge(S("ml_qn"), c + 1)
                    if c:
                        pe.wait_ge(S("ml_outc"), c)
                    for h in range(MH):
                        num, den = (bank(b)[:, h * n:(h + 1) * n] for b in (4, 5))
                        mm(num, vaug[0:n, h, 0:P], att[0:n, h, 0:n], True, False)
                        if c < NCH:
                            mm(num, Cst[:, h, 0:P], qh[:, h, cols], False, True)
                        else:
                            if h == 0:
                                pe.wait_ge(S("C_in"), 16)
                            for j in range(8):
                                mm(num[:, 8 * j:8 * j + 8], Cs[:, h, j, 0:P], qh[:, h, c0 + 8 * j:c0 + 8 * j + 8],
                                   False, j == 7)
                        mm(den, ones[0:n, :], att[0:n, h, 0:n], True, False)
                        last = mm(den, ones, qn[:, h, 0:n], False, True)
                    last.then_inc(S("ml_nd"), 1)
                    if c < NCH:
                        for h in range(MH):
                            last = mm(bank(6 + h // 2)[:, 129 * (h % 2):129 * (h % 2) + 129], ktok[:, h, :],
                                      vaug[:, h, :])
                        last.then_inc(S("ml_upd"), 1)
                    else:
                        pe.wait_ge(S("ml_km"), 1)
                        for g in range(11):
                            if g >= 2:
                                pe.wait_ge(S("ml_sst"), g - 1)
                            for e in range(3 * g, min(3 * g + 3, 32)):
                                last = mm(bank(6 + g % 2)[:, 129 * (e - 3 * g):129 * (e - 3 * g) + 129],
                                          Km[:, e // 8, e % 8, :], vaug[0:64, e // 8, :])
                            last.then_inc(S("ml_supd"), 1)
                pe.wait_ge(S("ml_outc"), 5)
                pe.wait_ge(S("ml_sst"), 11)
                for h in range(MH):
                    for a in range(2):
                        last = mm(PP[h][:, a, 0:TH], sel[:, h, :], r_e[:, a * TH:(a + 1) * TH])
                    last.then_inc(S("ml_emt"), 1)
                head_norm("mn", zm[:, 4:8, :], zm[:, 8:12, :], ones)

            def rwkv():
                for p in range(RP):
                    pe.wait_ge(S("rw_kksq"), p + 1)
                    for a in range(2):
                        last = mm(PP[p][:, a, 0:TH], headones, AR[:, p, 1, a * TH:(a + 1) * TH])
                    last.then_inc(S("rw_kkn"), 1)
                pe.wait_ge(S("rw_lora"), 2)
                pe.wait_ge(S("rw_kkmax"), 4)
                for p in range(RP):
                    if p >= 2:
                        pe.wait_ge(S("rw_sig"), 2 * (p - 1))
                    for q, r in ((0, 0), (1, 64)):
                        for a in range(2):
                            last = mm(PP[2 * (p % 2) + q][:, a, 0:TH], lora[r:r + 64, 0, p * P:(p + 1) * P],
                                      zr[r:r + 64, 12, a * TH:(a + 1) * TH])
                    last.then_inc(S("rw_up"), 1)
                pe.wait_ge(S("rw_sig"), 8)

                def rows2():
                    return [(slice(64 * h, 64 * h + 64)) for h in range(2)]

                def scores(c):
                    cols = slice(LR * c, LR * c + LR)
                    for p in range(RP):
                        pe.wait_ge(S("rw_prep"), p + 1)
                        if 4 * c + p >= 2:
                            pe.wait_ge(S("rk_g"), 4 * c + p - 1)
                        b = bank(p % 2)
                        for r in rows2():
                            mm(b[r, 0:128], BK[r, p, 0, cols], AR[r, p, :, cols])
                            mm(b[r, 128:256], BK[r, p, 1, cols], AR[r, p, :, cols])
                            last = mm(b[r, 256:320], AR[r, p, 0, cols], BK[r, p, 0, cols])
                        last.then_inc(S("rk_sc"), 1)

                def tokens(c):
                    cols = slice(LR * c, LR * c + LR)
                    for q in range(2):
                        if 2 * c + q >= 1:
                            pe.wait_ge(S("rk_tokc"), 2 * c + q)
                        for p in (2 * q, 2 * q + 1):
                            for r in rows2():
                                for k, src in enumerate((BK[r, p, 0, cols], BK[r, p, 1, cols], zr[r, 8 + p, cols])):
                                    e = 192 * (p % 2) + 64 * k
                                    last = mm(bank(4)[r, e:e + 64], src, ident[r, r])
                        last.then_inc(S("rk_tok"), 1)

                def level(c, k):
                    top = 5 if c < NCR else 2
                    for q in range(2):
                        if k == 0:
                            pe.wait_ge(S("rk_g"), 4 * c + 2 * q + 2)
                            if c:
                                pe.wait_ge(S(f"rk_lc{q}"), 6 * c)
                        else:
                            pe.wait_ge(S(f"rk_lc{q}"), 6 * c + k)
                        for pp in range(2):
                            p = 2 * q + pp
                            b = PP[1][:, q, 192 * pp:192 * pp + 192]
                            for r in rows2():
                                if k == 0:
                                    mm(b[r, 0:64], Gs[r, c % 2, p, 256:320], Gs[r, c % 2, p, 0:64])
                                    last = mm(b[r, 128:192], Gs[r, c % 2, p, 0:64], Gs[r, c % 2, p, 256:320])
                                    continue
                                v = XPA[r, q, k % 2, pp, :, :]
                                if k < top:
                                    mm(b[r, 0:128], v[:, 2, :], v[:, 0:2, :])
                                    last = mm(b[r, 128:192], v[:, 0, :], v[:, 2, :])
                                else:
                                    last = mm(b[r, 64:128], v[:, 2, :], v[:, 1, :])
                        last.then_inc(S(f"rk_lv{q}"), 1)

                def seq_r1(c):
                    g = c % 2
                    pe.wait_ge(S("rk_tokc"), 2 * c + 2)
                    pe.wait_ge(S("rk_st"), c + 1 if c < NCR else NCR + 1)
                    if c == NCR:
                        pe.wait_ge(S("rS_in"), 16)
                        pe.wait_ge(S("rk_uc"), c)
                        for p in range(RP):
                            for r in rows2():
                                for j in range(8):
                                    e = SEQ + 8 * j
                                    last = mm(bank(5)[r, 64 * p + 8 * j:64 * p + 8 * j + 8], SS[r, p, j, :],
                                              AR[r, p, 0, e:e + 8])
                        last.then_inc(S("rs_qt"), 1)
                        pe.wait_ge(S("rs_qtc"), 1)
                    elif c:
                        pe.wait_ge(S("rk_uc"), c)
                    for p in range(RP):
                        for r in rows2():
                            out = bank(5)[r, 64 * p:64 * p + 64]
                            if c < NCR:
                                mm(out, AR[r, p, 0, LR * c:LR * c + LR], Sr[r, p, :], True, False)
                            else:
                                mm(out, QT[r, p, :], ident[r, r], True, False)
                            last = mm(out, Gs[r, g, p, 128:192], tok[r, g, p, 2, :], False, True)
                    last.then_inc(S("rk_r1"), 1)

                def seq_u(c):
                    pe.wait_ge(S("rk_r1c"), c + 1)
                    for q in range(2):
                        pe.wait_ge(S(f"rk_lc{q}"), 6 * c + (6 if c < NCR else 3))
                    for p in range(RP):
                        for r in rows2():
                            last = mm(bank(5)[r, 256 + 64 * p:320 + 64 * p], PF[r, c % 2, p, :], R1[r, p, :])
                    last.then_inc(S("rk_u"), 1)

                def seq_ys(c):
                    g = c % 2
                    pe.wait_ge(S("rk_uc"), c + 1)
                    if c:
                        pe.wait_ge(S("rk_yc"), c)
                    for p in range(RP):
                        for r in rows2():
                            out = bank(6)[r, 64 * p:64 * p + 64]
                            mm(out, U[r, p, :], Gs[r, g, p, 64:128], True, False)
                            mm(out, tok[r, g, p, 2, :], Gs[r, g, p, 192:256], False, False)
                            if c < NCR:
                                last = mm(out, Sr[r, p, :], AR[r, p, 1, LR * c:LR * c + LR], False, True)
                            else:
                                for j in range(8):
                                    e = SEQ + 8 * j
                                    last = mm(out[:, 8 * j:8 * j + 8], SS[r, p, j, :], AR[r, p, 1, e:e + 8],
                                              False, j == 7)
                    last.then_inc(S("rk_y"), 1)
                    if c < NCR:
                        for p in range(RP):
                            for r in rows2():
                                out = bank(7)[r, 64 * p:64 * p + 64]
                                mm(out, tok[r, g, p, 0, :], U[r, p, :], True, False)
                                last = mm(out, tok[r, g, p, 1, :], tok[r, g, p, 2, :], False, True)
                        last.then_inc(S("rk_s"), 1)
                        return
                    pe.wait_ge(S("rs_uvm"), 1)
                    for p in range(RP):
                        if p >= 2:
                            pe.wait_ge(S("rs_sc"), p - 1)
                        for r in rows2():
                            mm(bank(p % 2)[r, :], tok[r, g, p, 0, :], UVm[r, 0, p, :, :], True, False)
                            last = mm(bank(p % 2)[r, :], tok[r, g, p, 1, :], UVm[r, 1, p, :, :], False, True)
                        last.then_inc(S("rs_s"), 1)

                for c in range(NCR + 1):
                    scores(c)
                    tokens(c)
                    level(c, 0)
                    if c:
                        seq_r1(c - 1)
                    level(c, 1)
                    if c:
                        seq_u(c - 1)
                    level(c, 2)
                    if c:
                        seq_ys(c - 1)
                    if c < NCR:
                        for k in (3, 4, 5):
                            level(c, k)
                seq_r1(NCR)
                seq_u(NCR)
                seq_ys(NCR)
                pe.wait_ge(S("rs_sc"), 4)
                pe.wait_ge(S("rk_yc"), NCR + 1)
                head_norm("rn", yr, AR[:, :, 0, :], headones)
                for p in range(RP):
                    pe.wait_ge(S("hn_std"), HN["rn"] + p + 1)
                    for a in range(2):
                        last = mm(PP[p][:, a, 0:TH], headones, rkp[:, p, a * TH:(a + 1) * TH])
                    last.then_inc(S("rw_bonus"), 1)
                for p in range(RP):
                    pe.wait_ge(S("rw_bonusc"), p + 1)
                    for a in range(2):
                        last = mm(PP[p][:, a, 0:TH], lora[:, 1, p * P:(p + 1) * P], zr[:, 13, a * TH:(a + 1) * TH])
                    last.then_inc(S("rw_gate"), 1)

            pe.wait_ge(S("consts_in"), 16)
            norm(0)
            pe.wait_ge(S("h_ready"), 8)
            pe.wait_ge(S("e_small_in"), 16 * 5)
            for a in range(2):
                for k in range(KT):
                    last = mm(PP[2][0:36, a, 0:TH], wif[:, k, :], hT[:, k, a * TH:(a + 1) * TH], k == 0, k == KT - 1)
            last.then_inc(S("gates_done"), 1)
            project("e_in", hT)
            mlstm()
            rwkv()
            pe.wait_ge(S("ycat"), 8)
            project("e_out", hT)
            norm(1)
            pe.wait_ge(S("h_ready"), 16)
            project("ffn0", hT)
            down(0)
            if do_odd:
                odd_pe(pe, norm, project, head_norm)
                norm(3)
                pe.wait_ge(S("h_ready"), 32)
                project("ffn1", hT)
                down(1)
                norm(4)

        @block.scalar
        def _(act):
            A = nc.scalar.activation
            chain = Chain(act, S("act_chain"))

            def norm(n):
                for k in range(KT):
                    if n == 0:
                        act.wait_ge(S("x_in"), 16 * KT)
                    else:
                        act.wait_ge(FREE[k % 2], USE[ADDS[n - 1]] // 2 + k // 2 + 2)
                    if 8 * n + k >= 2:
                        act.wait_ge(S("sq_used"), 8 * n + k - 1)
                    A(sq[:, k % 2, :], xT[:, k, :], ACT.Square).then_inc(S("sq_ready"), 1)
                act.wait_ge(S("sq_used"), 8 * n + 8)
                A(halves(rstd[:, :]), pair(3), ACT.Sqrt, scale=1.0 / D_MODEL, bias=EPS).then_inc(S("rms_sqrt"), 1)

            def evac(name, j0, n, func, dst, scale=1.0):
                with act.Fori(0, n // 2) as i:
                    for s in range(2):
                        act.wait_ge(S("proj_done"), 2 * i + (USE[name] + j0 + s + 1))
                        out = dst[:, bass.ds(2 * i + s, 1), :].rearrange("p a n -> p (a n)")
                        A(halves(out), pair(s), func, scale=scale).then_inc(FREE[s], 1)

            def to_ext(s, lead):
                e = ext[:, s, :]
                A(e[:, lead:lead + TH], PP[s][:, 0, 0:TH], ACT.Copy)
                A(e[:, lead + TH:lead + SEQ], PP[s][:, 1, 0:SEQ - TH], ACT.Copy)
                samp = e[:, lead + SEQ:lead + SEQ + (8 + lead) * 8].rearrange("p (j n) -> p j n", j=8)
                return A(samp[:, :, lead:lead + 8],
                         PP[s][:, 1, SEQ - TH:TH].rearrange("p (j n) -> p j n", j=8), ACT.Copy)

            def head_norm(nm, src, sqs, n, eps, mean=True):
                for h in range(4):
                    act.wait_ge(S("hn_xc" if mean else "hn_src"), HN[nm] + h + 1)
                    A(sqs[:, h, :], src[:, h, :], ACT.Square).then_inc(S("hn_sq"), 1)
                for h in range(4):
                    act.wait_ge(S("hn_var"), HN[nm] + h + 1)
                    A(halves(sqs[:, h, :]), pair(h), ACT.Sqrt, scale=1.0 / n, bias=eps).then_inc(S("hn_std"), 1)

            def ffn(l):
                base = USE[f"ffn{l}"]
                with act.Fori(0, FT) as i:
                    for s in range(2):
                        act.wait_ge(S("proj_done"), 2 * i + (base + s + 1))
                        act.wait_ge(S(f"ext_free{s}"), i + (1 + 7 + FT * l))
                        to_ext(s, 2).then_inc(FREE[s], 1)
                    act.wait_ge(S("gate_conv"), i + (1 + FT * l))
                    A(cv[:, 2, :], cv[:, 1, :], ACT.Silu).then_inc(S("silu_done"), 1)

            norm(0)
            act.wait_ge(S("vec_in"), 16)
            act.wait_ge(S("gates_done"), 1)
            A(halves(r_i), PP[2][0:4, :, 0:TH], ACT.Identity, bias=v_("b_if", rows=4))
            chain(A(halves(r_f), PP[2][32:36, :, 0:TH], ACT.Identity, bias=v_("b_if", rows=4, r0=32)))
            chain(A(r_B, r_f, ACT.Abs))
            chain(A(r_B, r_B, ACT.Exp, scale=-1.0))
            A(r_B, r_B, ACT.Ln, bias=1.0).then_inc(S("ml_softplus"), 1)
            evac("e_in", 0, 4, ACT.Copy, zm[:, 0:4, :])
            evac("e_in", 4, 4, ACT.Copy, zm[:, 4:8, :], MHD ** -0.5)
            evac("e_in", 8, 4, ACT.Copy, zm[:, 8:12, :])
            evac("e_in", 12, 4, ACT.Sigmoid, zm[:, 12:16, :])
            with act.Fori(0, 7) as i:
                for s in range(2):
                    act.wait_ge(S("proj_done"), 2 * i + (16 + s + 1))
                    act.wait_ge(S(f"ext_free{s}"), i + 1)
                    to_ext(s, 1).then_inc(FREE[s], 1)
            act.wait_ge(S("ml_rows"), 1)
            for r in (r_s, r_w, r_dec[:, 0:12]):
                A(r, r, ACT.Exp).then_inc(S("ml_exps"), 1)
            A(r_e, r_m, ACT.Exp, scale=-1.0).then_inc(S("ml_exps"), 1)
            for c in range(NCH + 1):
                n, c0 = (L, L * c) if c < NCH else (NSAMP, SEQ)
                act.wait_ge(S("ml_dm"), c + 1)
                dm = Dm[0:n, :, :].rearrange("p a b -> p (a b)")[:, 0:4 * n]
                A(dm, dm, ACT.Exp).then_inc(S("ml_w"), 1)
                act.wait_ge(S("ml_nd"), c + 1)
                for b, k in ((4, 4), (5, 8)):
                    last = A(zm[:, k:k + 4, c0:c0 + n], bank(b)[:, 0:4 * n].rearrange("p (h n) -> p h n", h=4), ACT.Copy)
                last.then_inc(S("ml_outc"), 1)
            act.wait_ge(S("ml_outc"), NCH + 1)
            for h in range(MH):
                A(zm[:, 8 + h, :], zm[:, 8 + h, :], ACT.Abs).then_inc(S("ml_abs"), 1)
            head_norm("mn", zm[:, 4:8, :], zm[:, 8:12, :], MHD, EPS)
            act.wait_ge(S("shifted"), 14)
            A(zr[0:64, 12, :], zr[0:64, 12, :], ACT.Tanh).then_inc(S("rw_lora"), 1)
            A(zr[:, 13, :], zr[:, 13, :], ACT.Sigmoid).then_inc(S("rw_lora"), 1)
            for p in range(RP):
                act.wait_ge(S("rw_kk"), p + 1)
                A(AR[:, p, 1, :], AR[:, p, 0, :], ACT.Square).then_inc(S("rw_kksq"), 1)
            for p in range(RP):
                act.wait_ge(S("rw_kkmax"), p + 1)
                A(AR[:, p, 1, :], AR[:, p, 1, :], ACT.Sqrt).then_inc(S("rw_kksqrt"), 1)
            for p in range(RP):
                act.wait_ge(S("rw_up"), p + 1)
                if p == 0:
                    act.wait_ge(S("ycat"), 4)
                if p >= 2:
                    act.wait_ge(S("rw_prep"), p - 1)
                for q, b in ((0, "w0"), (1, "a0")):
                    A(halves(prep[:, q, p % 2, :]), pair(2 * (p % 2) + q), ACT.Sigmoid,
                      bias=v_(b, p)).then_inc(S("rw_sig"), 1)
                act.wait_ge(S("rw_cum"), p + 1)
                A(prep[:, 4, p % 2, :], prep[:, 2, p % 2, :], ACT.Exp, scale=-1.0)
                A(prep[:, 2, p % 2, :], prep[:, 2, p % 2, :], ACT.Exp)
                A(prep[:, 3, p % 2, :], prep[:, 3, p % 2, :], ACT.Exp).then_inc(S("rw_exp"), 1)

            def r1_copy(c):
                if c == NCR:
                    act.wait_ge(S("rs_qt"), 1)
                    A(QT, bank(5)[:, 0:256].rearrange("p (a b) -> p a b", a=4), ACT.Copy).then_inc(S("rs_qtc"), 1)
                act.wait_ge(S("rk_r1"), c + 1)
                A(R1, bank(5)[:, 0:256].rearrange("p (a b) -> p a b", a=4), ACT.Copy).then_inc(S("rk_r1c"), 1)

            def u_copy(c):
                act.wait_ge(S("rk_u"), c + 1)
                A(U, bank(5)[:, 256:512].rearrange("p (a b) -> p a b", a=4), ACT.Copy).then_inc(S("rk_uc"), 1)

            def y_copy(c):
                act.wait_ge(S("rk_y"), c + 1)
                A(yr[:, :, LR * c:LR * c + LR], bank(6)[:, 0:256].rearrange("p (a b) -> p a b", a=4),
                  ACT.Copy).then_inc(S("rk_yc"), 1)

            act.wait_ge(S("rw_prep"), 4)
            for c in range(NCR + 1):
                if c >= 2:
                    act.wait_ge(S("rk_s"), c - 1)
                for q in range(2):
                    act.wait_ge(S("rk_tok"), 2 * c + q + 1)
                    A(tok[:, c % 2, 2 * q:2 * q + 2, :, :].rearrange("p a b c -> p (a b c)"), bank(4)[:, 0:384],
                      ACT.Copy).then_inc(S("rk_tokc"), 1)
                if c:
                    r1_copy(c - 1)
                    u_copy(c - 1)
                    y_copy(c - 1)
            r1_copy(NCR)
            u_copy(NCR)
            y_copy(NCR)
            head_norm("rn", yr, AR[:, :, 0, :], RHD, RWKV_EPS)
            norm(1)
            ffn(0)
            if do_odd:
                odd_act(act, A, chain, norm, evac, head_norm)
                norm(3)
                ffn(1)
                norm(4)

        @block.vector
        def _(dve):
            V = nc.vector
            chain = Chain(dve, S("dve_chain"))

            def norm(n, vname, k0, out=None):
                dve.wait_ge(S("rms_sqrt"), n + 1)
                chain(V.reciprocal(rstd[:, :], rstd[:, :]))
                for k in range(KT):
                    stt(hT[:, k, :], xT[:, k, :], v_(vname, k0 + k), rstd[:, :], ALU.mult,
                        ALU.mult).then_inc(S("h_ready"), 1)

            def residual(name):
                with dve.Fori(0, 4) as i:
                    for s in range(2):
                        dve.wait_ge(S("proj_done"), 2 * i + (USE[name] + s + 1))
                        x = xT[:, bass.ds(2 * i + s, 1), :].rearrange("p a n -> p (a n)")
                        tt(V, halves(x), pair(s), halves(x), ALU.add).then_inc(FREE[s], 1)

            def head_norm(nm, src, sqs, n, mean=True):
                if mean:
                    for h in range(4):
                        dve.wait_ge(S("hn_mean"), HN[nm] + h + 1)
                        stt(halves(src[:, h, :]), pair(h), -1.0 / n, halves(src[:, h, :]), ALU.mult,
                            ALU.add).then_inc(S("hn_xc"), 1)
                for h in range(4):
                    dve.wait_ge(S("hn_std"), HN[nm] + h + 1)
                    chain(V.reciprocal(sqs[:, h, :], sqs[:, h, :]))
                    chain(tt(V, src[:, h, :], src[:, h, :], sqs[:, h, :], ALU.mult))

            def ffn(l):
                base = USE[f"ffn{l}"] // 2
                dve.wait_ge(S("convin_in"), 16 * (l + 1))
                chain(V.memset(ext[:, :, 0:2], 0.0))
                with dve.Fori(0, FT) as i:
                    chain.loop(i, 7)
                    for s in range(2):
                        dve.wait_ge(FREE[s], i + (base + 2))
                        e = ext[:, s, :]
                        samp = e[:, 2 + SEQ:2 + SEQ + 80].rearrange("p (j n) -> p j n", j=8)
                        par = convp[:, l, :].rearrange("p (t s k) -> p t s k", s=2, k=4)[
                            :, bass.ds(i, 1), s, :].rearrange("p a k -> p (a k)")
                        cin = convin.rearrange("p (t s) k -> p t s k", s=2)[:, bass.ds(i, 1), s, :].rearrange(
                            "p a k -> p (a k)").rearrange("p (j n) -> p j n", j=8)
                        cout = convout.rearrange("p (t s) k -> p t s k", s=2)[:, bass.ds(i, 1), s, :].rearrange(
                            "p a k -> p (a k)")
                        chain(V.tensor_copy(samp[:, :, 0:2], cin))
                        c = cv[:, s, :]
                        cs = c[:, SEQ:T].rearrange("p (j n) -> p j n", j=8)
                        V.tensor_scalar(c[:, 0:SEQ], e[:, 0:SEQ], par[:, 0:1], par[:, 3:4], ALU.mult, ALU.add)
                        chain(V.tensor_scalar(cs, samp[:, :, 0:8], par[:, 0:1], par[:, 3:4], ALU.mult, ALU.add))
                        for k in (1, 2):
                            stt(c[:, 0:SEQ], e[:, k:k + SEQ], par[:, k:k + 1], c[:, 0:SEQ], ALU.mult, ALU.add)
                            ins = stt(cs, samp[:, :, k:k + 8], par[:, k:k + 1], cs, ALU.mult, ALU.add)
                            if k == 1 or s == 0:
                                chain(ins)
                            else:
                                ins.then_inc(S("gate_conv"), 1)
                        V.tensor_copy(cout[:, 0:2], e[:, SEQ:SEQ + 2])
                        V.tensor_copy(cout[:, 2:18].rearrange("p (j n) -> p j n", j=8),
                                      samp[:, :, 8:10]).then_inc(S(f"ext_free{s}"), 1)
                    dve.wait_ge(S("silu_done"), i + (1 + FT * l))
                    out = actv[:, bass.ds(i, 1), :].rearrange("p a n -> p (a n)")
                    tt(V, out, cv[:, 0, :], cv[:, 2, :], ALU.mult).then_inc(S("act_ready"), 1)
                    chain.end_loop(FT)

            def mlstm_rows():
                dve.wait_ge(S("ml_softplus"), 1)
                chain(stt(r_f, r_f, 0.0, r_B, ALU.min, ALU.subtract))
                chain(V.tensor_tensor_scan(r_B, c_("scan128", T, 4), r_f, 0.0, ALU.mult, ALU.add))
                dve.wait_ge(S("e_small_in"), 80)
                sf, si = r_a[:, 0:64], r_s[:, 0:64]
                chain(V.tensor_copy(sf, r_f[:, SEQ:T]))
                chain(V.tensor_copy(si, r_i[:, SEQ:T]))
                f8, i8 = (x.rearrange("p (j n) -> p j n", j=8)[:, :, 0] for x in (sf, si))
                chain(tt(V, f8, f8, r_m0[:, 0:8], ALU.add))
                chain(tt(V, i8, i8, f8, ALU.max))
                chain(V.memset(f8, NEG))
                chain(V.tensor_tensor_scan(r_m[:, 0:SEQ], r_f[:, 0:SEQ], r_i[:, 0:SEQ], M_INIT, ALU.add, ALU.max))
                chain(V.tensor_tensor_scan(r_m[:, SEQ:T], sf, si, NEG, ALU.add, ALU.max))
                chain(tt(V, r_i, r_i, r_B, ALU.subtract))
                chain(tt(V, r_a, r_B, r_m, ALU.subtract))
                m_s = r_m[:, SEQ:T].rearrange("p (j n) -> p j n", j=8)[:, :, 7]
                chain(V.memset(r_mp[:, 0:1], M_INIT))
                m_p = r_m[:, 0:SEQ].rearrange("p (c n) -> p c n", n=L)[:, :, L - 1]
                chain(V.tensor_copy(r_mp[:, 1:NCH], m_p[:, 0:NCH - 1]))
                chain(V.tensor_copy(r_mp[:, NCH:NCH + 8], r_m0[:, 0:8]))
                chain(V.tensor_copy(r_rl[:, 0:NCH], r_a[:, 0:SEQ].rearrange("p (c n) -> p c n", n=L)[:, :, L - 1]))
                chain(V.tensor_copy(r_rl[:, NCH:NCH + 8],
                                    r_a[:, SEQ:T].rearrange("p (j n) -> p j n", j=8)[:, :, 7]))
                for dst, src, add in ((r_s, r_a, r_mp), (r_w, r_i, r_rl)):
                    tt(V, dst[:, 0:SEQ].rearrange("p (c n) -> p c n", n=L), src[:, 0:SEQ].rearrange(
                        "p (c n) -> p c n", n=L), bc(add[:, 0:NCH], 2, L), ALU.add)
                    tt(V, dst[:, SEQ:T].rearrange("p (j n) -> p j n", j=8), src[:, SEQ:T].rearrange(
                        "p (j n) -> p j n", j=8), bc(add[:, NCH:NCH + 8], 2, 8), ALU.add)
                tt(V, r_dec[:, 0:12], r_rl[:, 0:12], r_mp[:, 0:12], ALU.add).then_inc(S("ml_rows"), 1)
                V.tensor_copy(r_mo[:, 0:1], r_m[:, SEQ - 1:SEQ])
                V.tensor_copy(r_mo[:, 1:9], m_s).then_inc(S("ml_m_out"), 1)

            def token_shift():
                dve.wait_ge(S("e_small_in"), 80)
                chain(V.memset(ext[:, :, 0:1], 0.0))
                for s in range(2):
                    dve.sem_inc(S(f"ext_free{s}"), 1)
                tmp = sq_tmp
                with dve.Fori(0, 7) as i:
                    chain.loop(i, 4)
                    for s in range(2):
                        dve.wait_ge(FREE[s], i + (8 + 2))
                        e = ext[:, s, :]
                        samp = e[:, 1 + SEQ:1 + SEQ + 72].rearrange("p (j n) -> p j n", j=8)
                        k = 2 * i + s
                        sin = shin[:, bass.ds(k, 1), :].rearrange("p a n -> p (a n)")
                        so = shout[:, bass.ds(k, 1), :].rearrange("p a n -> p (a n)")
                        mu = vec[:, bass.ds(k + VEC["mu"], 1)]
                        z = zr[:, bass.ds(k, 1), :].rearrange("p a n -> p (a n)")
                        chain(V.tensor_copy(samp[:, :, 0], sin))
                        d1 = tmp[:, s, :]
                        tt(V, d1[:, 0:SEQ], e[:, 0:SEQ], e[:, 1:SEQ + 1], ALU.subtract)
                        chain(tt(V, d1[:, SEQ:T].rearrange("p (j n) -> p j n", j=8), samp[:, :, 0:8],
                                 samp[:, :, 1:9], ALU.subtract))
                        stt(z[:, 0:SEQ], d1[:, 0:SEQ], mu, e[:, 1:SEQ + 1], ALU.mult, ALU.add)
                        stt(z[:, SEQ:T].rearrange("p (j n) -> p j n", j=8),
                            d1[:, SEQ:T].rearrange("p (j n) -> p j n", j=8), mu, samp[:, :, 1:9], ALU.mult,
                            ALU.add).then_inc(S("shifted"), 1)
                        V.tensor_copy(so[:, 0:1], e[:, SEQ:SEQ + 1])
                        V.tensor_copy(so[:, 1:9], samp[:, :, 8]).then_inc(S(f"ext_free{s}"), 1)
                    chain.end_loop(7)

            def mlstm():
                for h in range(MH):
                    dve.wait_ge(S("ml_bcast"), h + 1)
                    tt(V, halves(qh[:, h, :]), halves(zm[:, h, :]), pair(h % 2), ALU.mult).then_inc(S("ml_qh"), 1)
                dve.wait_ge(S("ml_qh"), 4)
                dve.wait_ge(S("ml_small"), 1)
                V.tensor_copy(decb.rearrange("p a b -> p (a b)"), bank(4)[:, 0:48])
                V.tensor_copy(wlc[:, 0:NCH, :].rearrange("p a b -> p (a b)"), bank(4)[:, 48:48 + 4 * NCH])
                V.tensor_copy(wlc[0:64, NCH, :], bank(4)[0:64, 48 + 4 * NCH:52 + 4 * NCH])
                V.memset(vaug[:, :, 128:129], 1.0)
                chain(V.memset(Cst, 0.0))
                for c in range(NCH + 1):
                    n, c0 = (L, L * c) if c < NCH else (NSAMP, SEQ)
                    dm, at_ = (x[0:n, :, :].rearrange("p a b -> p (a b)")[:, 0:4 * n].rearrange(
                        "p (h n) -> p h n", h=4) for x in (Dm, att))
                    if c == NCH:
                        at_ = att[0:n, :, 0:n]
                    neg = c_("mneg", 128) if c < NCH else c_("mneg_s", 64, 64)
                    dve.wait_ge(S("ml_scores"), c + 1)
                    tt(V, dm, bank(1)[0:n, 0:4 * n].rearrange("p (h n) -> p h n", h=4), bc(neg, 1, 4),
                       ALU.add).then_inc(S("ml_dm"), 1)
                    q = qh[:, :, c0:c0 + n]
                    if c < NCH:
                        tt(V, qn, q, bc(Cst[:, :, 128], 2, L), ALU.mult).then_inc(S("ml_qn"), 1)
                    else:
                        dve.wait_ge(S("C_in"), 16)
                        tt(V, qn[:, :, 0:n].rearrange("p h (j n) -> p h j n", j=8),
                           q.rearrange("p h (j n) -> p h j n", j=8), bc(Cs[:, :, :, 128], 3, 8),
                           ALU.mult).then_inc(S("ml_qn"), 1)
                    dve.wait_ge(S("ml_w"), c + 1)
                    tt(V, at_, bank(0)[0:n, 0:4 * n].rearrange("p (h n) -> p h n", h=4), dm,
                       ALU.mult).then_inc(S("ml_att"), 1)
                    dve.wait_ge(S("ml_tok"), c + 1)
                    vt = V.tensor_copy(vaug[0:n, :, 0:128], bank(2)[0:n, :].rearrange("p (h n) -> p h n", h=4))
                    kp = bank(3)[0:n, :].rearrange("p (h n) -> p h n", h=4)
                    if c < NCH:
                        tt(V, ktok, kp, bc(wlc[:, c, :], 2, 128), ALU.mult).then_inc(S("ml_tokc"), 1)
                        dve.wait_ge(S("ml_upd"), c + 1)
                        for h in range(MH):
                            last = stt(Cst[:, h, :], Cst[:, h, :], decb[:, h, c:c + 1],
                                       bank(6 + h // 2)[:, 129 * (h % 2):129 * (h % 2) + 129], ALU.mult, ALU.add)
                        last.then_inc(S("ml_state"), 1)
                        dve.wait_ge(S("ml_state"), c + 1)
                    else:
                        vt.then_inc(S("ml_tokc"), 1)
                        chain(tt(V, wlm[0:64], bc(wlc[0:64, c, :], 2, 8), bc(seqmask[0:64, :], 1, 4), ALU.mult))
                        for h in range(MH):
                            last = tt(V, Km[:, h], bc(kp[:, h, :], 1, 8), bc(wlm[0:64, h, :], 2, 128), ALU.mult)
                        last.then_inc(S("ml_km"), 1)
                        dve.wait_ge(S("ml_nd"), NCH + 1)
                        chain(tt(V, Cs, Cs, bc(decb[:, :, NCH:NCH + 8], 3, 129), ALU.mult))
                        for g in range(11):
                            e0, e1 = 3 * g, min(3 * g + 3, 32)
                            dve.wait_ge(S("ml_supd"), g + 1)
                            tt(V, Csf[:, e0:e1, :], Csf[:, e0:e1, :], bank(6 + g % 2)[:, 0:129 * (e1 - e0)].rearrange(
                                "p (a b) -> p a b", b=129), ALU.add).then_inc(S("ml_sst"), 1)
                for h in range(MH):
                    dve.wait_ge(S("ml_abs"), h + 1)
                    dve.wait_ge(S("ml_emt"), h + 1)
                    den = zm[:, 8 + h, :]
                    chain(tt(V, halves(den), halves(den), pair(h), ALU.max))
                    chain(V.reciprocal(den, den))
                    tt(V, zm[:, 4 + h, :], zm[:, 4 + h, :], den, ALU.mult).then_inc(S("hn_src"), 1)
                dve.wait_ge(S("hn_src"), 4)
                head_norm("mn", zm[:, 4:8, :], zm[:, 8:12, :], MHD)
                dve.wait_ge(S("sC_written"), 16)
                for h in range(MH):
                    stt(hT[:, h, :], zm[:, 4 + h, :], v_("ln_m_g", h), zm[:, 12 + h, :], ALU.mult,
                        ALU.mult).then_inc(S("ycat"), 1)

            def rwkv_prep():
                chain(V.tensor_scalar(omka, vec[:, VEC["k_a"]:VEC["k_a"] + 4], -1.0, 1.0, ALU.mult, ALU.add))
                dve.wait_ge(S("ycat"), 4)
                for p in range(RP):
                    V.tensor_scalar(AR[:, p, 0, :], zr[:, 4 + p, :], v_("k_k", p), None,
                                    ALU.mult).then_inc(S("rw_kk"), 1)
                for p in range(RP):
                    dve.wait_ge(S("rw_kkn"), p + 1)
                    V.tensor_scalar(halves(AR[:, p, 1, :]), pair(p), 1e-24, None, ALU.max).then_inc(S("rw_kkmax"), 1)
                for p in range(RP):
                    dve.wait_ge(S("rw_kksqrt"), p + 1)
                    chain(V.reciprocal(AR[:, p, 1, :], AR[:, p, 1, :]))
                    chain(tt(V, AR[:, p, 0, :], AR[:, p, 0, :], AR[:, p, 1, :], ALU.mult))
                for p in range(RP):
                    ld, a, cum, ex, em = (prep[:, k, p % 2, :] for k in range(5))
                    dve.wait_ge(S("rw_sig"), 2 * p + 2)
                    chain(V.tensor_scalar(ld, ld, -float(np.exp(-0.5)), None, ALU.mult))
                    chain(V.tensor_tensor_scan(cum, c_("scan64", T), ld, 0.0, ALU.mult, ALU.add))
                    tt(V, ex, cum, ld, ALU.subtract).then_inc(S("rw_cum"), 1)
                    kk, r, kr = AR[:, p, 0, :], zr[:, p, :], zr[:, 4 + p, :]
                    chain(tt(V, BK[:, p, 0, :], kk, a, ALU.mult))
                    chain(V.tensor_scalar(a, a, v_("k_a", p), omka[:, p:p + 1], ALU.mult, ALU.add))
                    chain(tt(V, a, a, kr, ALU.mult))
                    chain(stt(rkp[:, p, :], r, v_("r_k", p), a, ALU.mult, ALU.mult))
                    dve.wait_ge(S("rw_exp"), p + 1)
                    chain(tt(V, BK[:, p, 0, :], BK[:, p, 0, :], em, ALU.mult))
                    chain(tt(V, BK[:, p, 1, :], a, em, ALU.mult))
                    chain(tt(V, AR[:, p, 1, :], r, cum, ALU.mult))
                    chain(V.tensor_copy(PL[:, p, 0:8], cum[:, 0:SEQ].rearrange("p (c n) -> p c n", n=LR)[:, :, LR - 1]))
                    chain(V.tensor_copy(PL[:, p, 8:16], cum[:, SEQ:T].rearrange("p (c n) -> p c n", n=8)[:, :, 7]))
                    stt(kk, kk, -1.0, ex, ALU.mult, ALU.mult).then_inc(S("rw_prep"), 1)

            def rwkv():
                V.memset(Sr, 0.0).then_inc(S("rk_st"), 1)

                def gate(c):
                    if c >= 2:
                        dve.wait_ge(S("rk_y"), c - 1)
                    m = c_("rk" if c < NCR else "rk_s", 320)
                    for p in range(RP):
                        dve.wait_ge(S("rk_sc"), 4 * c + p + 1)
                        tt(V, Gs[:, c % 2, p, :], bank(p % 2)[:, 0:320], m, ALU.mult).then_inc(S("rk_g"), 1)
                    dve.wait_ge(S("rk_g"), 4 * c + 4)

                def level(c, k):
                    top = 5 if c < NCR else 2
                    for q in range(2):
                        b = PP[1][:, q, 0:384].rearrange("p (a k n) -> p a k n", a=2, k=3)
                        new = XPA[:, q, (k + 1) % 2]
                        dve.wait_ge(S(f"rk_lv{q}"), 6 * c + k + 1)
                        if k == 0:
                            tt(V, new[:, :, 1, :], Gs[:, c % 2, 2 * q:2 * q + 2, 0:64],
                               bc(c_("idpair", 64), 1, 2), ALU.add)
                        else:
                            dst = new[:, :, 1, :] if k < top else PF[:, c % 2, 2 * q:2 * q + 2, :]
                            last = tt(V, dst, XPA[:, q, k % 2, :, 1, :], b[:, :, 1, :], ALU.add)
                        if k < top:
                            last = V.tensor_copy(new[:, :, 0:3:2, :], b[:, :, 0:3:2, :])
                        last.then_inc(S(f"rk_lc{q}"), 1)
                        dve.wait_ge(S(f"rk_lc{q}"), 6 * c + k + 1)

                def state(c):
                    dve.wait_ge(S("rk_s"), c + 1)
                    chain(tt(V, Sr, Sr, bank(7)[:, 0:256].rearrange("p (a b) -> p a b", a=4), ALU.add))
                    tt(V, Sr, Sr, bc(PL[:, :, c], 2, 64), ALU.mult).then_inc(S("rk_st"), 1)
                    dve.wait_ge(S("rk_st"), c + 2)

                for c in range(NCR + 1):
                    gate(c)
                    for k in range(3):
                        level(c, k)
                    if c:
                        state(c - 1)
                    if c < NCR:
                        for k in (3, 4, 5):
                            level(c, k)
                dve.wait_ge(S("rk_uc"), NCR + 1)
                for p in range(RP):
                    tt(V, UVm[:, 0, p], bc(U[:, p, :], 1, 8), bc(seqmask, 2, 64), ALU.mult)
                    last = tt(V, UVm[:, 1, p], bc(tok[:, NCR % 2, p, 2, :], 1, 8), bc(seqmask, 2, 64), ALU.mult)
                last.then_inc(S("rs_uvm"), 1)
                for p in range(RP):
                    dve.wait_ge(S("rs_s"), p + 1)
                    tt(V, SS[:, p], SS[:, p], bank(p % 2).rearrange("p (j n) -> p j n", j=8),
                       ALU.add).then_inc(S("rs_sc"), 1)
                dve.wait_ge(S("rs_sc"), 4)
                tt(V, SS, SS, bc(PL[:, :, 8:16], 3, 64), ALU.mult).then_inc(S("rs_st"), 1)
                dve.wait_ge(S("rk_yc"), NCR + 1)
                dve.sem_inc(S("hn_src"), 4)
                head_norm("rn", yr, AR[:, :, 0, :], RHD)
                for p in range(RP):
                    chain(V.tensor_scalar(yr[:, p, :], yr[:, p, :], v_("ln_r_g", p), v_("ln_r_b", p), ALU.mult,
                                          ALU.add))
                    dve.wait_ge(S("rw_bonus"), p + 1)
                    tt(V, halves(AR[:, p, 0, :]), pair(p), halves(zr[:, 8 + p, :]), ALU.mult).then_inc(
                        S("rw_bonusc"), 1)
                    dve.wait_ge(S("rw_bonusc"), p + 1)
                    chain(tt(V, yr[:, p, :], yr[:, p, :], AR[:, p, 0, :], ALU.add))
                for p in range(RP):
                    dve.wait_ge(S("rw_gate"), p + 1)
                    tt(V, halves(hT[:, 4 + p, :]), halves(yr[:, p, :]), pair(p), ALU.mult).then_inc(S("ycat"), 1)

            sq_tmp = sq
            for s in range(2):
                dve.sem_inc(FREE[s], 1)
            dve.wait_ge(S("vec_in"), 16)
            dve.wait_ge(S("consts_in"), 16)
            dve.wait_ge(S("x_in"), 16 * KT)
            norm(0, "norm_mix", 0)
            mlstm_rows()
            token_shift()
            mlstm()
            rwkv_prep()
            rwkv()
            residual("e_out")
            norm(1, "norm_ffn", 0)
            ffn(0)
            residual("down0")
            if do_odd:
                odd_dve(dve, V, chain, norm, residual, head_norm)
                norm(3, "norm_ffn", 8)
                ffn(1)
                residual("down1")
                norm(4, "norm_final", 0)


def _tiles(w):
    k, n = w.shape
    return w.reshape(k // P, P, n // P, P).transpose(2, 1, 0, 3).reshape(n // P, P, k)


def _cols(v):
    return v.reshape(-1, P).T


def _pairs(w):
    return w.reshape(w.shape[0], 2, FT, P).transpose(0, 2, 1, 3).reshape(w.shape[0], -1)


def host_arrays(x_prompt, x_sample, state_mlstm_C, state_mlstm_n, state_mlstm_m, state_rwkv_S, state_rwkv_shift,
                state_gla_S, state_s5_re, state_s5_im, state_ffn_conv, norm_mix, norm_ffn, norm_final,
                e_w_in, e_b_if, e_mu, e_w0, e_w_up, e_a0, e_a_up, e_g_up, e_k_k, e_k_a, e_r_k,
                e_ln_m_g, e_ln_r_g, e_ln_r_b, e_w_out, o_w_in, o_a_up, o_a_b, o_ln_g, o_lam_re, o_lam_im,
                o_log_step, o_b_re, o_b_im, o_c_re, o_c_im, o_d, o_w_glu, o_w_out,
                f_w_up, f_conv_w, f_conv_b, f_w_down):
    d = {}
    x = np.concatenate([x_prompt.reshape(SEQ, D_MODEL), x_sample.reshape(NSAMP, D_MODEL)])
    d["x"] = x.T.reshape(KT, P, T).transpose(1, 0, 2)
    d["consts"] = shape_constants()
    w = e_w_in[0]
    m4 = 4 * HALF
    wo = o_w_in[0]
    w_list = [np.concatenate([w[:, :m4], w[:, m4 + 8:]], 1), e_w_out[0], _pairs(f_w_up[0]),
              np.concatenate([wo[:, :1536], wo[:, 1552:]], 1), o_w_out[0], _pairs(f_w_up[1])]
    d["w"] = np.concatenate([_tiles(a) for a in w_list])
    wif = np.zeros((D_MODEL, 36), np.float32)
    wif[:, 0:4], wif[:, 32:36] = w[:, m4:m4 + 4], w[:, m4 + 4:m4 + 8]
    d["w_if"] = wif.reshape(KT, P, 36).transpose(1, 0, 2)
    d["w_down"] = np.concatenate([_tiles(a) for a in f_w_down])
    vec = np.zeros((P, NVEC), np.float32)

    def put(name, v):
        v = _cols(v)
        vec[:, VEC[name]:VEC[name] + v.shape[1]] = v

    for name, v in (("norm_mix", norm_mix.reshape(-1)), ("norm_ffn", norm_ffn.reshape(-1)), ("norm_final", norm_final),
                    ("mu", e_mu[0]), ("w0", e_w0[0]), ("a0", e_a0[0]), ("k_k", e_k_k[0]), ("k_a", e_k_a[0]),
                    ("r_k", e_r_k[0]), ("ln_m_g", e_ln_m_g[0]), ("ln_r_g", e_ln_r_g[0]), ("ln_r_b", e_ln_r_b[0]),
                    ("a_b", o_a_b[0]), ("o_ln_g", o_ln_g[0]), ("o_d", o_d[0])):
        put(name, v)
    vec[0:4, VEC["b_if"]], vec[32:36, VEC["b_if"]] = e_b_if[0, 0:4], e_b_if[0, 4:8]
    vec[0:64, VEC["sgn"]], vec[64:128, VEC["sgn"]] = -1.0, 1.0
    d["vec"] = vec
    cp = np.concatenate([_pairs(f_conv_w[k]).reshape(3, 2 * FT, P) for k in range(2)]).reshape(2, 3, 2 * FT, P)
    cb = _pairs(f_conv_b).reshape(2, 1, 2 * FT, P)
    d["convp"] = np.concatenate([cp, cb], 1).transpose(3, 0, 2, 1).reshape(P, 2, CONVC)
    cs = np.stack([_pairs(state_ffn_conv[k].reshape(16, -1)) for k in range(2)])
    d["conv_state"] = cs.reshape(2, 16, 2 * FT, P).transpose(0, 3, 2, 1)
    d["shift"] = state_rwkv_shift[0].reshape(8, 14, P).transpose(2, 1, 0)
    d["lora"] = np.stack([np.concatenate([e_w_up[0], e_a_up[0]]), e_g_up[0]], 1)
    d["m0"] = state_mlstm_m[0].T
    C = state_mlstm_C[0].transpose(3, 1, 0, 2)
    n = state_mlstm_n[0].transpose(2, 1, 0)[..., None]
    d["C"] = np.concatenate([C, n], 3).reshape(P, 32, 129)
    d["rS"] = state_rwkv_S[0].reshape(8, 4, 2, 64, 64).transpose(2, 4, 1, 0, 3).reshape(P, 4, 8, 64)
    d["w_ad"] = wo[:, 1536:1552].reshape(KT, P, GRANK).transpose(1, 0, 2)
    d["a_up"] = o_a_up[0]
    d["gS"] = state_gla_S[0].reshape(8, 2, 2, GDK, GDV).transpose(2, 3, 1, 0, 4).reshape(P, 2, 8, GDV)
    lam = [np.concatenate([a.T, a.T]) for a in (o_lam_re[0], o_lam_im[0])]
    d["s5_lam"] = np.stack(lam + [np.broadcast_to(o_log_step[0], (P, SG))], 1)
    b = [a[0].transpose(1, 0, 2) for a in (o_b_re, o_b_im)]
    c = [a[0].transpose(2, 0, 1) for a in (o_c_re, o_c_im)]
    d["s5_bc"] = np.stack([np.concatenate(x) for x in (b, b[::-1], c, c[::-1])], 1)
    x0 = [a[0].transpose(2, 1, 0) for a in (state_s5_re, state_s5_im)]
    d["s5_x0"] = np.stack([np.concatenate(x0), np.concatenate(x0[::-1])], 1)
    d["w_glu"] = o_w_glu[0].reshape(4, P, HALF).transpose(1, 0, 2)
    return {k: np.ascontiguousarray(v, dtype=np.float32) for k, v in d.items()}


OUT = {"shift": (P, 14, NSEQ), "m": (4, NSEQ), "pC": (P, 4, 129), "sC": (P, 32, 129), "pS": (P, 4, 64),
       "sS": (P, 4, 8, 64), "conv0": (P, 2 * FT, 18), "y": (P, KT, T),
       "pG": (P, 2, GDV), "sG": (P, 2, 8, GDV), "s5": (P, SG, NSEQ), "conv1": (P, 2 * FT, 18)}


def _tokens(y):
    y = y.transpose(1, 0, 2).reshape(D_MODEL, T).T
    return y[:SEQ].reshape(1, SEQ, D_MODEL), y[SEQ:].reshape(DEC_BATCH, DEC_SEQ, D_MODEL)


def _even_states(r):
    pC, sC = r["pC"], r["sC"].reshape(P, 4, 8, 129)
    sh = r["shift"].transpose(2, 1, 0).reshape(NSEQ, -1)
    m = r["m"].T
    pS = r["pS"].reshape(2, 64, 4, 64).transpose(2, 0, 3, 1).reshape(1, 1, 8, 64, 64)
    sS = r["sS"].reshape(2, 64, 4, 8, 64).transpose(3, 2, 0, 4, 1).reshape(1, 8, 8, 64, 64)
    p = (pC[:, :, :128].transpose(1, 2, 0)[None, None], pC[:, :, 128].T[None, None], m[0][None, None], pS,
         sh[0][None, None])
    s = (sC[:, :, :, :128].transpose(2, 1, 3, 0)[None], sC[:, :, :, 128].transpose(2, 1, 0)[None], m[1:][None], sS,
         sh[1:][None])
    return p, s


def _conv(c):
    return c.reshape(P, FT, 2, NSEQ, 2).transpose(3, 4, 2, 1, 0).reshape(NSEQ, 2, 2 * D_FF)


def kernel(**inputs):
    import concourse.bacc as bacc
    from concourse.bass_utils import run_bass_kernel_spmd as run

    ins = host_arrays(**{k: np.asarray(v) for k, v in inputs.items()})
    nc = bacc.Bacc("TRN2", target_bir_lowering=False, num_devices=1)
    d = {k: nc.dram_tensor(f"in_{k}", v.shape, F32, kind="ExternalInput").ap() for k, v in ins.items()}
    o = {k: nc.dram_tensor(f"out_{k}", v, F32, kind="ExternalOutput").ap() for k, v in OUT.items()}
    program(nc, d, o, 2)
    r = run(nc, [{f"in_{k}": v for k, v in ins.items()}], core_ids=[0]).results[0]
    r = {k: r[f"out_{k}"] for k in OUT}
    p, s = _even_states(r)
    pG = r["pG"].reshape(2, GDK, 2, GDV).transpose(2, 0, 1, 3).reshape(1, 1, GH, GDK, GDV)
    sG = r["sG"].reshape(2, GDK, 2, 8, GDV).transpose(3, 2, 0, 1, 4).reshape(1, 8, GH, GDK, GDV)
    x5 = r["s5"].transpose(2, 1, 0)
    re, im = x5[None, :, :, :SP], x5[None, :, :, SP:]
    conv = np.stack([_conv(r["conv0"]), _conv(r["conv1"])])
    out = (*_tokens(r["y"]), *p, pG, re[:, :1], im[:, :1], conv[:, :1], *s, sG, re[:, 1:], im[:, 1:], conv[:, 1:])
    return tuple(np.ascontiguousarray(a) for a in out)
```

```python
from contextlib import ExitStack

import numpy as np

import concourse.bass as bass
from concourse import mybir
from concourse.alu_op_type import AluOpType as ALU

F32 = mybir.dt.float32
ACT = mybir.ActivationFunctionType
AX = mybir.AxisListType

P = 128
D_MODEL, SEQ, DEC_BATCH, DEC_SEQ = 1024, 512, 8, 8
HALF = D_MODEL // 2
NSAMP = DEC_BATCH * DEC_SEQ
T = SEQ + NSAMP
TH = T // 2
KT = D_MODEL // P
D_FF = ((8 * D_MODEL // 3 + 255) // 256) * 256
FT = D_FF // P
NSEQ = 1 + DEC_BATCH
MH, MHD = 4, 128
RP, RHD = 4, 64
GH, GDK, GDV = 4, 64, 128
L = 128
LR = 64
NCH = SEQ // L
NCR = SEQ // LR
SG, SC, SP = 32, 16, 64
BL = 8
NB = T // BL
NBP = SEQ // BL
GRANK, GLA_TAU = 16, 16.0
EPS = 1e-6
RWKV_EPS = 64e-5
M_INIT = -1e30
NEG = -1e30
TWO_PI = 6.283185307179586
HN = {"mn": 0, "rn": 4, "gn": 8}
ROUND = 12582912.0

E_TILES = 30
O_TILES = 16
ADDS = ("e_out", "down0", "o_out", "down1")
RUNS = {"e_in": (0, E_TILES), "e_out": (30, 8), "ffn0": (38, 2 * FT),
        "o_in": (38 + 2 * FT, O_TILES), "o_out": (54 + 2 * FT, 8), "ffn1": (62 + 2 * FT, 2 * FT)}
W_TILES = 62 + 4 * FT
DCH = ((0, 8), (8, 7), (15, 7))
CHUNK0 = {}
_u = 0
for _name, _n in (("e_in", E_TILES), ("e_out", 8), ("ffn0", 2 * FT), ("down0", 24),
                  ("o_in", O_TILES), ("o_out", 8), ("ffn1", 2 * FT), ("down1", 24)):
    CHUNK0[_name] = _u
    _u += _n
SPLIT = {"e_in": 0, "e_out": 1, "ffn0": 2, "o_in": 3, "o_out": 4, "ffn1": 5}
NEXT = {"e_in": "e_out", "e_out": "ffn0", "ffn0": "down0", "down0": "o_in", "o_in": "o_out", "o_out": "ffn1",
        "ffn1": "down1", "down1": None}
AHEAD = FT - KT
USE = {}
_u = 0
for _name, _n in (("e_in", E_TILES), ("e_out", 8), ("ffn0", 2 * FT), ("down0", 8),
                  ("o_in", O_TILES), ("o_out", 8), ("ffn1", 2 * FT), ("down1", 8)):
    USE[_name] = _u
    _u += _n

VEC = {}
_c = 0
for _name, _n in (("norm_mix", 16), ("norm_ffn", 16), ("norm_final", 8), ("mu", 14), ("w0", 4), ("a0", 4),
                  ("k_k", 4), ("k_a", 4), ("r_k", 4), ("ln_m_g", 4), ("ln_r_g", 4), ("ln_r_b", 4),
                  ("a_b", 2), ("o_ln_g", 4), ("o_d", 4), ("sgn", 1), ("b_if", 1)):
    VEC[_name] = _c
    _c += _n
NVEC = _c
CONVC = 4 * 2 * FT

CONST = {}
_c = 0
GLEV = 8
for _name, _n in (("ident", 128), ("ones", 128), ("headones", 128), ("scan128", T), ("scan64", T),
                  ("mneg", 128), ("mneg_s", 64), ("gla", GLEV * 128), ("gla_s", 4 * 64),
                  ("rk", 5 * 64), ("rk_s", 5 * 64), ("seq", 8), ("idpair", 64), ("sel", 4 * 128)):
    CONST[_name] = _c
    _c += _n
NCONST = _c


def shape_constants():
    c = np.zeros((P, NCONST), np.float32)

    def put(name, a):
        c[:a.shape[0], CONST[name]:CONST[name] + a.shape[1]] = a

    i = np.arange(P)
    put("ident", np.eye(P))
    put("ones", np.ones((P, P)))
    put("headones", (i[:, None] // 64 == i[None] // 64) * 1.0)
    t = np.arange(T)
    for name, n in (("scan128", L), ("scan64", LR)):
        start = np.where(t < SEQ, t % n == 0, (t - SEQ) % DEC_SEQ == 0)
        put(name, np.broadcast_to(1.0 - start, (P, T)))
    s, tt = i[:, None], i[None]
    put("mneg", np.where(s <= tt, 0.0, NEG))
    s8, t8 = s[:64], tt[:, :64]
    same = s8 // 8 == t8 // 8
    put("mneg_s", np.where(same & (s8 <= t8), 0.0, NEG))
    lev = [((s // (2 * h) == tt // (2 * h)) & (s % (2 * h) < h) & (tt % (2 * h) >= h)) * 1.0
           for h in (64, 32, 16, 8, 4, 2, 1)] + [np.eye(P)]
    put("gla", np.concatenate(lev, 1))
    put("gla_s", np.concatenate([m[:64, :64] for m in lev[4:]], 1))
    s2 = (i % 64)[:, None]
    t2 = np.arange(64)[None]
    for name, ok in (("rk", np.ones((P, 64), bool)), ("rk_s", s2 // 8 == t2 // 8)):
        up, upi, low = (s2 < t2) & ok, (s2 <= t2) & ok, (s2 > t2) & ok
        put(name, np.concatenate([up, upi, up, upi, low], 1) * 1.0)
    put("idpair", (s2 == t2) * 1.0)
    put("seq", (s2 // 8 == np.arange(8)[None]) * 1.0)
    sel = np.zeros((4, 4, 128))
    sel[np.arange(4), np.arange(4)] = 1.0
    put("sel", sel.reshape(4, 512))
    return c


class Chain:

    def __init__(self, eng, sem):
        self.eng, self.sem, self.n, self.i, self.per = eng, sem, 0, None, 0

    def __call__(self, ins):
        ins.then_inc(self.sem, 1)
        self.n += 1
        if self.i is None:
            self.eng.wait_ge(self.sem, self.n)
        else:
            self.eng.wait_ge(self.sem, self.i * self.per + self.n)

    def loop(self, i, per, first=0):
        self.i, self.per, self.start = i, per, self.n
        self.n -= per * first
        self.first = first

    def end_loop(self, times):
        assert self.n + self.per * self.first - self.start == self.per, (self.n - self.start, self.per)
        self.n = self.start + self.per * times
        self.i = None


def program(nc, d, o, stages):
    ctx = ExitStack()
    with ctx:
        def sb(name, *shape):
            return ctx.enter_context(nc.sbuf_tensor(name, list(shape), F32))

        def both(name, *shape):
            with nc.sbuf_tensor(name + "_r", list(shape), mybir.dt.float32r) as rounded:
                pass
            return sb(name, *shape), rounded

        def sem(name):
            return ctx.enter_context(nc.semaphore(name))

        class Sems:

            def __init__(self):
                self.made = {}

            def __call__(self, name):
                if name not in self.made:
                    self.made[name] = sem(name)
                return self.made[name]

        S = Sems()

        xT = sb("xT", P, KT, T)
        hT, hT_r = both("hT", P, KT, T)
        w_ring = sb("w_ring", P, 2, KT * P)
        dual, dual_r = both("dual", P, 5632)
        cst = sb("cst", P, NCONST)
        vec = sb("vec", P, NVEC)
        convp = sb("convp", P, 2, CONVC)
        ext = sb("ext", P, 2, 2 + SEQ + 10 * DEC_BATCH)
        rstd = sb("rstd", P, T)
        sq = sb("sq", P, 2, T)
        NA = 28600
        R0, R1_ = (0, 12672), (15896, 12672)
        with nc.sbuf_tensor("arena_r0", [P, R0[1]], mybir.dt.float32r) as arena_r0:
            with nc.sbuf_tensor("gap", [P, R1_[0] - R0[1]], F32):
                with nc.sbuf_tensor("arena_r1", [P, R1_[1]], mybir.dt.float32r) as arena_r1:
                    pass
        arena = sb("arena", P, NA)
        PP = [ctx.enter_context(nc.psum_tensor(f"PP{i}", [P, 2, 512], F32)) for i in range(4)]

        def bank(b, n=512):
            return PP[b // 2][:, b % 2, 0:n]

        def pair(i):
            return PP[i][:, :, 0:TH]

        def at(off, *shape, mem=None):
            n = int(np.prod(shape))
            assert off + n <= NA, (off, n)
            v = (arena if mem is None else mem)[:, off:off + n]
            if len(shape) == 1:
                return v
            names = [f"a{i}" for i in range(len(shape))]
            return v.rearrange(f"p ({' '.join(names)}) -> p {' '.join(names)}", **dict(zip(names[1:], shape[1:])))

        def halves(v):
            return v.rearrange("p (a n) -> p a n", a=2)

        def c_(name, n, rows=P, r0=0):
            return cst[r0:r0 + rows, CONST[name]:CONST[name] + n]

        def v_(name, k=0, rows=P, r0=0):
            return vec[r0:r0 + rows, VEC[name] + k:VEC[name] + k + 1]

        ident, ones, headones = c_("ident", 128), c_("ones", 128), c_("headones", 128)
        sel = c_("sel", 512, 4).rearrange("p (h n) -> p h n", h=4)
        seqmask = c_("seq", 8)

        def tt(eng, out, a, b, op):
            return eng.tensor_tensor(out, a, b, op)

        def stt(out, a, s, b, op0, op1):
            return nc.vector.scalar_tensor_tensor(out=out, in0=a, scalar=s, in1=b, op0=op0, op1=op1)

        def bc(v, axis, n):
            v = v.unsqueeze(axis)
            shape = list(v.shape)
            shape[axis] = n
            return v.to_broadcast(shape)

        def mm(out, lhsT, rhs, start=True, stop=True):
            return nc.tensor.matmul(out, lhsT, rhs, start=start, stop=stop)

        def mm3(out, w, w_low, x, x_low, start, stop):
            mm(out, w, x, start, False)
            mm(out, w, x_low, False, False)
            return mm(out, w_low, x, False, stop)

        zm = at(0, 16, T)
        zr = at(9216, 14, T)
        W0 = 9216 + 14 * T
        lora = at(W0, 2, 512)
        wif = at(W0 + 1024, KT, 36)
        shin = at(W0 + 1312, 14, DEC_BATCH)
        shout = at(W0 + 1424, 14, NSEQ)
        W1 = W0 + 1552
        rows = at(W1, 8, T)
        r_f, r_i, r_B, r_m, r_a, r_s, r_w, r_e = (rows[0:4, k, :] for k in range(8))
        W2 = W1 + 8 * T
        qh = at(W2, 4, T)
        W3 = W2 + 4 * T
        sqf = sq[:, :, :].rearrange("p a b -> p (a b)")
        qn = sqf[:, 0:512].rearrange("p (h n) -> p h n", h=4)
        att = sqf[:, 512:1024].rearrange("p (h n) -> p h n", h=4)
        Dm = at(W3, 4, L)
        vaug = at(W3 + 512, 4, 129)
        ktok = at(W3 + 1028, 4, L)
        PL = at(W3 + 1540, 4, 16)
        omka = at(W3 + 1604, 4)
        W4 = W3 + 1612
        Cst = at(W4 + 160, 4, 129)
        wlc = at(W4, 5, 4)
        decb = at(W4 + 20, 4, 12)
        rsm = at(W4 + 68, 5, 12)
        wlm = at(W4 + 128, 4, 8)
        r_mp, r_rl, r_dec, r_m0, r_mo = (rsm[0:4, k, :] for k in range(5))
        Cs = hT[:, :, :].rearrange("p a b -> p (a b)")[:, 0:4128].rearrange("p (h j n) -> p h j n", h=4, j=8)
        Csf = hT[:, :, :].rearrange("p a b -> p (a b)")[:, 0:4128].rearrange("p (g n) -> p g n", n=129)
        dring = dual[:, :]

        class Rounded:

            def __init__(self, f, r):
                self.f, self.r = f, r

        def on(where, off, *shape):
            n = int(np.prod(shape))
            if where == DUAL:
                return Rounded(at(off, *shape, mem=dual), at(off, *shape, mem=dual_r))
            r, base = (arena_r0, 0) if off < R1_[0] else (arena_r1, R1_[0])
            assert off - base + n <= R1_[1]
            return Rounded(at(off, *shape), at(off - base, *shape, mem=r))

        DUAL, ARENA = 0, 1
        w_hi, w_lo = (on(DUAL, o, 2, KT * P) for o in (0, 2 * KT * P))
        wif_hi = on(DUAL, 5248, KT, 36)
        wif_lo = on(ARENA, W2 + 6 * T, KT, 36)
        wad_hi, wad_lo = (on(DUAL, 5248 + KT * GRANK * k, KT, GRANK) for k in range(2))
        H_HI = {"e_in": [on(ARENA, W2 + T * k, T) for k in range(6)] + [on(DUAL, 4096 + T * k, T)
                                                                      for k in range(2)]}
        for name_, off in (("e_out", 4608), ("ffn0", 15896), ("o_in", 22848), ("o_out", 4608), ("ffn1", 15896)):
            H_HI[name_] = [on(ARENA, off + T * k, T) for k in range(KT)]
        Km = dring[0:64, 0:4096].rearrange("p (h j n) -> p h j n", h=4, j=8)

        AR = at(0, 4, 2, T)
        BK = at(4608, 4, 2, T)
        rkp = at(W1, 4, T)
        yr = at(W1 + 2304, 4, T)
        X0 = W1 + 4608
        prep = at(W1 + 2304, 5, 2, T)
        XPA = at(X0, 2, 2, 2, 3, 64)
        PF = at(X0 + 1536, 2, 4, 64)
        tok = at(X0 + 2048, 2, 4, 3, 64)
        R1 = sqf[:, 0:256].rearrange("p (a b) -> p a b", a=4)
        U = sqf[:, 256:512].rearrange("p (a b) -> p a b", a=4)
        Sr = at(W4 + 932, 4, 64)
        QT = at(W4 + 676, 4, 64)
        Gs = at(9216, 2, 4, 320)
        SS = at(9216 + 2560, 4, 8, 64)
        UVm = dring[:, 0:4096].rearrange("p (a q j n) -> p a q j n", a=2, q=4, j=8)

        actv = at(0, FT, T)
        cv = at(12672, 3, T)
        convin = at(14400, 2 * FT, 16)
        convout = at(15104, 2 * FT, 18)
        act_lo = on(ARENA, 0, FT, T)
        act_hi = on(ARENA, 15896, FT, T)

        block = ctx.enter_context(nc.Block())
        do_odd = stages > 1

        WL = [S("w_landed0"), S("w_landed1")]
        FREE = [S("psum_free0"), S("psum_free1")]
        runs = ["e_in", "e_out", "ffn0"] + (["o_in", "o_out", "ffn1"] if do_odd else [])
        last_tile = RUNS[runs[-1]][0] + RUNS[runs[-1]][1]

        def all_free(eng, name, n):
            for s in range(2):
                eng.wait_ge(FREE[s], (USE[name] + n) // 2 + 1)

        zo = at(0, 16, T)
        adown = at(9216, T)[0:GRANK]
        aup = at(9792, 256)[0:GRANK]
        wad = at(10048, KT, GRANK)
        LA = at(10176, 2, T)
        BC = at(11328, 2, T)
        QG = at(12480, 2, T)
        KG = at(13632, 2, T)
        XL = at(14784, 2, 7, T)
        attg = at(22848, 4, 128)
        attw = at(23360, 2, 1024)
        vt = at(25408, 4, 128)
        kgt = at(25920, 2, 128)
        Sg = at(26176, 2, 128)
        ebl = at(26432, 2, 12)
        E1 = at(26456, 2, T)
        hflat = hT[:, :, :].rearrange("p a b -> p (a b)")
        SSg = hflat[:, 0:2048].rearrange("p (t j n) -> p t j n", t=2, j=8)
        Vm = dring[0:64, 0:4096].rearrange("p (h j n) -> p h j n", h=4, j=8)
        Gy = at(0, SG, BL + 1, SC)
        Ub = at(4608, SG, NB)
        FZT = at(9216, SG, P)
        Mt = at(13312, SG, P)
        FZ = at(17408, SG, BL, SC)
        Yb = at(17408, SG, NB)
        Yf = at(19712, 4, BL, NB)
        ZZ = at(21504, 2, SG, NB)
        Kb = at(21504, SG, P)[0:SC]
        fsw = at(21504, 2, SG, SC)
        gsw = at(22528, 2, SG, SC)
        ft = at(23552, SG, SC)
        gt = at(24064, SG, SC)
        XX = at(26112, SG, NB + 1)
        BC4 = at(26112, 4, SG, SC)
        up = dring[:, 0:4 * T].rearrange("p (a s b) -> p a s b", a=4, s=BL)
        wglu = at(9216, 4, HALF)
        LAX = at(14784, 4, T)
        Yf_tok = at(0, 4, T)
        sgl = at(2304, 4, T)
        x0st = dring[:, 0:256].rearrange("p (g j) -> p g j", g=SG)
        x0sw = dring[:, 4352:4608].rearrange("p (g j) -> p g j", g=SG)
        SO = dring[:, 4608:4896].rearrange("p (g j) -> p g j", g=SG)
        st1 = dring[:, 4896:5152].rearrange("p (g j) -> p g j", g=SG)
        st2 = dring[:, 5152:5408].rearrange("p (g j) -> p g j", g=SG)
        tab = sqf[:, 0:768].rearrange("p (k g) -> p k g", g=SG)
        UC, US = (at(17408 + 2048 * k, SG, NBP) for k in range(2))
        TA = XX[:, :, 0:NBP]
        TB = hflat[:, 4 * T:4 * T + SG * NBP].rearrange("p (g b) -> p g b", g=SG)
        (l_re, l_im, l_st, t_a, t_b, t_er, t_s, t_c, t_n, lr, li, lis, wr, wi, wis, t_d,
         lr8, li8) = (tab[:, k, :] for k in range(18))
        li2 = tab[:, 18:20, :]
        lis8 = li2[:, 0, :]
        t_e, t_f = tab[:, 20, :], tab[:, 21, :]
        u_scr = nc.dram_tensor("u_scratch", (4 * P, BL, NB), F32, kind="Internal").ap()
        y_scr = nc.dram_tensor("y_scratch", (4 * P, BL, NB), F32, kind="Internal").ap()

        def odd_sp(sp, stream, out):
            sp.wait_ge(S("proj_done"), USE["down0"] + 8)
            sp.dma_start(wad, d["w_ad"]).then_inc(S("o_small_in"), 16)
            sp.dma_start(aup, d["a_up"]).then_inc(S("o_small_in"), 16)
            stream("o_in")
            sp.wait_ge(S("proj_done"), USE["o_in"] + O_TILES)
            sp.dma_start(SSg, d["gS"]).then_inc(S("gS_in"), 16)
            sp.wait_ge(S("gl_st"), NCH + 1)
            out("pG", Sg)
            sp.wait_ge(S("gs_st"), 2)
            sp.dma_start(o["sG"], SSg).then_inc(S("sG_written"), 16)
            sp.wait_ge(S("ycat"), 12)
            sp.wait_ge(S("out_written"), 16 * 6)
            sp.dma_start(tab[:, 0:3, :], d["s5_lam"]).then_inc(S("s5_in"), 16)
            sp.dma_start(BC4, d["s5_bc"]).then_inc(S("s5_in"), 16)
            sp.dma_start(x0sw, d["s5_x0"][:, 1]).then_inc(S("x0_in"), 16)
            sp.wait_ge(S("s5_up"), 1)
            sp.dma_start(u_scr.rearrange("(a p) s b -> p a (s b)", p=P),
                         up.rearrange("p a s b -> p a (s b)")).then_inc(S("u_scratched"), 16)
            sp.wait_ge(S("u_scratched"), 16)
            sp.dma_start(x0st, d["s5_x0"][:, 0]).then_inc(S("x0_in"), 16)
            uv = u_scr.rearrange("(g c) s b -> s c g b", c=SC)
            for s in range(BL):
                sp.dma_start(Ub[SC * s:SC * s + SC], uv[s]).then_inc(S("U_in"), 16)
            sp.wait_ge(S("s5_mzero"), 1)
            sp.wait_ge(S("s5_kc"), 8)
            for s in range(BL):
                sp.dma_start(Mt[SC * s:SC * s + SC, :, SC * s:P], Kb[:, :, 0:P - SC * s]).then_inc(S("M_in"), 16)
            sp.wait_ge(S("s5_zc"), 8)
            sp.dma_start(wglu, d["w_glu"]).then_inc(S("glu_in"), 16)
            for r in range(2):
                sp.dma_start(ZZ[64 * r:64 * r + 64, 1], ZZ[64 - 64 * r:128 - 64 * r, 0]).then_inc(S("zsw_in"), 16)
            sp.wait_ge(S("s5_yc"), 8)
            yv = y_scr.rearrange("(g c) t b -> t c g b", c=SC)
            for t in range(BL):
                sp.dma_start(yv[t], Yb[SC * t:SC * t + SC]).then_inc(S("y_scratched"), 16)
            sp.wait_ge(S("y_scratched"), 16 * BL)
            sp.dma_start(Yf.rearrange("p a s b -> p a (s b)"),
                         y_scr.rearrange("(a p) s b -> p a (s b)", p=P)).then_inc(S("Y_in"), 16)
            sp.wait_ge(S("s5_scan"), 1)
            out("s5", SO)
            stream("o_out")
            sp.wait_ge(S("proj_done"), USE["ffn1"])
            sp.wait_ge(S("out_written"), 16 * 7)
            sp.dma_start(convin, d["conv_state"][1]).then_inc(S("convin_in"), 16)
            stream("ffn1")
            stream("down1")
            for s in range(2):
                sp.wait_ge(S(f"ext_free{s}"), 1 + 7 + 2 * FT)
            out("conv1", convout)
            sp.wait_ge(S("h_ready"), 40)
            out("y", hT[:])

        def odd_pool(pool, chain):
            G = nc.gpsimd
            pool.wait_ge(S("ycat"), 12)
            G.memset(Mt.rearrange("p a b -> p (a b)"), 0.0).then_inc(S("s5_mzero"), 1)
            pool.wait_ge(S("s5_lam"), 1)
            neg = v_("sgn")
            chain(G.tensor_scalar(Gy[:, :, 0, :], BC4[:, 2], neg, -1.0, ALU.mult, ALU.mult))
            chain(G.tensor_scalar(gsw[:, 0], BC4[:, 3], neg, None, ALU.mult))
            for k in range(BL):
                g, sw, nsw = Gy[:, :, k, :], gsw[:, k % 2], gsw[:, (k + 1) % 2]
                r, i = bc(lr, 2, SC), bc(lis, 2, SC)
                chain(tt(G, Gy[:, :, k + 1, :], g, r, ALU.mult))
                chain(tt(G, gt, sw, i, ALU.mult))
                chain(tt(G, Gy[:, :, k + 1, :], Gy[:, :, k + 1, :], gt, ALU.subtract))
                chain(tt(G, nsw, sw, r, ALU.mult))
                chain(tt(G, gt, g, i, ALU.mult))
                tt(G, nsw, nsw, gt, ALU.add).then_inc(S("s5_g"), 1)
                pool.wait_ge(S("s5_g"), k + 1)

        def odd_pe(pe, norm, project, head_norm):
            norm(2)
            pe.wait_ge(S("h_lo"), 32)
            pe.wait_ge(S("small_split"), 2)
            for a in range(2):
                h = slice(a * TH, (a + 1) * TH)
                for k in range(KT):
                    last = mm3(PP[2][0:GRANK, a, 0:TH], wad_hi.r[:, k, :], wad_lo.r[:, k, :],
                               H_HI["o_in"][k].r[:, h], hT_r[:, k, h], k == 0, k == KT - 1)
            last.then_inc(S("ad_done"), 1)
            project("o_in")
            pe.wait_ge(S("ad_copied"), 1)
            for t in range(2):
                for a in range(2):
                    last = mm(PP[2 + t][:, a, 0:TH], aup[:, t * P:(t + 1) * P], adown[:, a * TH:(a + 1) * TH])
                last.then_inc(S("gl_up"), 1)
            pe.wait_ge(S("gl_qk"), 2)
            pe.wait_ge(S("gl_x"), 14)
            all_free(pe, "o_in", O_TILES)
            for c in range(NCH + 1):
                n, c0 = (L, L * c) if c < NCH else (NSAMP, SEQ)
                cols = slice(c0, c0 + n)
                if c:
                    pe.wait_ge(S("gl_tokc"), c)
                    pe.wait_ge(S("gl_st"), c + 1)
                for h in range(GH):
                    nc.tensor.transpose(bank(4)[0:n, h * P:(h + 1) * P], zo[:, 4 + h, cols], ident)
                for t in range(2):
                    last = nc.tensor.transpose(bank(5)[0:n, t * P:(t + 1) * P], KG[:, t, cols], ident)
                last.then_inc(S("gl_tok"), 1)
                for h in range(GH):
                    t, r = h // 2, slice(64 * (h % 2), 64 * (h % 2) + 64)
                    if 4 * c + h >= 2:
                        pe.wait_ge(S("gl_am"), 4 * c + h - 1)
                    lev = range(8) if c < NCH else range(4, 8)
                    for e, v in enumerate(lev):
                        out = PP[h % 2][0:n, (e * n) // 512, (e * n) % 512:(e * n) % 512 + n]
                        lhs, rhs = ((XL[r, t, v, cols], XL[r, t, v, cols]) if v < 7
                                    else (zo[r, 2 + t, cols], zo[r, t, cols]))
                        last = mm(out, lhs, rhs)
                    last.then_inc(S("gl_sc"), 1)
                pe.wait_ge(S("gl_tokc"), c + 1)
                pe.wait_ge(S("gl_st"), c + 1)
                if c == NCH:
                    pe.wait_ge(S("gS_in"), 16)
                if c:
                    pe.wait_ge(S("gl_oc"), c)
                for h in range(GH):
                    t, r = h // 2, slice(64 * (h % 2), 64 * (h % 2) + 64)
                    out = bank(6 + h % 2)[:, t * n:(t + 1) * n]
                    pe.wait_ge(S("gl_at"), 4 * c + h + 1)
                    mm(out, vt[:, h, :], attg[:, h, 0:n], True, False)
                    if c < NCH:
                        last = mm(out, Sg[r, t, :], QG[r, t, cols], False, True)
                    else:
                        for j in range(8):
                            last = mm(out[:, 8 * j:8 * j + 8], SSg[r, t, j, :], QG[r, t, c0 + 8 * j:c0 + 8 * j + 8],
                                      False, j == 7)
                last.then_inc(S("gl_o"), 1)
                if c < NCH:
                    for h in range(GH):
                        t, r = h // 2, slice(64 * (h % 2), 64 * (h % 2) + 64)
                        last = mm(bank(5)[r, 256 + t * P:256 + (t + 1) * P], kgt[0:n, t, r], vt[0:n, h, :])
                    last.then_inc(S("gl_s"), 1)
                else:
                    pe.wait_ge(S("gs_vm"), 1)
                    pe.wait_ge(S("gl_am"), 20)
                    for t in range(2):
                        for h in (2 * t, 2 * t + 1):
                            r = slice(64 * (h % 2), 64 * (h % 2) + 64)
                            for a in range(2):
                                last = mm(PP[t][r, a, :], kgt[0:n, t, r], Vm[:, h, 4 * a:4 * a + 4, :])
                        last.then_inc(S("gs_s"), 1)
            pe.wait_ge(S("gs_st"), 2)
            head_norm("gn", zo[:, 0:4, :], LAX, ones, mean=False)

            pe.wait_ge(S("ycat"), 12)
            pe.wait_ge(S("s5_f"), 8)
            for b in range(8):
                if b >= 2:
                    pe.wait_ge(S("s5_ftc"), b - 1)
                for e in range(4):
                    last = nc.tensor.transpose(bank(b % 2)[:, e * P:(e + 1) * P],
                                               FZ[:, 4 * b + e, :, :].rearrange("p s c -> p (s c)"), ident)
                last.then_inc(S("s5_ft"), 1)
            pe.wait_ge(S("s5_g"), 8)
            for b in range(8):
                if b >= 2:
                    pe.wait_ge(S("s5_kc"), b - 1)
                for e in range(4):
                    g = 4 * b + e
                    last = mm(bank(2 + b % 2)[0:SC, e * P:(e + 1) * P], FZ[:, g, BL - 1, :],
                              Gy[:, g, 0:BL, :].rearrange("p s c -> p (s c)"))
                last.then_inc(S("s5_k"), 1)
            pe.wait_ge(S("U_in"), 16 * BL)
            pe.wait_ge(S("s5_ftc"), 8)
            for b in range(8):
                if b >= 2:
                    pe.wait_ge(S("s5_zc"), b - 1)
                for e in range(4):
                    last = mm(bank(4 + b % 2)[:, e * NB:(e + 1) * NB], FZT[:, 4 * b + e, :], Ub[:, 4 * b + e, :])
                last.then_inc(S("s5_z"), 1)
            pe.wait_ge(S("M_in"), 16 * BL)
            pe.wait_ge(S("s5_scan"), 2)
            for b in range(8):
                if b >= 2:
                    pe.wait_ge(S("s5_yc"), b - 1)
                for e in range(4):
                    g = 4 * b + e
                    out = bank(6 + b % 2)[:, e * NB:(e + 1) * NB]
                    mm(out, Mt[:, g, :], Ub[:, g, :], True, False)
                    last = mm(out, Gy[:, g, 1:BL + 1, :].rearrange("p s c -> p (s c)"), XX[:, g, 0:NB], False, True)
                last.then_inc(S("s5_y"), 1)
            pe.wait_ge(S("s5_gelu"), 4)
            pe.wait_ge(S("glu_in"), 16)
            for m in range(4):
                for a in range(2):
                    for k in range(4):
                        last = mm(PP[m][:, a, 0:TH], wglu[:, k, m * P:(m + 1) * P], Yf_tok[:, k, a * TH:(a + 1) * TH],
                                  k == 0, k == 3)
                last.then_inc(S("s5_glu"), 1)
            project("o_out")

        def odd_act(act, A, chain, norm, evac, head_norm, split_h):
            norm(2)
            split_h("o_in")
            act.wait_ge(S("ad_done"), 1)
            A(halves(adown), PP[2][0:GRANK, :, 0:TH], ACT.Copy).then_inc(S("ad_copied"), 1)
            evac("o_in", 0, 2, ACT.Copy, zo[:, 0:2, :], GDK ** -0.5)
            evac("o_in", 2, 6, ACT.Copy, zo[:, 2:8, :])
            evac("o_in", 8, 4, ACT.Silu, zo[:, 8:12, :])
            evac("o_in", 12, 4, ACT.Copy, zo[:, 12:16, :])
            for t in range(2):
                act.wait_ge(S("gl_up"), t + 1)
                chain(A(halves(LA[:, t, :]), pair(2 + t), ACT.Identity, bias=v_("a_b", t)))
                chain(A(BC[:, t, :], LA[:, t, :], ACT.Abs))
            for t in range(2):
                chain(A(BC[:, t, :], BC[:, t, :], ACT.Exp, scale=-1.0))
                A(BC[:, t, :], BC[:, t, :], ACT.Ln, bias=1.0).then_inc(S("gl_sp"), 1)
            for t in range(2):
                act.wait_ge(S("gl_kd"), t + 1)
                A(E1[:, t, :], BC[:, t, :], ACT.Exp)
                A(KG[:, t, :], KG[:, t, :], ACT.Exp).then_inc(S("gl_e1"), 1)
            for k in range(14):
                t, v = k // 7, k % 7
                n = SEQ if v < 4 else T
                act.wait_ge(S("gl_d"), k + 1)
                A(XL[:, t, v, 0:n], XL[:, t, v, 0:n], ACT.Exp).then_inc(S("gl_e"), 1)
            for c in range(NCH + 1):
                n, c0 = (L, L * c) if c < NCH else (NSAMP, SEQ)
                act.wait_ge(S("gl_tok"), c + 1)
                A(vt[0:n].rearrange("p a b -> p (a b)"), bank(4)[0:n, :], ACT.Copy)
                A(kgt[0:n].rearrange("p a b -> p (a b)"), bank(5)[0:n, 0:256], ACT.Copy).then_inc(S("gl_tokc"), 1)
                act.wait_ge(S("gl_o"), c + 1)
                for a in range(2):
                    last = A(zo[:, a:4:2, c0:c0 + n], bank(6 + a)[:, 0:2 * n].rearrange("p (h n) -> p h n", h=2),
                             ACT.Copy)
                last.then_inc(S("gl_oc"), 1)
            act.wait_ge(S("gl_oc"), NCH + 1)
            for h in range(4):
                act.sem_inc(S("hn_src"), 1)
            head_norm("gn", zo[:, 0:4, :], LAX, GDV, EPS, mean=False)

            act.wait_ge(S("ycat"), 12)
            act.wait_ge(S("s5_in"), 32)
            A(t_s, l_st, ACT.Exp).then_inc(S("s5_trig"), 1)
            act.wait_ge(S("s5_ab"), 1)
            A(t_er, t_a, ACT.Exp)
            A(t_s, t_s, ACT.Sin)
            A(t_c, t_c, ACT.Sin).then_inc(S("s5_trig"), 1)
            for b in range(8):
                act.wait_ge(S("s5_ft"), b + 1)
                A(FZT[:, 4 * b:4 * b + 4, :].rearrange("p a b -> p (a b)"), bank(b % 2), ACT.Copy).then_inc(
                    S("s5_ftc"), 1)
            for b in range(8):
                act.wait_ge(S("s5_k"), b + 1)
                A(Kb[:, 4 * b:4 * b + 4, :].rearrange("p a b -> p (a b)"), bank(2 + b % 2)[0:SC, :],
                  ACT.Copy).then_inc(S("s5_kc"), 1)
            act.wait_ge(S("M_in"), 16 * BL)
            for b in range(8):
                act.wait_ge(S("s5_z"), b + 1)
                A(ZZ[:, 0, 4 * b:4 * b + 4, :].rearrange("p a b -> p (a b)"), bank(4 + b % 2)[:, 0:4 * NB],
                  ACT.Copy).then_inc(S("s5_zc"), 1)
            for b in range(8):
                act.wait_ge(S("s5_y"), b + 1)
                A(Yb[:, 4 * b:4 * b + 4, :].rearrange("p a b -> p (a b)"), bank(6 + b % 2)[:, 0:4 * NB],
                  ACT.Copy).then_inc(S("s5_yc"), 1)
            for k in range(4):
                act.wait_ge(S("s5_ys"), k + 1)
                A(Yf_tok[:, k, :], Yf_tok[:, k, :], ACT.Gelu_apprx_tanh).then_inc(S("s5_gelu"), 1)
            for m in range(4):
                act.wait_ge(S("s5_glu"), m + 1)
                A(halves(sgl[:, m, :]), pair(m), ACT.Sigmoid).then_inc(S("s5_sig"), 1)
            split_h("o_out")

        def odd_dve(dve, V, chain, norm, residual, head_norm, split_h):
            norm(2, "norm_mix", 8)
            split_h("o_in")
            dve.wait_ge(S("out_written"), 16 * 5)
            for t in range(2):
                dve.wait_ge(S("gl_sp"), t + 1)
                la, b_ = LA[:, t, :], BC[:, t, :]
                chain(stt(la, la, 0.0, b_, ALU.min, ALU.subtract))
                chain(V.tensor_scalar(la, la, 1.0 / GLA_TAU, None, ALU.mult))
                chain(V.tensor_tensor_scan(b_, c_("scan128", T), la, 0.0, ALU.mult, ALU.add))
                kd = KG[:, t, :]
                for c0, m, n in ((0, NCH, L), (SEQ, 8, 8)):
                    b3, k3 = (x[:, c0:c0 + m * n].rearrange("p (c n) -> p c n", n=n) for x in (b_, kd))
                    last = tt(V, k3, bc(b3[:, :, n - 1], 2, n), b3, ALU.subtract)
                last.then_inc(S("gl_kd"), 1)
            for t in range(2):
                dve.wait_ge(S("gl_e1"), t + 1)
                e1 = E1[:, t, :]
                V.tensor_copy(ebl[:, t, 0:4], e1[:, 0:SEQ].rearrange("p (c n) -> p c n", n=L)[:, :, L - 1])
                V.tensor_copy(ebl[:, t, 4:12], e1[:, SEQ:T].rearrange("p (c n) -> p c n", n=8)[:, :, 7])
                tt(V, QG[:, t, :], zo[:, t, :], e1, ALU.mult)
                tt(V, KG[:, t, :], zo[:, 2 + t, :], KG[:, t, :], ALU.mult).then_inc(S("gl_qk"), 1)

            def parts(x, v):
                h = 64 >> v
                n = SEQ if v < 4 else T
                b = x[:, 0:n].rearrange("p (b a h) -> p b a h", a=2, h=h)
                return b[:, :, 0, :], b[:, :, 1, :], h

            def diffs(k):
                t, v = k // 7, k % 7
                low, high, h = parts(XL[:, t, v, :], v)
                bl, bh, _ = parts(BC[:, t, :], v)
                ref = bc(bl[:, :, h - 1], 2, h)
                tt(V, low, ref, bl, ALU.subtract)
                tt(V, high, bh, ref, ALU.subtract).then_inc(S("gl_d"), 1)

            def scales(k):
                t, v = k // 7, k % 7
                dve.wait_ge(S("gl_e"), k + 1)
                low, high, _ = parts(XL[:, t, v, :], v)
                kl, _, _ = parts(zo[:, 2 + t, :], v)
                _, qh_, _ = parts(zo[:, t, :], v)
                tt(V, low, low, kl, ALU.mult)
                tt(V, high, high, qh_, ALU.mult).then_inc(S("gl_x"), 1)

            diffs(0)
            diffs(1)
            for k in range(14):
                if k < 12:
                    diffs(k + 2)
                scales(k)
            V.memset(Sg, 0.0).then_inc(S("gl_st"), 1)
            for c in range(NCH + 1):
                n = L if c < NCH else NSAMP
                nl = 8 if c < NCH else 4
                m = c_("gla", 1024) if c < NCH else c_("gla_s", 256, 64)
                for h in range(GH):
                    w = attw[0:n, h % 2, 0:nl * n]
                    dve.wait_ge(S("gl_sc"), 4 * c + h + 1)
                    if c == NCH and h == 0:
                        V.memset(attg[NSAMP:P, :, 0:NSAMP], 0.0)
                    if c < NCH:
                        tt(V, w.rearrange("p (a b) -> p a b", a=2), PP[h % 2][:, :, :],
                           m.rearrange("p (a b) -> p a b", a=2), ALU.mult).then_inc(S("gl_am"), 1)
                    else:
                        tt(V, w, PP[h % 2][0:n, 0, 0:256], m, ALU.mult).then_inc(S("gl_am"), 1)
                    dve.wait_ge(S("gl_am"), 4 * c + h + 1)
                    V.tensor_reduce(attg[0:n, h, 0:n], w.rearrange("p (v n) -> p n v", v=nl), AX.X,
                                    ALU.add).then_inc(S("gl_at"), 1)
                if c < NCH:
                    dve.wait_ge(S("gl_s"), c + 1)
                    for t in range(2):
                        last = stt(Sg[:, t, :], Sg[:, t, :], ebl[:, t, c:c + 1], bank(5)[:, 256 + t * P:256 + (t + 1) * P],
                                   ALU.mult, ALU.add)
                    last.then_inc(S("gl_st"), 1)
                    dve.wait_ge(S("gl_st"), c + 2)
            dve.wait_ge(S("gl_tokc"), NCH + 1)
            for h in range(GH):
                last = tt(V, Vm[:, h], bc(vt[0:64, h, :], 1, 8), bc(seqmask[0:64, :], 2, P), ALU.mult)
            last.then_inc(S("gs_vm"), 1)
            dve.wait_ge(S("gl_o"), NCH + 1)
            dve.wait_ge(S("gS_in"), 16)
            for t in range(2):
                chain(tt(V, SSg[:, t], SSg[:, t], bc(ebl[:, t, 4:12], 2, P), ALU.mult))
                dve.wait_ge(S("gs_s"), t + 1)
                s4 = SSg[:, t].rearrange("p (a j) n -> p a (j n)", a=2)
                tt(V, s4, s4, PP[t][:, :, :], ALU.add).then_inc(S("gs_st"), 1)
            head_norm("gn", zo[:, 0:4, :], LAX, GDV, mean=False)
            dve.wait_ge(S("sG_written"), 16)
            for h in range(4):
                stt(hT[:, h, :], zo[:, h, :], v_("o_ln_g", h), zo[:, 8 + h, :], ALU.mult,
                    ALU.mult).then_inc(S("ycat"), 1)

            dve.wait_ge(S("ycat"), 12)
            for k in range(4):
                last = V.tensor_copy(up[:, k], zo[:, 12 + k, :].rearrange("p (b s) -> p s b", s=BL))
            last.then_inc(S("s5_up"), 1)
            dve.wait_ge(S("s5_trig"), 1)
            chain(tt(V, t_a, l_re, t_s, ALU.mult))
            chain(tt(V, t_b, l_im, t_s, ALU.mult))
            for out, shift in ((t_s, 0.0), (t_c, np.pi / 2)):
                chain(V.tensor_scalar(t_n, t_b, 1.0 / TWO_PI, shift / TWO_PI, ALU.mult, ALU.add))
                chain(V.tensor_scalar(t_n, t_n, ROUND, None, ALU.add))
                chain(V.tensor_scalar(t_n, t_n, -ROUND, None, ALU.add))
                chain(stt(out, t_n, -6.28125, t_b, ALU.mult, ALU.add))
                chain(stt(out, t_n, -(TWO_PI - 6.28125), out, ALU.mult, ALU.add))
                chain(V.tensor_scalar(out, out, float(shift), 3.1415925, ALU.add, ALU.min))
                ins = V.tensor_scalar(out, out, -3.1415925, None, ALU.max)
                if shift:
                    ins.then_inc(S("s5_ab"), 1)
                else:
                    chain(ins)
            dve.wait_ge(S("s5_trig"), 2)
            chain(tt(V, lr, t_er, t_c, ALU.mult))
            chain(tt(V, li, t_er, t_s, ALU.mult))
            V.tensor_scalar(lis, li, v_("sgn"), None, ALU.mult).then_inc(S("s5_lam"), 1)
            dve.wait_ge(S("s5_lam"), 1)
            chain(tt(V, t_d, l_re, l_re, ALU.mult))
            chain(tt(V, t_e, l_im, l_im, ALU.mult))
            chain(tt(V, t_d, t_d, t_e, ALU.add))
            chain(V.reciprocal(t_d, t_d))
            chain(V.tensor_scalar(t_f, lr, -1.0, None, ALU.add))
            for out, x, y, op in ((wr, l_re, l_im, ALU.add), (wi, l_im, l_re, ALU.subtract)):
                chain(tt(V, out, t_f, x, ALU.mult))
                chain(tt(V, t_e, li, y, ALU.mult))
                if op == ALU.add:
                    chain(tt(V, out, out, t_e, ALU.add))
                else:
                    chain(tt(V, out, t_e, out, ALU.subtract))
                chain(tt(V, out, out, t_d, ALU.mult))
            chain(V.tensor_scalar(wis, wi, v_("sgn"), None, ALU.mult))

            def turn(out, osw, x, xsw, r, i, done=None):
                r, i = bc(r, 2, SC), bc(i, 2, SC)
                chain(tt(V, out, x, r, ALU.mult))
                chain(tt(V, ft, xsw, i, ALU.mult))
                chain(tt(V, out, out, ft, ALU.add))
                chain(tt(V, osw, xsw, r, ALU.mult))
                chain(tt(V, ft, x, i, ALU.mult))
                tt(V, osw, osw, ft, ALU.subtract).then_inc(S("s5_f"), 1)
                dve.wait_ge(S("s5_f"), done)

            turn(FZ[:, :, BL - 1, :], fsw[:, 0], BC4[:, 0], BC4[:, 1], wr, wis, 1)
            for k in range(1, BL):
                s = BL - 1 - k
                turn(FZ[:, :, s, :], fsw[:, k % 2], FZ[:, :, s + 1, :], fsw[:, (k + 1) % 2], lr, lis, k + 1)
            chain(V.tensor_copy(lr8, lr))
            chain(V.tensor_copy(li8, li))
            for _ in range(3):
                chain(tt(V, t_d, lr8, lr8, ALU.mult))
                chain(tt(V, t_e, li8, li8, ALU.mult))
                chain(tt(V, li8, lr8, li8, ALU.mult))
                chain(V.tensor_scalar(li8, li8, 2.0, None, ALU.mult))
                chain(tt(V, lr8, t_d, t_e, ALU.subtract))
            chain(V.tensor_scalar(lis8, li8, v_("sgn"), None, ALU.mult))
            chain(V.tensor_scalar(li2[:, 1, :], lis8, -1.0, None, ALU.mult))
            uc, us, r8 = t_a, t_b, t_er
            for _ in range(3):
                chain(tt(V, r8, r8, r8, ALU.mult))
            chain(V.tensor_copy(uc, t_c))
            chain(V.tensor_scalar(us, t_s, v_("sgn"), None, ALU.mult))

            def unit():
                tt(V, t_d, uc, uc, ALU.mult)
                chain(tt(V, t_e, us, us, ALU.mult))
                chain(tt(V, t_d, t_d, t_e, ALU.add))
                chain(V.tensor_scalar(t_d, t_d, -0.5, 1.5, ALU.mult, ALU.add))
                tt(V, uc, uc, t_d, ALU.mult)
                chain(tt(V, us, us, t_d, ALU.mult))

            def square():
                tt(V, t_d, uc, uc, ALU.mult)
                tt(V, t_e, us, us, ALU.mult)
                chain(stt(us, uc, 2.0, us, ALU.mult, ALU.mult))
                chain(tt(V, uc, t_d, t_e, ALU.subtract))
                unit()

            unit()
            for _ in range(3):
                square()
            dve.wait_ge(S("s5_k"), 8)
            V.memset(UC[:, :, 0:1], 1.0)
            chain(V.memset(US[:, :, 0:1], 0.0))
            n = 1
            while n < NBP:
                c0, s0, c1, s1 = UC[:, :, 0:n], US[:, :, 0:n], UC[:, :, n:2 * n], US[:, :, n:2 * n]
                cn, sn = bc(uc, 2, n), bc(us, 2, n)
                ta, tb = TA[:, :, 0:n], TB[:, :, 0:n]
                tt(V, c1, c0, cn, ALU.mult)
                tt(V, s1, s0, cn, ALU.mult)
                tt(V, ta, s0, sn, ALU.mult)
                chain(tt(V, tb, c0, sn, ALU.mult))
                tt(V, c1, c1, ta, ALU.subtract)
                chain(tt(V, s1, s1, tb, ALU.add))
                n *= 2
                if n < NBP:
                    square()
            dve.wait_ge(S("s5_g"), 8)
            dve.wait_ge(S("s5_kc"), 8)
            dve.wait_ge(S("zsw_in"), 32)
            z, zs = (ZZ[:, k, :, 0:NBP] for k in range(2))
            tt(V, TA, zs, US, ALU.mult)
            tt(V, TB, z, US, ALU.mult)
            tt(V, z, z, UC, ALU.mult)
            chain(tt(V, zs, zs, UC, ALU.mult))
            tt(V, z, z, TA, ALU.subtract)
            chain(tt(V, zs, zs, TB, ALU.add))
            for g in range(SG):
                for w in (z, zs):
                    last = V.tensor_tensor_scan(w[:, g, :], r8[:, g:g + 1].to_broadcast([P, NBP]), w[:, g, :], 0.0,
                                                ALU.mult, ALU.add)
            chain(last)
            tt(V, zs, zs, US, ALU.mult)
            tt(V, z, z, UC, ALU.mult)
            chain(V.memset(XX[:, :, 0:1], 0.0))
            chain(tt(V, XX[:, :, 1:NBP + 1], z, zs, ALU.add))
            chain(V.tensor_copy(SO[:, :, 0], XX[:, :, NBP]))
            dve.wait_ge(S("x0_in"), 32)
            x0 = x0st
            tt(V, st1, x0, bc(lr8, 2, 8), ALU.mult)
            chain(tt(V, st2, x0sw, bc(lis8, 2, 8), ALU.mult))
            chain(tt(V, st1, st1, st2, ALU.add))
            tt(V, SO[:, :, 1:9], st1, ZZ[:, 0, :, NBP:NB], ALU.add).then_inc(S("s5_scan"), 1)
            V.tensor_copy(XX[:, :, NBP:NB], x0).then_inc(S("s5_scan"), 1)
            dve.wait_ge(S("Y_in"), 16)
            dve.wait_ge(S("s5_y"), 8)
            for k in range(4):
                stt(Yf_tok[:, k, :].rearrange("p (b s) -> p b s", s=BL),
                    zo[:, 12 + k, :].rearrange("p (b s) -> p b s", s=BL), v_("o_d", k),
                    Yf[:, k].rearrange("p s b -> p b s"), ALU.mult, ALU.add).then_inc(S("s5_ys"), 1)
            for m in range(4):
                dve.wait_ge(S("s5_sig"), m + 1)
                tt(V, hT[:, 4 + m, :], Yf_tok[:, m, :], sgl[:, m, :], ALU.mult).then_inc(S("ycat"), 1)
            split_h("o_out")
            residual("o_out")

        @block.sync
        def _(sp):
            def stream(name):
                c0 = CHUNK0[name]
                if name in RUNS:
                    t0, n = RUNS[name]
                    with sp.Fori(0, (n - 2) // 2) as i:
                        for s in range(2):
                            sp.wait_ge(S("w_split"), 2 * i + (c0 + s + 1))
                            sp.dma_start(w_ring[:, s, :], d["w"][bass.ds(2 * i + (t0 + 2 + s), 1)].rearrange(
                                "a p n -> p (a n)")).then_inc(WL[s], 16)
                    done = c0 + n
                else:
                    l = int(name[4:])

                    def load(e, i):
                        tile, j = e // 3, e % 3
                        k0, nk = DCH[j]
                        if i is None:
                            sp.wait_ge(S("w_split"), c0 + e - 1)
                            src = d["w_down"][8 * l + tile, :, k0 * P:(k0 + nk) * P]
                        else:
                            sp.wait_ge(S("w_split"), 6 * i + (c0 + e - 1))
                            src = d["w_down"][bass.ds(2 * i + (8 * l + tile), 1), :, k0 * P:(k0 + nk) * P].rearrange(
                                "a p n -> p (a n)")
                        sp.dma_start(w_ring[:, e % 2, 0:nk * P], src).then_inc(WL[e % 2], 16)

                    with sp.Fori(0, 3) as i:
                        for e in range(2, 8):
                            load(e, i)
                    for e in range(20, 24):
                        load(e, None)
                    done = c0 + 24
                nxt = NEXT[name]
                if nxt is None:
                    return
                for s in range(2):
                    sp.wait_ge(S("w_split"), done + s - 1)
                    if nxt in RUNS:
                        sp.dma_start(w_ring[:, s, :], d["w"][RUNS[nxt][0] + s]).then_inc(WL[s], 16)
                    else:
                        k0, nk = DCH[s]
                        sp.dma_start(w_ring[:, s, 0:nk * P], d["w_down"][8 * int(nxt[4:]), :, k0 * P:(k0 + nk) * P]
                                     ).then_inc(WL[s], 16)

            nout = [0]

            def out(name, src):
                nout[0] += 16
                sp.dma_start(o[name], src).then_inc(S("out_written"), 16)

            sp.dma_start(cst[:], d["consts"]).then_inc(S("consts_in"), 16)
            for k in range(KT):
                sp.dma_start(xT[:, k, :], d["x"][:, k, :]).then_inc(S("x_in"), 16)
            sp.dma_start(vec[:], d["vec"]).then_inc(S("vec_in"), 16)
            sp.dma_start(wif, d["w_if"]).then_inc(S("e_small_in"), 16)
            for s in range(2):
                sp.dma_start(w_ring[:, s, :], d["w"][s]).then_inc(WL[s], 16)
            sp.dma_start(shin, d["shift"]).then_inc(S("e_small_in"), 16)
            sp.dma_start(lora, d["lora"]).then_inc(S("e_small_in"), 16)
            sp.dma_start(r_m0[:, 0:8], d["m0"]).then_inc(S("e_small_in"), 16)
            sp.dma_start(convp[:], d["convp"]).then_inc(S("e_small_in"), 16)
            stream("e_in")
            sp.wait_ge(S("proj_done"), E_TILES)
            sp.dma_start(Csf, d["C"]).then_inc(S("C_in"), 16)
            for s in range(2):
                sp.wait_ge(S(f"ext_free{s}"), 1 + 7)
            out("shift", shout)
            sp.wait_ge(S("ml_m_out"), 1)
            out("m", r_mo[:, 0:NSEQ])
            sp.wait_ge(S("ml_state"), 4)
            out("pC", Cst)
            sp.wait_ge(S("ml_sst"), 11)
            sp.dma_start(o["sC"], Csf).then_inc(S("sC_written"), 16)
            sp.wait_ge(S("rw_prep"), 4)
            sp.dma_start(SS, d["rS"]).then_inc(S("rS_in"), 16)
            sp.wait_ge(S("rk_st"), NCR + 1)
            out("pS", Sr)
            sp.wait_ge(S("rs_st"), 1)
            sp.dma_start(o["sS"], SS).then_inc(S("sS_written"), 16)
            stream("e_out")
            sp.wait_ge(S("sS_written"), 16)
            sp.wait_ge(S("proj_done"), USE["ffn0"])
            sp.dma_start(convin, d["conv_state"][0]).then_inc(S("convin_in"), 16)
            stream("ffn0")
            stream("down0")
            for s in range(2):
                sp.wait_ge(S(f"ext_free{s}"), 1 + 7 + FT)
            out("conv0", convout)
            if do_odd:
                odd_sp(sp, stream, out)
            if not do_odd:
                all_free(sp, "down0", 8)
                out("y", xT[:])
            for n in ("sC_written", "sS_written", "sG_written"):
                sp.wait_ge(S(n), 16)
            sp.wait_ge(S("out_written"), nout[0])

        @block.gpsimd
        def _(pool):
            G = nc.gpsimd
            chain = Chain(pool, S("pool_chain"))

            def split(w, hi, lo, sem):
                one = (bc(ones[:, 0:w.shape[1]], 2, w.shape[2]) if len(w.shape) == 3
                       else ones[:, 0:1].to_broadcast(list(w.shape)))
                chain(tt(G, hi.r, w, one, ALU.mult))
                tt(G, lo.r, w, hi.r, ALU.subtract).then_inc(sem, 1)

            def chunk(s, n=KT * P):
                hi, lo = (Rounded(v.f[:, s, 0:n], v.r[:, s, 0:n]) for v in (w_hi, w_lo))
                split(w_ring[:, s, 0:n], hi, lo, S("w_split"))

            def project(name, first=0):
                with pool.Fori(first, RUNS[name][1] // 2) as i:
                    chain.loop(i, 2, first)
                    for s in range(2):
                        pool.wait_ge(WL[s], 16 * i + 16 * (CHUNK0[name] // 2 + 1))
                        pool.wait_ge(S("proj_done"), 2 * i + (USE[name] + s - 1))
                        chunk(s)
                    chain.end_loop(RUNS[name][1] // 2 - first)

            def down(l):
                pool.wait_ge(S("proj_done"), USE[f"down{l}"] - 1)
                with pool.Fori(0, 4) as i:
                    chain.loop(i, 6)
                    for e in range(6):
                        tile, j = e // 3, e % 3
                        pool.wait_ge(WL[e % 2], 48 * i + 16 * (CHUNK0[f"down{l}"] // 2 + e // 2 + 1))
                        if j == 1:
                            pool.wait_ge(S("proj_done"), 2 * i + (USE[f"down{l}"] + tile))
                        else:
                            pool.wait_ge(S("chunk_used"), 4 * i + (16 * l + 2 * tile + (j == 2) + 1))
                        chunk(e % 2, DCH[j][1] * P)
                    chain.end_loop(4)

            pool.sem_inc(S("chunk_used"), 1)
            pool.wait_ge(S("consts_in"), 16)
            pool.wait_ge(S("e_small_in"), 16 * 5)
            split(wif, wif_hi, wif_lo, S("small_split"))
            for s in range(2):
                pool.wait_ge(WL[s], 16)
                chunk(s)
            project("e_in", 1)
            pool.wait_ge(S("rs_st"), 1)
            project("e_out")
            project("ffn0")
            down(0)
            pool.wait_ge(S("chunk_used"), 17)
            pool.wait_ge(S("o_small_in"), 32)
            split(wad, wad_hi, wad_lo, S("small_split"))
            project("o_in")
            odd_pool(pool, chain)
            pool.wait_ge(S("s5_scan"), 2)
            project("o_out")
            project("ffn1")
            down(1)

        @block.tensor
        def _(pe):
            def norm(n):
                for k in range(KT):
                    pe.wait_ge(S("sq_ready"), 8 * n + k + 1)
                    for a in range(2):
                        last = mm(PP[3][:, a, 0:TH], ones, sq[:, k % 2, a * TH:(a + 1) * TH], k == 0, k == KT - 1)
                    last.then_inc(S("sq_used"), 1)

            def project(name):
                t0, n = RUNS[name]
                pe.wait_ge(S("h_lo"), 8 * (SPLIT[name] + 1))
                with pe.Fori(0, n // 2) as i:
                    for s in range(2):
                        pe.wait_ge(S("w_split"), 2 * i + (CHUNK0[name] + s + 1))
                        pe.wait_ge(FREE[s], i + (USE[name] // 2 + 1))
                        for a in range(2):
                            h = slice(a * TH, (a + 1) * TH)
                            for k in range(KT):
                                c = slice(k * P, (k + 1) * P)
                                last = mm3(PP[s][:, a, 0:TH], w_hi.r[:, s, c], w_lo.r[:, s, c],
                                           H_HI[name][k].r[:, h], hT_r[:, k, h], k == 0, k == KT - 1)
                        last.then_inc(S("proj_done"), 1)

            def down(l):
                c0 = CHUNK0[f"down{l}"]
                with pe.Fori(0, 4) as i:
                    for s in range(2):
                        pe.wait_ge(FREE[s], i + (USE[f"down{l}"] // 2 + 1))
                        for j, (k0, nk) in enumerate(DCH):
                            c = (3 * s + j) % 2
                            pe.wait_ge(S("w_split"), 6 * i + (c0 + 3 * s + j + 1))
                            pe.wait_ge(S("act_lo"), FT * l + (AHEAD if k0 + nk <= AHEAD else FT if k0 + nk == FT
                                                              else k0 + nk))
                            for a in range(2):
                                h = slice(a * TH, (a + 1) * TH)
                                for k in range(k0, k0 + nk):
                                    b = slice((k - k0) * P, (k - k0 + 1) * P)
                                    last = mm3(PP[s][:, a, 0:TH], w_hi.r[:, c, b], w_lo.r[:, c, b],
                                               act_hi.r[:, (k + KT) % FT, h], act_lo.r[:, k, h], k == 0,
                                               k == FT - 1)
                            last.then_inc(S("proj_done" if j == 2 else "chunk_used"), 1)

            def head_norm(nm, src, sqs, avg, mean=True):
                if mean:
                    for h in range(4):
                        pe.wait_ge(S("hn_src"), HN[nm] + h + 1)
                        for a in range(2):
                            last = mm(PP[h][:, a, 0:TH], avg, src[:, h, a * TH:(a + 1) * TH])
                        last.then_inc(S("hn_mean"), 1)
                for h in range(4):
                    pe.wait_ge(S("hn_sq"), HN[nm] + h + 1)
                    for a in range(2):
                        last = mm(PP[h][:, a, 0:TH], avg, sqs[:, h, a * TH:(a + 1) * TH])
                    last.then_inc(S("hn_var"), 1)

            def mlstm():
                pe.wait_ge(S("ml_exps"), 4)
                pe.wait_ge(FREE[0], USE["e_out"] // 2 + 1)
                pe.wait_ge(FREE[1], USE["e_out"] // 2 + 1)
                for h in range(MH):
                    if h >= 2:
                        pe.wait_ge(S("ml_qh"), h - 1)
                    for a in range(2):
                        last = mm(PP[h % 2][:, a, 0:TH], sel[:, h, :], r_s[:, a * TH:(a + 1) * TH])
                    last.then_inc(S("ml_bcast"), 1)
                for h in range(MH):
                    mm(bank(4)[:, 12 * h:12 * h + 12], sel[:, h, :], r_dec[:, 0:12])
                for c in range(NCH + 1):
                    n = L if c < NCH else NSAMP
                    last = mm(bank(4)[0:n, 48 + 4 * c:52 + 4 * c], r_w[:, L * c:L * c + n], ident[0:4, 0:4])
                last.then_inc(S("ml_small"), 1)
                pe.wait_ge(S("ml_qh"), 4)
                for c in range(NCH + 1):
                    n, c0 = (L, L * c) if c < NCH else (NSAMP, SEQ)
                    cols = slice(c0, c0 + n)
                    if c:
                        pe.wait_ge(S("ml_att"), c)
                    for h in range(MH):
                        mm(bank(0)[0:n, h * n:(h + 1) * n], zm[:, 4 + h, cols], zm[:, h, cols])
                    for h in range(MH):
                        mm(bank(1)[0:n, h * n:(h + 1) * n], sel[:, h, 0:n], r_a[:, cols], True, False)
                        last = mm(bank(1)[0:n, h * n:(h + 1) * n], r_i[:, cols], sel[:, h, 0:n], False, True)
                    last.then_inc(S("ml_scores"), 1)
                    if c:
                        pe.wait_ge(S("ml_tokc"), c)
                    for h in range(MH):
                        nc.tensor.transpose(bank(2)[0:n, h * P:(h + 1) * P], zm[:, 8 + h, cols], ident)
                    for h in range(MH):
                        last = nc.tensor.transpose(bank(3)[0:n, h * P:(h + 1) * P], zm[:, 4 + h, cols], ident)
                    last.then_inc(S("ml_tok"), 1)
                    pe.wait_ge(S("ml_att"), c + 1)
                    pe.wait_ge(S("ml_tokc"), c + 1)
                    pe.wait_ge(S("ml_qn"), c + 1)
                    if c:
                        pe.wait_ge(S("ml_outc"), c)
                    for h in range(MH):
                        num, den = (bank(b)[:, h * n:(h + 1) * n] for b in (4, 5))
                        mm(num, vaug[0:n, h, 0:P], att[0:n, h, 0:n], True, False)
                        if c < NCH:
                            mm(num, Cst[:, h, 0:P], qh[:, h, cols], False, True)
                        else:
                            if h == 0:
                                pe.wait_ge(S("C_in"), 16)
                            for j in range(8):
                                mm(num[:, 8 * j:8 * j + 8], Cs[:, h, j, 0:P], qh[:, h, c0 + 8 * j:c0 + 8 * j + 8],
                                   False, j == 7)
                        mm(den, ones[0:n, :], att[0:n, h, 0:n], True, False)
                        last = mm(den, ones, qn[:, h, 0:n], False, True)
                    last.then_inc(S("ml_nd"), 1)
                    if c < NCH:
                        for h in range(MH):
                            last = mm(bank(6 + h // 2)[:, 129 * (h % 2):129 * (h % 2) + 129], ktok[:, h, :],
                                      vaug[:, h, :])
                        last.then_inc(S("ml_upd"), 1)
                    else:
                        pe.wait_ge(S("ml_km"), 1)
                        for g in range(11):
                            if g >= 2:
                                pe.wait_ge(S("ml_sst"), g - 1)
                            for e in range(3 * g, min(3 * g + 3, 32)):
                                last = mm(bank(6 + g % 2)[:, 129 * (e - 3 * g):129 * (e - 3 * g) + 129],
                                          Km[:, e // 8, e % 8, :], vaug[0:64, e // 8, :])
                            last.then_inc(S("ml_supd"), 1)
                pe.wait_ge(S("ml_outc"), 5)
                pe.wait_ge(S("ml_sst"), 11)
                for h in range(MH):
                    for a in range(2):
                        last = mm(PP[h][:, a, 0:TH], sel[:, h, :], r_e[:, a * TH:(a + 1) * TH])
                    last.then_inc(S("ml_emt"), 1)
                head_norm("mn", zm[:, 4:8, :], zm[:, 8:12, :], ones)

            def rwkv():
                for p in range(RP):
                    pe.wait_ge(S("rw_kksq"), p + 1)
                    for a in range(2):
                        last = mm(PP[p][:, a, 0:TH], headones, AR[:, p, 1, a * TH:(a + 1) * TH])
                    last.then_inc(S("rw_kkn"), 1)
                pe.wait_ge(S("rw_lora"), 2)
                pe.wait_ge(S("rw_kkmax"), 4)
                for p in range(RP):
                    if p >= 2:
                        pe.wait_ge(S("rw_sig"), 2 * (p - 1))
                    for q, r in ((0, 0), (1, 64)):
                        for a in range(2):
                            last = mm(PP[2 * (p % 2) + q][:, a, 0:TH], lora[r:r + 64, 0, p * P:(p + 1) * P],
                                      zr[r:r + 64, 12, a * TH:(a + 1) * TH])
                    last.then_inc(S("rw_up"), 1)
                pe.wait_ge(S("rw_sig"), 8)

                def rows2():
                    return [(slice(64 * h, 64 * h + 64)) for h in range(2)]

                def scores(c):
                    cols = slice(LR * c, LR * c + LR)
                    for p in range(RP):
                        pe.wait_ge(S("rw_prep"), p + 1)
                        if 4 * c + p >= 2:
                            pe.wait_ge(S("rk_g"), 4 * c + p - 1)
                        b = bank(p % 2)
                        for r in rows2():
                            mm(b[r, 0:128], BK[r, p, 0, cols], AR[r, p, :, cols])
                            mm(b[r, 128:256], BK[r, p, 1, cols], AR[r, p, :, cols])
                            last = mm(b[r, 256:320], AR[r, p, 0, cols], BK[r, p, 0, cols])
                        last.then_inc(S("rk_sc"), 1)

                def tokens(c):
                    cols = slice(LR * c, LR * c + LR)
                    for q in range(2):
                        if 2 * c + q >= 1:
                            pe.wait_ge(S("rk_tokc"), 2 * c + q)
                        for p in (2 * q, 2 * q + 1):
                            for r in rows2():
                                for k, src in enumerate((BK[r, p, 0, cols], BK[r, p, 1, cols], zr[r, 8 + p, cols])):
                                    e = 192 * (p % 2) + 64 * k
                                    last = mm(bank(4)[r, e:e + 64], src, ident[r, r])
                        last.then_inc(S("rk_tok"), 1)

                def level(c, k):
                    top = 5 if c < NCR else 2
                    for q in range(2):
                        if k == 0:
                            pe.wait_ge(S("rk_g"), 4 * c + 2 * q + 2)
                            if c:
                                pe.wait_ge(S(f"rk_lc{q}"), 6 * c)
                        else:
                            pe.wait_ge(S(f"rk_lc{q}"), 6 * c + k)
                        for pp in range(2):
                            p = 2 * q + pp
                            b = PP[1][:, q, 192 * pp:192 * pp + 192]
                            for r in rows2():
                                if k == 0:
                                    mm(b[r, 0:64], Gs[r, c % 2, p, 256:320], Gs[r, c % 2, p, 0:64])
                                    last = mm(b[r, 128:192], Gs[r, c % 2, p, 0:64], Gs[r, c % 2, p, 256:320])
                                    continue
                                v = XPA[r, q, k % 2, pp, :, :]
                                if k < top:
                                    mm(b[r, 0:128], v[:, 2, :], v[:, 0:2, :])
                                    last = mm(b[r, 128:192], v[:, 0, :], v[:, 2, :])
                                else:
                                    last = mm(b[r, 64:128], v[:, 2, :], v[:, 1, :])
                        last.then_inc(S(f"rk_lv{q}"), 1)

                def seq_r1(c):
                    g = c % 2
                    pe.wait_ge(S("rk_tokc"), 2 * c + 2)
                    pe.wait_ge(S("rk_st"), c + 1 if c < NCR else NCR + 1)
                    if c == NCR:
                        pe.wait_ge(S("rS_in"), 16)
                        pe.wait_ge(S("rk_uc"), c)
                        for p in range(RP):
                            for r in rows2():
                                for j in range(8):
                                    e = SEQ + 8 * j
                                    last = mm(bank(5)[r, 64 * p + 8 * j:64 * p + 8 * j + 8], SS[r, p, j, :],
                                              AR[r, p, 0, e:e + 8])
                        last.then_inc(S("rs_qt"), 1)
                        pe.wait_ge(S("rs_qtc"), 1)
                    elif c:
                        pe.wait_ge(S("rk_uc"), c)
                    for p in range(RP):
                        for r in rows2():
                            out = bank(5)[r, 64 * p:64 * p + 64]
                            if c < NCR:
                                mm(out, AR[r, p, 0, LR * c:LR * c + LR], Sr[r, p, :], True, False)
                            else:
                                mm(out, QT[r, p, :], ident[r, r], True, False)
                            last = mm(out, Gs[r, g, p, 128:192], tok[r, g, p, 2, :], False, True)
                    last.then_inc(S("rk_r1"), 1)

                def seq_u(c):
                    pe.wait_ge(S("rk_r1c"), c + 1)
                    for q in range(2):
                        pe.wait_ge(S(f"rk_lc{q}"), 6 * c + (6 if c < NCR else 3))
                    for p in range(RP):
                        for r in rows2():
                            last = mm(bank(5)[r, 256 + 64 * p:320 + 64 * p], PF[r, c % 2, p, :], R1[r, p, :])
                    last.then_inc(S("rk_u"), 1)

                def seq_ys(c):
                    g = c % 2
                    pe.wait_ge(S("rk_uc"), c + 1)
                    if c:
                        pe.wait_ge(S("rk_yc"), c)
                    for p in range(RP):
                        for r in rows2():
                            out = bank(6)[r, 64 * p:64 * p + 64]
                            mm(out, U[r, p, :], Gs[r, g, p, 64:128], True, False)
                            mm(out, tok[r, g, p, 2, :], Gs[r, g, p, 192:256], False, False)
                            if c < NCR:
                                last = mm(out, Sr[r, p, :], AR[r, p, 1, LR * c:LR * c + LR], False, True)
                            else:
                                for j in range(8):
                                    e = SEQ + 8 * j
                                    last = mm(out[:, 8 * j:8 * j + 8], SS[r, p, j, :], AR[r, p, 1, e:e + 8],
                                              False, j == 7)
                    last.then_inc(S("rk_y"), 1)
                    if c < NCR:
                        for p in range(RP):
                            for r in rows2():
                                out = bank(7)[r, 64 * p:64 * p + 64]
                                mm(out, tok[r, g, p, 0, :], U[r, p, :], True, False)
                                last = mm(out, tok[r, g, p, 1, :], tok[r, g, p, 2, :], False, True)
                        last.then_inc(S("rk_s"), 1)
                        return
                    pe.wait_ge(S("rs_uvm"), 1)
                    for p in range(RP):
                        if p >= 2:
                            pe.wait_ge(S("rs_sc"), p - 1)
                        for r in rows2():
                            mm(bank(p % 2)[r, :], tok[r, g, p, 0, :], UVm[r, 0, p, :, :], True, False)
                            last = mm(bank(p % 2)[r, :], tok[r, g, p, 1, :], UVm[r, 1, p, :, :], False, True)
                        last.then_inc(S("rs_s"), 1)

                for c in range(NCR + 1):
                    scores(c)
                    tokens(c)
                    level(c, 0)
                    if c:
                        seq_r1(c - 1)
                    level(c, 1)
                    if c:
                        seq_u(c - 1)
                    level(c, 2)
                    if c:
                        seq_ys(c - 1)
                    if c < NCR:
                        for k in (3, 4, 5):
                            level(c, k)
                seq_r1(NCR)
                seq_u(NCR)
                seq_ys(NCR)
                pe.wait_ge(S("rs_sc"), 4)
                pe.wait_ge(S("rk_yc"), NCR + 1)
                head_norm("rn", yr, AR[:, :, 0, :], headones)
                for p in range(RP):
                    pe.wait_ge(S("hn_std"), HN["rn"] + p + 1)
                    for a in range(2):
                        last = mm(PP[p][:, a, 0:TH], headones, rkp[:, p, a * TH:(a + 1) * TH])
                    last.then_inc(S("rw_bonus"), 1)
                for p in range(RP):
                    pe.wait_ge(S("rw_bonusc"), p + 1)
                    for a in range(2):
                        last = mm(PP[p][:, a, 0:TH], lora[:, 1, p * P:(p + 1) * P], zr[:, 13, a * TH:(a + 1) * TH])
                    last.then_inc(S("rw_gate"), 1)

            pe.wait_ge(S("consts_in"), 16)
            norm(0)
            pe.wait_ge(S("h_lo"), 8)
            pe.wait_ge(S("small_split"), 1)
            for a in range(2):
                h = slice(a * TH, (a + 1) * TH)
                for k in range(KT):
                    last = mm3(PP[2][0:36, a, 0:TH], wif_hi.r[:, k, :], wif_lo.r[:, k, :],
                               H_HI["e_in"][k].r[:, h], hT_r[:, k, h], k == 0, k == KT - 1)
            last.then_inc(S("gates_done"), 1)
            project("e_in")
            mlstm()
            rwkv()
            project("e_out")
            norm(1)
            project("ffn0")
            down(0)
            if do_odd:
                odd_pe(pe, norm, project, head_norm)
                norm(3)
                project("ffn1")
                down(1)
                norm(4)

        @block.scalar
        def _(act):
            A = nc.scalar.activation
            chain = Chain(act, S("act_chain"))

            def norm(n):
                for k in range(KT):
                    if n == 0:
                        act.wait_ge(S("x_in"), 16 * KT)
                    else:
                        act.wait_ge(FREE[k % 2], USE[ADDS[n - 1]] // 2 + k // 2 + 2)
                    if 8 * n + k >= 2:
                        act.wait_ge(S("sq_used"), 8 * n + k - 1)
                    A(sq[:, k % 2, :], xT[:, k, :], ACT.Square).then_inc(S("sq_ready"), 1)
                act.wait_ge(S("sq_used"), 8 * n + 8)
                chain(A(halves(rstd[:, :]), pair(3), ACT.Ln, scale=1.0 / D_MODEL, bias=EPS))
                A(rstd[:, :], rstd[:, :], ACT.Exp, scale=-0.5).then_inc(S("rstd_ready"), 1)

            def split_h(name):
                q = SPLIT[name]
                for k in range(KT):
                    if name[1:] == "_out":
                        act.wait_ge(S("ycat"), (0 if name == "e_out" else 8) + k + 1)
                    else:
                        act.wait_ge(S("h_ready"), 8 * {"e_in": 0, "ffn0": 1, "o_in": 2, "ffn1": 3}[name] + k + 1)
                    A(H_HI[name][k].r, hT[:, k, :], ACT.Copy).then_inc(S("h_hi"), 1)

            def evac(name, j0, n, func, dst, scale=1.0):
                with act.Fori(0, n // 2) as i:
                    for s in range(2):
                        act.wait_ge(S("proj_done"), 2 * i + (USE[name] + j0 + s + 1))
                        out = dst[:, bass.ds(2 * i + s, 1), :].rearrange("p a n -> p (a n)")
                        A(halves(out), pair(s), func, scale=scale).then_inc(FREE[s], 1)

            def to_ext(s, lead):
                e = ext[:, s, :]
                A(e[:, lead:lead + TH], PP[s][:, 0, 0:TH], ACT.Copy)
                A(e[:, lead + TH:lead + SEQ], PP[s][:, 1, 0:SEQ - TH], ACT.Copy)
                samp = e[:, lead + SEQ:lead + SEQ + (8 + lead) * 8].rearrange("p (j n) -> p j n", j=8)
                return A(samp[:, :, lead:lead + 8],
                         PP[s][:, 1, SEQ - TH:TH].rearrange("p (j n) -> p j n", j=8), ACT.Copy)

            def head_norm(nm, src, sqs, n, eps, mean=True):
                for h in range(4):
                    act.wait_ge(S("hn_xc" if mean else "hn_src"), HN[nm] + h + 1)
                    A(sqs[:, h, :], src[:, h, :], ACT.Square).then_inc(S("hn_sq"), 1)
                for h in range(4):
                    act.wait_ge(S("hn_var"), HN[nm] + h + 1)
                    chain(A(halves(sqs[:, h, :]), pair(h), ACT.Ln, scale=1.0 / n, bias=eps))
                    A(sqs[:, h, :], sqs[:, h, :], ACT.Exp, scale=-0.5).then_inc(S("hn_std"), 1)

            def ffn(l):
                base = USE[f"ffn{l}"]
                for first, end in ((0, AHEAD), (AHEAD, FT)):
                    with act.Fori(first, end) as i:
                        for s in range(2):
                            act.wait_ge(S("proj_done"), 2 * i + (base + s + 1))
                            act.wait_ge(S(f"ext_free{s}"), i + (1 + 7 + FT * l))
                            to_ext(s, 2).then_inc(FREE[s], 1)
                        act.wait_ge(S("gate_conv"), i + (1 + FT * l))
                        A(cv[:, 2, :], cv[:, 1, :], ACT.Silu).then_inc(S("silu_done"), 1)
                        if end == AHEAD:
                            act.wait_ge(S("act_ready"), i + (1 + FT * l))
                            src, dst = (v[:, bass.ds(i + o, 1), :].rearrange("p a n -> p (a n)")
                                        for v, o in ((actv, 0), (act_hi.r, KT)))
                            A(dst, src, ACT.Copy).then_inc(S("act_hi"), 1)
                act.wait_ge(S("proj_done"), base + 2 * FT)
                for k in range(AHEAD, FT):
                    act.wait_ge(S("act_ready"), k + 1 + FT * l)
                    A(act_hi.r[:, k - AHEAD, :], actv[:, k, :], ACT.Copy).then_inc(S("act_hi"), 1)

            norm(0)
            split_h("e_in")
            act.wait_ge(S("vec_in"), 16)
            act.wait_ge(S("gates_done"), 1)
            A(halves(r_i), PP[2][0:4, :, 0:TH], ACT.Identity, bias=v_("b_if", rows=4))
            chain(A(halves(r_f), PP[2][32:36, :, 0:TH], ACT.Identity, bias=v_("b_if", rows=4, r0=32)))
            chain(A(r_B, r_f, ACT.Abs))
            chain(A(r_B, r_B, ACT.Exp, scale=-1.0))
            A(r_B, r_B, ACT.Ln, bias=1.0).then_inc(S("ml_softplus"), 1)
            evac("e_in", 0, 4, ACT.Copy, zm[:, 0:4, :])
            evac("e_in", 4, 4, ACT.Copy, zm[:, 4:8, :], MHD ** -0.5)
            evac("e_in", 8, 4, ACT.Copy, zm[:, 8:12, :])
            evac("e_in", 12, 4, ACT.Sigmoid, zm[:, 12:16, :])
            with act.Fori(0, 7) as i:
                for s in range(2):
                    act.wait_ge(S("proj_done"), 2 * i + (16 + s + 1))
                    act.wait_ge(S(f"ext_free{s}"), i + 1)
                    to_ext(s, 1).then_inc(FREE[s], 1)
            act.wait_ge(S("ml_rows"), 1)
            for r in (r_s, r_w, r_dec[:, 0:12]):
                A(r, r, ACT.Exp).then_inc(S("ml_exps"), 1)
            A(r_e, r_m, ACT.Exp, scale=-1.0).then_inc(S("ml_exps"), 1)
            for c in range(NCH + 1):
                n, c0 = (L, L * c) if c < NCH else (NSAMP, SEQ)
                act.wait_ge(S("ml_dm"), c + 1)
                dm = Dm[0:n, :, :].rearrange("p a b -> p (a b)")[:, 0:4 * n]
                A(dm, dm, ACT.Exp).then_inc(S("ml_w"), 1)
                act.wait_ge(S("ml_nd"), c + 1)
                for b, k in ((4, 4), (5, 8)):
                    last = A(zm[:, k:k + 4, c0:c0 + n], bank(b)[:, 0:4 * n].rearrange("p (h n) -> p h n", h=4), ACT.Copy)
                last.then_inc(S("ml_outc"), 1)
            act.wait_ge(S("ml_outc"), NCH + 1)
            for h in range(MH):
                A(zm[:, 8 + h, :], zm[:, 8 + h, :], ACT.Abs).then_inc(S("ml_abs"), 1)
            head_norm("mn", zm[:, 4:8, :], zm[:, 8:12, :], MHD, EPS)
            act.wait_ge(S("shifted"), 14)
            A(zr[0:64, 12, :], zr[0:64, 12, :], ACT.Tanh).then_inc(S("rw_lora"), 1)
            A(zr[:, 13, :], zr[:, 13, :], ACT.Sigmoid).then_inc(S("rw_lora"), 1)
            for p in range(RP):
                act.wait_ge(S("rw_kk"), p + 1)
                A(AR[:, p, 1, :], AR[:, p, 0, :], ACT.Square).then_inc(S("rw_kksq"), 1)
            for p in range(RP):
                act.wait_ge(S("rw_kkmax"), p + 1)
                A(AR[:, p, 1, :], AR[:, p, 1, :], ACT.Sqrt).then_inc(S("rw_kksqrt"), 1)
            for p in range(RP):
                act.wait_ge(S("rw_up"), p + 1)
                if p == 0:
                    act.wait_ge(S("ycat"), 4)
                if p >= 2:
                    act.wait_ge(S("rw_prep"), p - 1)
                for q, b in ((0, "w0"), (1, "a0")):
                    A(halves(prep[:, q, p % 2, :]), pair(2 * (p % 2) + q), ACT.Sigmoid,
                      bias=v_(b, p)).then_inc(S("rw_sig"), 1)
                act.wait_ge(S("rw_cum"), p + 1)
                A(prep[:, 4, p % 2, :], prep[:, 2, p % 2, :], ACT.Exp, scale=-1.0)
                A(prep[:, 2, p % 2, :], prep[:, 2, p % 2, :], ACT.Exp)
                A(prep[:, 3, p % 2, :], prep[:, 3, p % 2, :], ACT.Exp).then_inc(S("rw_exp"), 1)

            def r1_copy(c):
                if c == NCR:
                    act.wait_ge(S("rs_qt"), 1)
                    A(QT, bank(5)[:, 0:256].rearrange("p (a b) -> p a b", a=4), ACT.Copy).then_inc(S("rs_qtc"), 1)
                act.wait_ge(S("rk_r1"), c + 1)
                A(R1, bank(5)[:, 0:256].rearrange("p (a b) -> p a b", a=4), ACT.Copy).then_inc(S("rk_r1c"), 1)

            def u_copy(c):
                act.wait_ge(S("rk_u"), c + 1)
                A(U, bank(5)[:, 256:512].rearrange("p (a b) -> p a b", a=4), ACT.Copy).then_inc(S("rk_uc"), 1)

            def y_copy(c):
                act.wait_ge(S("rk_y"), c + 1)
                A(yr[:, :, LR * c:LR * c + LR], bank(6)[:, 0:256].rearrange("p (a b) -> p a b", a=4),
                  ACT.Copy).then_inc(S("rk_yc"), 1)

            act.wait_ge(S("rw_prep"), 4)
            for c in range(NCR + 1):
                if c >= 2:
                    act.wait_ge(S("rk_s"), c - 1)
                for q in range(2):
                    act.wait_ge(S("rk_tok"), 2 * c + q + 1)
                    A(tok[:, c % 2, 2 * q:2 * q + 2, :, :].rearrange("p a b c -> p (a b c)"), bank(4)[:, 0:384],
                      ACT.Copy).then_inc(S("rk_tokc"), 1)
                if c:
                    r1_copy(c - 1)
                    u_copy(c - 1)
                    y_copy(c - 1)
            r1_copy(NCR)
            u_copy(NCR)
            y_copy(NCR)
            head_norm("rn", yr, AR[:, :, 0, :], RHD, RWKV_EPS)
            split_h("e_out")
            norm(1)
            act.wait_ge(S("out_written"), 16 * 4)
            split_h("ffn0")
            ffn(0)
            if do_odd:
                odd_act(act, A, chain, norm, evac, head_norm, split_h)
                norm(3)
                split_h("ffn1")
                ffn(1)
                norm(4)

        @block.vector
        def _(dve):
            V = nc.vector
            chain = Chain(dve, S("dve_chain"))

            def norm(n, vname, k0, out=None):
                dve.wait_ge(S("rstd_ready"), n + 1)
                for k in range(KT):
                    stt(hT[:, k, :], xT[:, k, :], v_(vname, k0 + k), rstd[:, :], ALU.mult,
                        ALU.mult).then_inc(S("h_ready"), 1)

            def split_h(name):
                for k in range(KT):
                    dve.wait_ge(S("h_hi"), 8 * SPLIT[name] + k + 1)
                    tt(V, hT_r[:, k, :], hT[:, k, :], H_HI[name][k].r, ALU.subtract).then_inc(S("h_lo"), 1)

            def residual(name):
                with dve.Fori(0, 4) as i:
                    for s in range(2):
                        dve.wait_ge(S("proj_done"), 2 * i + (USE[name] + s + 1))
                        x = xT[:, bass.ds(2 * i + s, 1), :].rearrange("p a n -> p (a n)")
                        tt(V, halves(x), pair(s), halves(x), ALU.add).then_inc(FREE[s], 1)

            def head_norm(nm, src, sqs, n, mean=True):
                if mean:
                    for h in range(4):
                        dve.wait_ge(S("hn_mean"), HN[nm] + h + 1)
                        stt(halves(src[:, h, :]), pair(h), -1.0 / n, halves(src[:, h, :]), ALU.mult,
                            ALU.add).then_inc(S("hn_xc"), 1)
                for h in range(4):
                    dve.wait_ge(S("hn_std"), HN[nm] + h + 1)
                    chain(tt(V, src[:, h, :], src[:, h, :], sqs[:, h, :], ALU.mult))

            def conv_pair(l, i):
                base = USE[f"ffn{l}"] // 2
                if True:
                    for s in range(2):
                        dve.wait_ge(FREE[s], i + (base + 2))
                        e = ext[:, s, :]
                        samp = e[:, 2 + SEQ:2 + SEQ + 80].rearrange("p (j n) -> p j n", j=8)
                        par = convp[:, l, :].rearrange("p (t s k) -> p t s k", s=2, k=4)[
                            :, bass.ds(i, 1), s, :].rearrange("p a k -> p (a k)")
                        cin = convin.rearrange("p (t s) k -> p t s k", s=2)[:, bass.ds(i, 1), s, :].rearrange(
                            "p a k -> p (a k)").rearrange("p (j n) -> p j n", j=8)
                        cout = convout.rearrange("p (t s) k -> p t s k", s=2)[:, bass.ds(i, 1), s, :].rearrange(
                            "p a k -> p (a k)")
                        chain(V.tensor_copy(samp[:, :, 0:2], cin))
                        c = cv[:, s, :]
                        cs = c[:, SEQ:T].rearrange("p (j n) -> p j n", j=8)
                        V.tensor_scalar(c[:, 0:SEQ], e[:, 0:SEQ], par[:, 0:1], par[:, 3:4], ALU.mult, ALU.add)
                        chain(V.tensor_scalar(cs, samp[:, :, 0:8], par[:, 0:1], par[:, 3:4], ALU.mult, ALU.add))
                        for k in (1, 2):
                            stt(c[:, 0:SEQ], e[:, k:k + SEQ], par[:, k:k + 1], c[:, 0:SEQ], ALU.mult, ALU.add)
                            ins = stt(cs, samp[:, :, k:k + 8], par[:, k:k + 1], cs, ALU.mult, ALU.add)
                            if k == 1 or s == 0:
                                chain(ins)
                            else:
                                ins.then_inc(S("gate_conv"), 1)
                        V.tensor_copy(cout[:, 0:2], e[:, SEQ:SEQ + 2])
                        V.tensor_copy(cout[:, 2:18].rearrange("p (j n) -> p j n", j=8),
                                      samp[:, :, 8:10]).then_inc(S(f"ext_free{s}"), 1)
                    dve.wait_ge(S("silu_done"), i + (1 + FT * l))
                    out = actv[:, bass.ds(i, 1), :].rearrange("p a n -> p (a n)")
                    tt(V, out, cv[:, 0, :], cv[:, 2, :], ALU.mult).then_inc(S("act_ready"), 1)

            def ffn(l):
                chain(V.memset(ext[:, :, 0:2], 0.0))
                dve.wait_ge(S("convin_in"), 16 * (l + 1))
                for first, end in ((0, AHEAD), (AHEAD, FT)):
                    with dve.Fori(first, end) as i:
                        chain.loop(i, 7, first)
                        conv_pair(l, i)
                        if end == AHEAD:
                            dve.wait_ge(S("act_hi"), i + (1 + FT * l))
                            lo, x, hi = (v[:, bass.ds(i + o, 1), :].rearrange("p a n -> p (a n)")
                                         for v, o in ((act_lo.r, 0), (actv, 0), (act_hi.r, KT)))
                            tt(V, lo, x, hi, ALU.subtract).then_inc(S("act_lo"), 1)
                        chain.end_loop(end - first)
                for k in range(AHEAD, FT):
                    dve.wait_ge(S("act_hi"), k + 1 + FT * l)
                    tt(V, act_lo.r[:, k, :], actv[:, k, :], act_hi.r[:, k - AHEAD, :],
                       ALU.subtract).then_inc(S("act_lo"), 1)

            def mlstm_rows():
                dve.wait_ge(S("ml_softplus"), 1)
                chain(stt(r_f, r_f, 0.0, r_B, ALU.min, ALU.subtract))
                chain(V.tensor_tensor_scan(r_B, c_("scan128", T, 4), r_f, 0.0, ALU.mult, ALU.add))
                dve.wait_ge(S("e_small_in"), 80)
                sf, si = r_a[:, 0:64], r_s[:, 0:64]
                chain(V.tensor_copy(sf, r_f[:, SEQ:T]))
                chain(V.tensor_copy(si, r_i[:, SEQ:T]))
                f8, i8 = (x.rearrange("p (j n) -> p j n", j=8)[:, :, 0] for x in (sf, si))
                chain(tt(V, f8, f8, r_m0[:, 0:8], ALU.add))
                chain(tt(V, i8, i8, f8, ALU.max))
                chain(V.memset(f8, NEG))
                chain(V.tensor_tensor_scan(r_m[:, 0:SEQ], r_f[:, 0:SEQ], r_i[:, 0:SEQ], M_INIT, ALU.add, ALU.max))
                chain(V.tensor_tensor_scan(r_m[:, SEQ:T], sf, si, NEG, ALU.add, ALU.max))
                chain(tt(V, r_i, r_i, r_B, ALU.subtract))
                chain(tt(V, r_a, r_B, r_m, ALU.subtract))
                m_s = r_m[:, SEQ:T].rearrange("p (j n) -> p j n", j=8)[:, :, 7]
                chain(V.memset(r_mp[:, 0:1], M_INIT))
                m_p = r_m[:, 0:SEQ].rearrange("p (c n) -> p c n", n=L)[:, :, L - 1]
                chain(V.tensor_copy(r_mp[:, 1:NCH], m_p[:, 0:NCH - 1]))
                chain(V.tensor_copy(r_mp[:, NCH:NCH + 8], r_m0[:, 0:8]))
                chain(V.tensor_copy(r_rl[:, 0:NCH], r_a[:, 0:SEQ].rearrange("p (c n) -> p c n", n=L)[:, :, L - 1]))
                chain(V.tensor_copy(r_rl[:, NCH:NCH + 8],
                                    r_a[:, SEQ:T].rearrange("p (j n) -> p j n", j=8)[:, :, 7]))
                for dst, src, add in ((r_s, r_a, r_mp), (r_w, r_i, r_rl)):
                    tt(V, dst[:, 0:SEQ].rearrange("p (c n) -> p c n", n=L), src[:, 0:SEQ].rearrange(
                        "p (c n) -> p c n", n=L), bc(add[:, 0:NCH], 2, L), ALU.add)
                    tt(V, dst[:, SEQ:T].rearrange("p (j n) -> p j n", j=8), src[:, SEQ:T].rearrange(
                        "p (j n) -> p j n", j=8), bc(add[:, NCH:NCH + 8], 2, 8), ALU.add)
                tt(V, r_dec[:, 0:12], r_rl[:, 0:12], r_mp[:, 0:12], ALU.add).then_inc(S("ml_rows"), 1)
                V.tensor_copy(r_mo[:, 0:1], r_m[:, SEQ - 1:SEQ])
                V.tensor_copy(r_mo[:, 1:9], m_s).then_inc(S("ml_m_out"), 1)

            def token_shift():
                dve.wait_ge(S("e_small_in"), 80)
                chain(V.memset(ext[:, :, 0:1], 0.0))
                for s in range(2):
                    dve.sem_inc(S(f"ext_free{s}"), 1)
                tmp = sq_tmp
                with dve.Fori(0, 7) as i:
                    chain.loop(i, 4)
                    for s in range(2):
                        dve.wait_ge(FREE[s], i + (8 + 2))
                        e = ext[:, s, :]
                        samp = e[:, 1 + SEQ:1 + SEQ + 72].rearrange("p (j n) -> p j n", j=8)
                        k = 2 * i + s
                        sin = shin[:, bass.ds(k, 1), :].rearrange("p a n -> p (a n)")
                        so = shout[:, bass.ds(k, 1), :].rearrange("p a n -> p (a n)")
                        mu = vec[:, bass.ds(k + VEC["mu"], 1)]
                        z = zr[:, bass.ds(k, 1), :].rearrange("p a n -> p (a n)")
                        chain(V.tensor_copy(samp[:, :, 0], sin))
                        d1 = tmp[:, s, :]
                        tt(V, d1[:, 0:SEQ], e[:, 0:SEQ], e[:, 1:SEQ + 1], ALU.subtract)
                        chain(tt(V, d1[:, SEQ:T].rearrange("p (j n) -> p j n", j=8), samp[:, :, 0:8],
                                 samp[:, :, 1:9], ALU.subtract))
                        stt(z[:, 0:SEQ], d1[:, 0:SEQ], mu, e[:, 1:SEQ + 1], ALU.mult, ALU.add)
                        stt(z[:, SEQ:T].rearrange("p (j n) -> p j n", j=8),
                            d1[:, SEQ:T].rearrange("p (j n) -> p j n", j=8), mu, samp[:, :, 1:9], ALU.mult,
                            ALU.add).then_inc(S("shifted"), 1)
                        V.tensor_copy(so[:, 0:1], e[:, SEQ:SEQ + 1])
                        V.tensor_copy(so[:, 1:9], samp[:, :, 8]).then_inc(S(f"ext_free{s}"), 1)
                    chain.end_loop(7)

            def mlstm():
                for h in range(MH):
                    dve.wait_ge(S("ml_bcast"), h + 1)
                    tt(V, halves(qh[:, h, :]), halves(zm[:, h, :]), pair(h % 2), ALU.mult).then_inc(S("ml_qh"), 1)
                dve.wait_ge(S("ml_qh"), 4)
                dve.wait_ge(S("ml_small"), 1)
                V.tensor_copy(decb.rearrange("p a b -> p (a b)"), bank(4)[:, 0:48])
                V.tensor_copy(wlc[:, 0:NCH, :].rearrange("p a b -> p (a b)"), bank(4)[:, 48:48 + 4 * NCH])
                V.tensor_copy(wlc[0:64, NCH, :], bank(4)[0:64, 48 + 4 * NCH:52 + 4 * NCH])
                V.memset(vaug[:, :, 128:129], 1.0)
                chain(V.memset(Cst, 0.0))
                for c in range(NCH + 1):
                    n, c0 = (L, L * c) if c < NCH else (NSAMP, SEQ)
                    dm, at_ = (x[0:n, :, :].rearrange("p a b -> p (a b)")[:, 0:4 * n].rearrange(
                        "p (h n) -> p h n", h=4) for x in (Dm, att))
                    if c == NCH:
                        at_ = att[0:n, :, 0:n]
                    neg = c_("mneg", 128) if c < NCH else c_("mneg_s", 64, 64)
                    dve.wait_ge(S("ml_scores"), c + 1)
                    tt(V, dm, bank(1)[0:n, 0:4 * n].rearrange("p (h n) -> p h n", h=4), bc(neg, 1, 4),
                       ALU.add).then_inc(S("ml_dm"), 1)
                    q = qh[:, :, c0:c0 + n]
                    if c < NCH:
                        tt(V, qn, q, bc(Cst[:, :, 128], 2, L), ALU.mult).then_inc(S("ml_qn"), 1)
                    else:
                        dve.wait_ge(S("C_in"), 16)
                        tt(V, qn[:, :, 0:n].rearrange("p h (j n) -> p h j n", j=8),
                           q.rearrange("p h (j n) -> p h j n", j=8), bc(Cs[:, :, :, 128], 3, 8),
                           ALU.mult).then_inc(S("ml_qn"), 1)
                    dve.wait_ge(S("ml_w"), c + 1)
                    tt(V, at_, bank(0)[0:n, 0:4 * n].rearrange("p (h n) -> p h n", h=4), dm,
                       ALU.mult).then_inc(S("ml_att"), 1)
                    dve.wait_ge(S("ml_tok"), c + 1)
                    vt = V.tensor_copy(vaug[0:n, :, 0:128], bank(2)[0:n, :].rearrange("p (h n) -> p h n", h=4))
                    kp = bank(3)[0:n, :].rearrange("p (h n) -> p h n", h=4)
                    if c < NCH:
                        tt(V, ktok, kp, bc(wlc[:, c, :], 2, 128), ALU.mult).then_inc(S("ml_tokc"), 1)
                        dve.wait_ge(S("ml_upd"), c + 1)
                        for h in range(MH):
                            last = stt(Cst[:, h, :], Cst[:, h, :], decb[:, h, c:c + 1],
                                       bank(6 + h // 2)[:, 129 * (h % 2):129 * (h % 2) + 129], ALU.mult, ALU.add)
                        last.then_inc(S("ml_state"), 1)
                        dve.wait_ge(S("ml_state"), c + 1)
                    else:
                        vt.then_inc(S("ml_tokc"), 1)
                        chain(tt(V, wlm[0:64], bc(wlc[0:64, c, :], 2, 8), bc(seqmask[0:64, :], 1, 4), ALU.mult))
                        for h in range(MH):
                            last = tt(V, Km[:, h], bc(kp[:, h, :], 1, 8), bc(wlm[0:64, h, :], 2, 128), ALU.mult)
                        last.then_inc(S("ml_km"), 1)
                        dve.wait_ge(S("ml_nd"), NCH + 1)
                        chain(tt(V, Cs, Cs, bc(decb[:, :, NCH:NCH + 8], 3, 129), ALU.mult))
                        for g in range(11):
                            e0, e1 = 3 * g, min(3 * g + 3, 32)
                            dve.wait_ge(S("ml_supd"), g + 1)
                            tt(V, Csf[:, e0:e1, :], Csf[:, e0:e1, :], bank(6 + g % 2)[:, 0:129 * (e1 - e0)].rearrange(
                                "p (a b) -> p a b", b=129), ALU.add).then_inc(S("ml_sst"), 1)
                for h in range(MH):
                    dve.wait_ge(S("ml_abs"), h + 1)
                    dve.wait_ge(S("ml_emt"), h + 1)
                    den = zm[:, 8 + h, :]
                    chain(tt(V, halves(den), halves(den), pair(h), ALU.max))
                    chain(V.reciprocal(den, den))
                    tt(V, zm[:, 4 + h, :], zm[:, 4 + h, :], den, ALU.mult).then_inc(S("hn_src"), 1)
                dve.wait_ge(S("hn_src"), 4)
                head_norm("mn", zm[:, 4:8, :], zm[:, 8:12, :], MHD)
                dve.wait_ge(S("sC_written"), 16)
                for h in range(MH):
                    stt(hT[:, h, :], zm[:, 4 + h, :], v_("ln_m_g", h), zm[:, 12 + h, :], ALU.mult,
                        ALU.mult).then_inc(S("ycat"), 1)

            def rwkv_prep():
                chain(V.tensor_scalar(omka, vec[:, VEC["k_a"]:VEC["k_a"] + 4], -1.0, 1.0, ALU.mult, ALU.add))
                dve.wait_ge(S("ycat"), 4)
                for p in range(RP):
                    V.tensor_scalar(AR[:, p, 0, :], zr[:, 4 + p, :], v_("k_k", p), None,
                                    ALU.mult).then_inc(S("rw_kk"), 1)
                for p in range(RP):
                    dve.wait_ge(S("rw_kkn"), p + 1)
                    V.tensor_scalar(halves(AR[:, p, 1, :]), pair(p), 1e-24, None, ALU.max).then_inc(S("rw_kkmax"), 1)
                for p in range(RP):
                    dve.wait_ge(S("rw_kksqrt"), p + 1)
                    chain(V.reciprocal(AR[:, p, 1, :], AR[:, p, 1, :]))
                    chain(tt(V, AR[:, p, 0, :], AR[:, p, 0, :], AR[:, p, 1, :], ALU.mult))
                for p in range(RP):
                    ld, a, cum, ex, em = (prep[:, k, p % 2, :] for k in range(5))
                    dve.wait_ge(S("rw_sig"), 2 * p + 2)
                    chain(V.tensor_scalar(ld, ld, -float(np.exp(-0.5)), None, ALU.mult))
                    chain(V.tensor_tensor_scan(cum, c_("scan64", T), ld, 0.0, ALU.mult, ALU.add))
                    tt(V, ex, cum, ld, ALU.subtract).then_inc(S("rw_cum"), 1)
                    kk, r, kr = AR[:, p, 0, :], zr[:, p, :], zr[:, 4 + p, :]
                    chain(tt(V, BK[:, p, 0, :], kk, a, ALU.mult))
                    chain(V.tensor_scalar(a, a, v_("k_a", p), omka[:, p:p + 1], ALU.mult, ALU.add))
                    chain(tt(V, a, a, kr, ALU.mult))
                    chain(stt(rkp[:, p, :], r, v_("r_k", p), a, ALU.mult, ALU.mult))
                    dve.wait_ge(S("rw_exp"), p + 1)
                    chain(tt(V, BK[:, p, 0, :], BK[:, p, 0, :], em, ALU.mult))
                    chain(tt(V, BK[:, p, 1, :], a, em, ALU.mult))
                    chain(tt(V, AR[:, p, 1, :], r, cum, ALU.mult))
                    chain(V.tensor_copy(PL[:, p, 0:8], cum[:, 0:SEQ].rearrange("p (c n) -> p c n", n=LR)[:, :, LR - 1]))
                    chain(V.tensor_copy(PL[:, p, 8:16], cum[:, SEQ:T].rearrange("p (c n) -> p c n", n=8)[:, :, 7]))
                    stt(kk, kk, -1.0, ex, ALU.mult, ALU.mult).then_inc(S("rw_prep"), 1)

            def rwkv():
                V.memset(Sr, 0.0).then_inc(S("rk_st"), 1)

                def gate(c):
                    if c >= 2:
                        dve.wait_ge(S("rk_y"), c - 1)
                    m = c_("rk" if c < NCR else "rk_s", 320)
                    for p in range(RP):
                        dve.wait_ge(S("rk_sc"), 4 * c + p + 1)
                        tt(V, Gs[:, c % 2, p, :], bank(p % 2)[:, 0:320], m, ALU.mult).then_inc(S("rk_g"), 1)
                    dve.wait_ge(S("rk_g"), 4 * c + 4)

                def level(c, k):
                    top = 5 if c < NCR else 2
                    for q in range(2):
                        b = PP[1][:, q, 0:384].rearrange("p (a k n) -> p a k n", a=2, k=3)
                        new = XPA[:, q, (k + 1) % 2]
                        dve.wait_ge(S(f"rk_lv{q}"), 6 * c + k + 1)
                        if k == 0:
                            tt(V, new[:, :, 1, :], Gs[:, c % 2, 2 * q:2 * q + 2, 0:64],
                               bc(c_("idpair", 64), 1, 2), ALU.add)
                        else:
                            dst = new[:, :, 1, :] if k < top else PF[:, c % 2, 2 * q:2 * q + 2, :]
                            last = tt(V, dst, XPA[:, q, k % 2, :, 1, :], b[:, :, 1, :], ALU.add)
                        if k < top:
                            last = V.tensor_copy(new[:, :, 0:3:2, :], b[:, :, 0:3:2, :])
                        last.then_inc(S(f"rk_lc{q}"), 1)
                        dve.wait_ge(S(f"rk_lc{q}"), 6 * c + k + 1)

                def state(c):
                    dve.wait_ge(S("rk_s"), c + 1)
                    chain(tt(V, Sr, Sr, bank(7)[:, 0:256].rearrange("p (a b) -> p a b", a=4), ALU.add))
                    tt(V, Sr, Sr, bc(PL[:, :, c], 2, 64), ALU.mult).then_inc(S("rk_st"), 1)
                    dve.wait_ge(S("rk_st"), c + 2)

                for c in range(NCR + 1):
                    gate(c)
                    for k in range(3):
                        level(c, k)
                    if c:
                        state(c - 1)
                    if c < NCR:
                        for k in (3, 4, 5):
                            level(c, k)
                dve.wait_ge(S("rk_uc"), NCR + 1)
                for p in range(RP):
                    tt(V, UVm[:, 0, p], bc(U[:, p, :], 1, 8), bc(seqmask, 2, 64), ALU.mult)
                    last = tt(V, UVm[:, 1, p], bc(tok[:, NCR % 2, p, 2, :], 1, 8), bc(seqmask, 2, 64), ALU.mult)
                last.then_inc(S("rs_uvm"), 1)
                for p in range(RP):
                    dve.wait_ge(S("rs_s"), p + 1)
                    tt(V, SS[:, p], SS[:, p], bank(p % 2).rearrange("p (j n) -> p j n", j=8),
                       ALU.add).then_inc(S("rs_sc"), 1)
                dve.wait_ge(S("rs_sc"), 4)
                tt(V, SS, SS, bc(PL[:, :, 8:16], 3, 64), ALU.mult).then_inc(S("rs_st"), 1)
                dve.wait_ge(S("rk_yc"), NCR + 1)
                dve.sem_inc(S("hn_src"), 4)
                head_norm("rn", yr, AR[:, :, 0, :], RHD)
                for p in range(RP):
                    chain(V.tensor_scalar(yr[:, p, :], yr[:, p, :], v_("ln_r_g", p), v_("ln_r_b", p), ALU.mult,
                                          ALU.add))
                    dve.wait_ge(S("rw_bonus"), p + 1)
                    tt(V, halves(AR[:, p, 0, :]), pair(p), halves(zr[:, 8 + p, :]), ALU.mult).then_inc(
                        S("rw_bonusc"), 1)
                    dve.wait_ge(S("rw_bonusc"), p + 1)
                    chain(tt(V, yr[:, p, :], yr[:, p, :], AR[:, p, 0, :], ALU.add))
                for p in range(RP):
                    dve.wait_ge(S("rw_gate"), p + 1)
                    tt(V, halves(hT[:, 4 + p, :]), halves(yr[:, p, :]), pair(p), ALU.mult).then_inc(S("ycat"), 1)

            sq_tmp = sq
            for s in range(2):
                dve.sem_inc(FREE[s], 1)
            dve.wait_ge(S("vec_in"), 16)
            dve.wait_ge(S("consts_in"), 16)
            dve.wait_ge(S("x_in"), 16 * KT)
            norm(0, "norm_mix", 0)
            split_h("e_in")
            mlstm_rows()
            token_shift()
            mlstm()
            rwkv_prep()
            rwkv()
            split_h("e_out")
            residual("e_out")
            norm(1, "norm_ffn", 0)
            split_h("ffn0")
            ffn(0)
            residual("down0")
            if do_odd:
                odd_dve(dve, V, chain, norm, residual, head_norm, split_h)
                norm(3, "norm_ffn", 8)
                split_h("ffn1")
                ffn(1)
                residual("down1")
                norm(4, "norm_final", 0)


def _tiles(w):
    k, n = w.shape
    return w.reshape(k // P, P, n // P, P).transpose(2, 1, 0, 3).reshape(n // P, P, k)


def _cols(v):
    return v.reshape(-1, P).T


def _pairs(w):
    return w.reshape(w.shape[0], 2, FT, P).transpose(0, 2, 1, 3).reshape(w.shape[0], -1)


def host_arrays(x_prompt, x_sample, state_mlstm_C, state_mlstm_n, state_mlstm_m, state_rwkv_S, state_rwkv_shift,
                state_gla_S, state_s5_re, state_s5_im, state_ffn_conv, norm_mix, norm_ffn, norm_final,
                e_w_in, e_b_if, e_mu, e_w0, e_w_up, e_a0, e_a_up, e_g_up, e_k_k, e_k_a, e_r_k,
                e_ln_m_g, e_ln_r_g, e_ln_r_b, e_w_out, o_w_in, o_a_up, o_a_b, o_ln_g, o_lam_re, o_lam_im,
                o_log_step, o_b_re, o_b_im, o_c_re, o_c_im, o_d, o_w_glu, o_w_out,
                f_w_up, f_conv_w, f_conv_b, f_w_down):
    d = {}
    x = np.concatenate([x_prompt.reshape(SEQ, D_MODEL), x_sample.reshape(NSAMP, D_MODEL)])
    d["x"] = x.T.reshape(KT, P, T).transpose(1, 0, 2)
    d["consts"] = shape_constants()
    w = e_w_in[0]
    m4 = 4 * HALF
    wo = o_w_in[0]
    w_list = [np.concatenate([w[:, :m4], w[:, m4 + 8:]], 1), e_w_out[0], _pairs(f_w_up[0]),
              np.concatenate([wo[:, :1536], wo[:, 1552:]], 1), o_w_out[0], _pairs(f_w_up[1])]
    d["w"] = np.concatenate([_tiles(a) for a in w_list])
    wif = np.zeros((D_MODEL, 36), np.float32)
    wif[:, 0:4], wif[:, 32:36] = w[:, m4:m4 + 4], w[:, m4 + 4:m4 + 8]
    d["w_if"] = wif.reshape(KT, P, 36).transpose(1, 0, 2)
    d["w_down"] = np.concatenate([_tiles(a) for a in f_w_down])
    vec = np.zeros((P, NVEC), np.float32)

    def put(name, v):
        v = _cols(v)
        vec[:, VEC[name]:VEC[name] + v.shape[1]] = v

    for name, v in (("norm_mix", norm_mix.reshape(-1)), ("norm_ffn", norm_ffn.reshape(-1)), ("norm_final", norm_final),
                    ("mu", e_mu[0]), ("w0", e_w0[0]), ("a0", e_a0[0]), ("k_k", e_k_k[0]), ("k_a", e_k_a[0]),
                    ("r_k", e_r_k[0]), ("ln_m_g", e_ln_m_g[0]), ("ln_r_g", e_ln_r_g[0]), ("ln_r_b", e_ln_r_b[0]),
                    ("a_b", o_a_b[0]), ("o_ln_g", o_ln_g[0]), ("o_d", o_d[0])):
        put(name, v)
    vec[0:4, VEC["b_if"]], vec[32:36, VEC["b_if"]] = e_b_if[0, 0:4], e_b_if[0, 4:8]
    vec[0:64, VEC["sgn"]], vec[64:128, VEC["sgn"]] = -1.0, 1.0
    d["vec"] = vec
    cp = np.concatenate([_pairs(f_conv_w[k]).reshape(3, 2 * FT, P) for k in range(2)]).reshape(2, 3, 2 * FT, P)
    cb = _pairs(f_conv_b).reshape(2, 1, 2 * FT, P)
    d["convp"] = np.concatenate([cp, cb], 1).transpose(3, 0, 2, 1).reshape(P, 2, CONVC)
    cs = np.stack([_pairs(state_ffn_conv[k].reshape(16, -1)) for k in range(2)])
    d["conv_state"] = cs.reshape(2, 16, 2 * FT, P).transpose(0, 3, 2, 1)
    d["shift"] = state_rwkv_shift[0].reshape(8, 14, P).transpose(2, 1, 0)
    d["lora"] = np.stack([np.concatenate([e_w_up[0], e_a_up[0]]), e_g_up[0]], 1)
    d["m0"] = state_mlstm_m[0].T
    C = state_mlstm_C[0].transpose(3, 1, 0, 2)
    n = state_mlstm_n[0].transpose(2, 1, 0)[..., None]
    d["C"] = np.concatenate([C, n], 3).reshape(P, 32, 129)
    d["rS"] = state_rwkv_S[0].reshape(8, 4, 2, 64, 64).transpose(2, 4, 1, 0, 3).reshape(P, 4, 8, 64)
    d["w_ad"] = wo[:, 1536:1552].reshape(KT, P, GRANK).transpose(1, 0, 2)
    d["a_up"] = o_a_up[0]
    d["gS"] = state_gla_S[0].reshape(8, 2, 2, GDK, GDV).transpose(2, 3, 1, 0, 4).reshape(P, 2, 8, GDV)
    lam = [np.concatenate([a.T, a.T]) for a in (o_lam_re[0], o_lam_im[0])]
    d["s5_lam"] = np.stack(lam + [np.broadcast_to(o_log_step[0], (P, SG))], 1)
    b = [a[0].transpose(1, 0, 2) for a in (o_b_re, o_b_im)]
    c = [a[0].transpose(2, 0, 1) for a in (o_c_re, o_c_im)]
    d["s5_bc"] = np.stack([np.concatenate(x) for x in (b, b[::-1], c, c[::-1])], 1)
    x0 = [a[0].transpose(2, 1, 0) for a in (state_s5_re, state_s5_im)]
    d["s5_x0"] = np.stack([np.concatenate(x0), np.concatenate(x0[::-1])], 1)
    d["w_glu"] = o_w_glu[0].reshape(4, P, HALF).transpose(1, 0, 2)
    return {k: np.ascontiguousarray(v, dtype=np.float32) for k, v in d.items()}


OUT = {"shift": (P, 14, NSEQ), "m": (4, NSEQ), "pC": (P, 4, 129), "sC": (P, 32, 129), "pS": (P, 4, 64),
       "sS": (P, 4, 8, 64), "conv0": (P, 2 * FT, 18), "y": (P, KT, T),
       "pG": (P, 2, GDV), "sG": (P, 2, 8, GDV), "s5": (P, SG, NSEQ), "conv1": (P, 2 * FT, 18)}


def _tokens(y):
    y = y.transpose(1, 0, 2).reshape(D_MODEL, T).T
    return y[:SEQ].reshape(1, SEQ, D_MODEL), y[SEQ:].reshape(DEC_BATCH, DEC_SEQ, D_MODEL)


def _even_states(r):
    pC, sC = r["pC"], r["sC"].reshape(P, 4, 8, 129)
    sh = r["shift"].transpose(2, 1, 0).reshape(NSEQ, -1)
    m = r["m"].T
    pS = r["pS"].reshape(2, 64, 4, 64).transpose(2, 0, 3, 1).reshape(1, 1, 8, 64, 64)
    sS = r["sS"].reshape(2, 64, 4, 8, 64).transpose(3, 2, 0, 4, 1).reshape(1, 8, 8, 64, 64)
    p = (pC[:, :, :128].transpose(1, 2, 0)[None, None], pC[:, :, 128].T[None, None], m[0][None, None], pS,
         sh[0][None, None])
    s = (sC[:, :, :, :128].transpose(2, 1, 3, 0)[None], sC[:, :, :, 128].transpose(2, 1, 0)[None], m[1:][None], sS,
         sh[1:][None])
    return p, s


def _conv(c):
    return c.reshape(P, FT, 2, NSEQ, 2).transpose(3, 4, 2, 1, 0).reshape(NSEQ, 2, 2 * D_FF)


def kernel(**inputs):
    import concourse.bacc as bacc
    from concourse.bass_utils import run_bass_kernel_spmd as run

    ins = host_arrays(**{k: np.asarray(v) for k, v in inputs.items()})
    nc = bacc.Bacc("TRN2", target_bir_lowering=False, num_devices=1)
    d = {k: nc.dram_tensor(f"in_{k}", v.shape, F32, kind="ExternalInput").ap() for k, v in ins.items()}
    o = {k: nc.dram_tensor(f"out_{k}", v, F32, kind="ExternalOutput").ap() for k, v in OUT.items()}
    program(nc, d, o, 2)
    r = run(nc, [{f"in_{k}": v for k, v in ins.items()}], core_ids=[0]).results[0]
    r = {k: r[f"out_{k}"] for k in OUT}
    p, s = _even_states(r)
    pG = r["pG"].reshape(2, GDK, 2, GDV).transpose(2, 0, 1, 3).reshape(1, 1, GH, GDK, GDV)
    sG = r["sG"].reshape(2, GDK, 2, 8, GDV).transpose(3, 2, 0, 1, 4).reshape(1, 8, GH, GDK, GDV)
    x5 = r["s5"].transpose(2, 1, 0)
    re, im = x5[None, :, :, :SP], x5[None, :, :, SP:]
    conv = np.stack([_conv(r["conv0"]), _conv(r["conv1"])])
    out = (*_tokens(r["y"]), *p, pG, re[:, :1], im[:, :1], conv[:, :1], *s, sG, re[:, 1:], im[:, 1:], conv[:, 1:])
    return tuple(np.ascontiguousarray(a) for a in out)
```

```python
from contextlib import ExitStack

import numpy as np

import concourse.bass as bass
from concourse import mybir
from concourse.alu_op_type import AluOpType as ALU

F32 = mybir.dt.float32
ACT = mybir.ActivationFunctionType
AX = mybir.AxisListType

P = 128
D_MODEL, SEQ, DEC_BATCH, DEC_SEQ = 1024, 512, 8, 8
HALF = D_MODEL // 2
NSAMP = DEC_BATCH * DEC_SEQ
T = SEQ + NSAMP
TH = T // 2
KT = D_MODEL // P
D_FF = ((8 * D_MODEL // 3 + 255) // 256) * 256
FT = D_FF // P
NSEQ = 1 + DEC_BATCH
MH, MHD = 4, 128
RP, RHD = 4, 64
GH, GDK, GDV = 4, 64, 128
L = 128
LR = 64
NCH = SEQ // L
NCR = SEQ // LR
SG, SC, SP = 32, 16, 64
BL = 8
NB = T // BL
NBP = SEQ // BL
GRANK, GLA_TAU = 16, 16.0
EPS = 1e-6
RWKV_EPS = 64e-5
M_INIT = -1e30
NEG = -1e30
TWO_PI = 6.283185307179586
HN = {"mn": 0, "rn": 4, "gn": 8}
ROUND = 12582912.0

E_TILES = 30
O_TILES = 16
ADDS = ("e_out", "down0", "o_out", "down1")
RUNS = {"e_in": (0, E_TILES), "e_out": (30, 8), "ffn0": (38, 2 * FT),
        "o_in": (38 + 2 * FT, O_TILES), "o_out": (54 + 2 * FT, 8), "ffn1": (62 + 2 * FT, 2 * FT)}
W_TILES = 62 + 4 * FT
DCH = ((0, 8), (8, 7), (15, 7))
CHUNK0 = {}
_u = 0
for _name, _n in (("e_in", E_TILES), ("e_out", 8), ("ffn0", 2 * FT), ("down0", 24),
                  ("o_in", O_TILES), ("o_out", 8), ("ffn1", 2 * FT), ("down1", 24)):
    CHUNK0[_name] = _u
    _u += _n
SPLIT = {"e_in": 0, "e_out": 1, "ffn0": 2, "o_in": 3, "o_out": 4, "ffn1": 5}
NEXT = {"e_in": "e_out", "e_out": "ffn0", "ffn0": "down0", "down0": "o_in", "o_in": "o_out", "o_out": "ffn1",
        "ffn1": "down1", "down1": None}
AHEAD = FT - KT
USE = {}
_u = 0
for _name, _n in (("e_in", E_TILES), ("e_out", 8), ("ffn0", 2 * FT), ("down0", 8),
                  ("o_in", O_TILES), ("o_out", 8), ("ffn1", 2 * FT), ("down1", 8)):
    USE[_name] = _u
    _u += _n

VEC = {}
_c = 0
for _name, _n in (("norm_mix", 16), ("norm_ffn", 16), ("norm_final", 8), ("mu", 14), ("w0", 4), ("a0", 4),
                  ("k_k", 4), ("k_a", 4), ("r_k", 4), ("ln_m_g", 4), ("ln_r_g", 4), ("ln_r_b", 4),
                  ("a_b", 2), ("o_ln_g", 4), ("o_d", 4), ("sgn", 1), ("b_if", 1)):
    VEC[_name] = _c
    _c += _n
NVEC = _c
CONVC = 4 * 2 * FT

CONST = {}
_c = 0
GLEV = 8
for _name, _n in (("ident", 128), ("ones", 128), ("headones", 128), ("scan128", T), ("scan64", T),
                  ("mneg", 128), ("mneg_s", 64), ("gla", GLEV * 128), ("gla_s", 4 * 64),
                  ("rk", 5 * 64), ("rk_s", 5 * 64), ("seq", 8), ("idpair", 64), ("sel", 4 * 128),
                  ("col4", 7), ("col8", 14)):
    CONST[_name] = _c
    _c += _n
NCONST = _c


def shape_constants():
    c = np.zeros((P, NCONST), np.float32)

    def put(name, a):
        c[:a.shape[0], CONST[name]:CONST[name] + a.shape[1]] = a

    i = np.arange(P)
    put("ident", np.eye(P))
    put("ones", np.ones((P, P)))
    put("headones", (i[:, None] // 64 == i[None] // 64) * 1.0)
    t = np.arange(T)
    for name, n in (("scan128", L), ("scan64", LR)):
        start = np.where(t < SEQ, t % n == 0, (t - SEQ) % DEC_SEQ == 0)
        put(name, np.broadcast_to(1.0 - start, (P, T)))
    s, tt = i[:, None], i[None]
    put("mneg", np.where(s <= tt, 0.0, NEG))
    s8, t8 = s[:64], tt[:, :64]
    same = s8 // 8 == t8 // 8
    put("mneg_s", np.where(same & (s8 <= t8), 0.0, NEG))
    lev = [((s // (2 * h) == tt // (2 * h)) & (s % (2 * h) < h) & (tt % (2 * h) >= h)) * 1.0
           for h in (64, 32, 16, 8, 4, 2, 1)] + [np.eye(P)]
    put("gla", np.concatenate(lev, 1))
    put("gla_s", np.concatenate([m[:64, :64] for m in lev[4:]], 1))
    s2 = (i % 64)[:, None]
    t2 = np.arange(64)[None]
    for name, ok in (("rk", np.ones((P, 64), bool)), ("rk_s", s2 // 8 == t2 // 8)):
        up, upi, low = (s2 < t2) & ok, (s2 <= t2) & ok, (s2 > t2) & ok
        put(name, np.concatenate([up, upi, up, upi, low], 1) * 1.0)
    put("idpair", (s2 == t2) * 1.0)
    put("seq", (s2 // 8 == np.arange(8)[None]) * 1.0)
    sel = np.zeros((4, 4, 128))
    sel[np.arange(4), np.arange(4)] = 1.0
    put("sel", sel.reshape(4, 512))
    c[64:72, CONST["sel"]:CONST["sel"] + 512] = (i[:8, None] == np.arange(512)[None] // 64) * 1.0
    put("col4", np.broadcast_to(np.arange(7) == 3, (P, 7)) * 1.0)
    put("col8", (np.arange(14)[None] == 6 + i[:, None] // 64) * 1.0)
    return c


class Chain:

    def __init__(self, eng, sem):
        self.eng, self.sem, self.n, self.i, self.per = eng, sem, 0, None, 0

    def __call__(self, ins):
        ins.then_inc(self.sem, 1)
        self.n += 1
        if self.i is None:
            self.eng.wait_ge(self.sem, self.n)
        else:
            self.eng.wait_ge(self.sem, self.i * self.per + self.n)

    def loop(self, i, per, first=0):
        self.i, self.per, self.start = i, per, self.n
        self.n -= per * first
        self.first = first

    def end_loop(self, times):
        assert self.n + self.per * self.first - self.start == self.per, (self.n - self.start, self.per)
        self.n = self.start + self.per * times
        self.i = None


def program(nc, d, o):
    ctx = ExitStack()
    with ctx:
        def sb(name, *shape):
            return ctx.enter_context(nc.sbuf_tensor(name, list(shape), F32))

        def both(name, *shape):
            with nc.sbuf_tensor(name + "_r", list(shape), mybir.dt.float32r) as rounded:
                pass
            return sb(name, *shape), rounded

        def sem(name):
            return ctx.enter_context(nc.semaphore(name))

        class Sems:

            def __init__(self):
                self.made = {}

            def __call__(self, name):
                if name not in self.made:
                    self.made[name] = sem(name)
                return self.made[name]

        S = Sems()

        xT = sb("xT", P, KT, T)
        hT, hT_r = both("hT", P, KT, T)
        w_ring = sb("w_ring", P, 2, KT * P)
        dual, dual_r = both("dual", P, 5632)
        cst = sb("cst", P, NCONST)
        vec = sb("vec", P, NVEC)
        convp = sb("convp", P, 2, CONVC)
        ext = sb("ext", P, 2, 2 + SEQ + 10 * DEC_BATCH)
        rstd = sb("rstd", P, T)
        sq = sb("sq", P, 2, T)
        NA = 28632
        R_EARLY, R_LATE = (0, FT * T), (15896, FT * T)
        with nc.sbuf_tensor("arena_r0", [P, R_EARLY[1]], mybir.dt.float32r) as arena_r0:
            with nc.sbuf_tensor("gap", [P, R_LATE[0] - R_EARLY[1]], F32):
                with nc.sbuf_tensor("arena_r1", [P, R_LATE[1]], mybir.dt.float32r) as arena_r1:
                    pass
        arena = sb("arena", P, NA)
        PP = [ctx.enter_context(nc.psum_tensor(f"PP{i}", [P, 2, 512], F32)) for i in range(4)]

        def bank(b, n=512):
            return PP[b // 2][:, b % 2, 0:n]

        def pair(i):
            return PP[i][:, :, 0:TH]

        def at(off, *shape, mem=None):
            n = int(np.prod(shape))
            assert off + n <= NA, (off, n)
            v = (arena if mem is None else mem)[:, off:off + n]
            if len(shape) == 1:
                return v
            names = [f"a{i}" for i in range(len(shape))]
            return v.rearrange(f"p ({' '.join(names)}) -> p {' '.join(names)}", **dict(zip(names[1:], shape[1:])))

        def halves(v):
            return v.rearrange("p (a n) -> p a n", a=2)

        def c_(name, n, rows=P, r0=0):
            return cst[r0:r0 + rows, CONST[name]:CONST[name] + n]

        def v_(name, k=0, rows=P, r0=0):
            return vec[r0:r0 + rows, VEC[name] + k:VEC[name] + k + 1]

        ident, ones, headones = c_("ident", 128), c_("ones", 128), c_("headones", 128)
        sel = c_("sel", 512, 4).rearrange("p (h n) -> p h n", h=4)
        seqmask = c_("seq", 8)
        headrow = c_("sel", 512, 8, 64).rearrange("p (h n) -> p h n", h=4)

        def col4(h, n):
            return cst[0:n, CONST["col4"] + 3 - h:CONST["col4"] + 7 - h]

        def col8(p):
            return cst[:, CONST["col8"] + 6 - 2 * p:CONST["col8"] + 14 - 2 * p]

        def tt(eng, out, a, b, op):
            return eng.tensor_tensor(out, a, b, op)

        def stt(out, a, s, b, op0, op1):
            return nc.vector.scalar_tensor_tensor(out=out, in0=a, scalar=s, in1=b, op0=op0, op1=op1)

        def bc(v, axis, n):
            v = v.unsqueeze(axis)
            shape = list(v.shape)
            shape[axis] = n
            return v.to_broadcast(shape)

        def mm(out, lhsT, rhs, start=True, stop=True):
            return nc.tensor.matmul(out, lhsT, rhs, start=start, stop=stop)

        def mm3(out, w, w_low, x, x_low, start, stop):
            mm(out, w, x, start, False)
            mm(out, w, x_low, False, False)
            return mm(out, w_low, x, False, stop)

        zm = at(0, 16, T)
        zr = at(9216, 14, T)
        W0 = 9216 + 14 * T
        lora = at(W0, 2, 512)
        wif = at(W0 + 1024, KT, 36)
        shin = at(W0 + 1312, 14, DEC_BATCH)
        shout = at(W0 + 1424, 14, NSEQ)
        W1 = W0 + 1552
        rows = at(W1, 8, T)
        r_f, r_i, r_B, r_m, r_a, r_s, r_w, r_e = (rows[0:4, k, :] for k in range(8))
        W2 = W1 + 8 * T
        qh = at(W2, 4, T)
        W3 = W2 + 4 * T
        sqf = sq[:, :, :].rearrange("p a b -> p (a b)")
        qn = sqf[:, 0:512].rearrange("p (h n) -> p h n", h=4)
        att = sqf[:, 512:1024].rearrange("p (h n) -> p h n", h=4)
        Dm = at(W3, 4, L)
        vaug = at(W3 + 512, 4, 129)
        ktok = at(W3 + 1028, 4, L)
        PL = at(W3 + 1540, 4, 16)
        omka = at(W3 + 1604, 4)
        W4 = W3 + 1612
        Cst = at(W4 + 160, 4, 129)
        wlc = at(W4, 5, 4)
        decb = at(W4 + 20, 4, 12)
        rsm = at(W4 + 68, 5, 12)
        wlm = at(W4 + 128, 4, 8)
        r_mp, r_rl, r_dec, r_m0, r_mo = (rsm[0:4, k, :] for k in range(5))
        Cs = hT[:, :, :].rearrange("p a b -> p (a b)")[:, 0:4128].rearrange("p (h j n) -> p h j n", h=4, j=8)
        Csf = hT[:, :, :].rearrange("p a b -> p (a b)")[:, 0:4128].rearrange("p (g n) -> p g n", n=129)
        dring = dual[:, :]

        DUAL, ARENA = 0, 1

        def on(where, off, *shape):
            if where == DUAL:
                return at(off, *shape, mem=dual_r)
            r, base = (arena_r0, R_EARLY[0]) if off < R_LATE[0] else (arena_r1, R_LATE[0])
            assert off - base + int(np.prod(shape)) <= R_LATE[1]
            return at(off - base, *shape, mem=r)

        w_hi, w_lo = (on(DUAL, o, 2, KT * P) for o in (0, 2 * KT * P))
        wif_hi = on(DUAL, 5248, KT, 36)
        wif_lo = on(ARENA, W2 + 6 * T, KT, 36)
        wad_hi, wad_lo = (on(DUAL, 5248 + KT * GRANK * k, KT, GRANK) for k in range(2))
        H_HI = {"e_in": [on(ARENA, W2 + T * k, T) for k in range(6)] + [on(DUAL, 4096 + T * k, T)
                                                                      for k in range(2)]}
        for name_, off in (("e_out", 4608), ("ffn0", 15896), ("o_in", 22848), ("o_out", 4608), ("ffn1", 15896)):
            H_HI[name_] = [on(ARENA, off + T * k, T) for k in range(KT)]
        Km = dring[0:64, 0:4096].rearrange("p (h j n) -> p h j n", h=4, j=8)

        BONUS_PAIR = (1, 2, 3, 1)
        kkrow = sqf[64:72, 0:T]
        AR = at(0, 4, 2, T)
        BK = at(4608, 4, 2, T)
        rkp = at(W1, 4, T)
        yr = at(W1 + 2304, 4, T)
        X0 = W1 + 4608
        prep = at(W1 + 2304, 5, 2, T)
        XPA = at(X0, 2, 2, 2, 3, 64)
        PF = at(X0 + 1536, 2, 4, 64)
        tok = at(X0 + 2048, 2, 4, 3, 64)
        R1 = sqf[:, 0:256].rearrange("p (a b) -> p a b", a=4)
        U = sqf[:, 256:512].rearrange("p (a b) -> p a b", a=4)
        Sr = at(W4 + 932, 4, 64)
        QT = at(W4 + 676, 4, 64)
        Gs = at(9216, 2, 4, 320)
        SS = at(9216 + 2560, 4, 8, 64)
        UVm = dring[:, 0:4096].rearrange("p (a q j n) -> p a q j n", a=2, q=4, j=8)

        actv = at(0, FT, T)
        cv = at(12672, 3, T)
        convin = at(14400, 2 * FT, 16)
        convout = at(15104, 2 * FT, 18)
        act_lo = on(ARENA, 0, FT, T)
        act_hi = on(ARENA, 15896, FT, T)

        block = ctx.enter_context(nc.Block())

        WL = [S("w_landed0"), S("w_landed1")]
        FREE = [S("psum_free0"), S("psum_free1")]

        def all_free(eng, name, n):
            for s in range(2):
                eng.wait_ge(FREE[s], (USE[name] + n) // 2 + 1)

        zo = at(0, 16, T)
        adown = at(9216, T)[0:GRANK]
        aup = at(9792, 256)[0:GRANK]
        wad = at(10048, KT, GRANK)
        LA = at(10176, 2, T)
        BC = at(11328, 2, T)
        QG = at(12480, 2, T)
        KG = at(13632, 2, T)
        XL = at(14784, 2, 7, T)
        attg = at(22848, 4, 128)
        attw = at(23360, 2, 1024)
        vt = at(25408, 4, 128)
        kgt = at(25920, 2, 128)
        Sg = at(26176, 2, 128)
        ebl = at(28608, 2, 12)
        E1 = at(27456, 2, T)
        hflat = hT[:, :, :].rearrange("p a b -> p (a b)")
        SSg = hflat[:, 0:2048].rearrange("p (t j n) -> p t j n", t=2, j=8)
        Vm = at(18752, 4096)[0:64].rearrange("p (h j n) -> p h j n", h=4, j=8)
        Gy = dual[:, 0:SG * (BL + 1) * SC].rearrange("p (g k c) -> p g k c", g=SG, k=BL + 1)
        Ub = at(4608, SG, NB)
        FZT = at(9216, SG, P)
        Mt = at(13312, SG, P)
        FZ = at(17408, SG, BL, SC)
        Yb = at(17408, SG, NB)
        Y_GROUPS = [(g, min(g + 7, SG)) for g in range(0, SG, 7)]
        Y_BANKS = (0, 1, 2, 3, 6)
        Yf = at(19712, 4, BL, NB)
        ZZ = at(21504, 2, SG, NB)
        Kb = at(21504, SG, P)[0:SC]
        fsw = at(21504, 2, SG, SC)
        gsw = at(11264, 2, SG, SC)
        ft = at(23552, SG, SC)
        gt = at(27456, SG, SC)
        XX = at(26112, SG, NB + 1)
        BC4 = at(9216, 4, SG, SC)
        up = hflat[:, 2048:2048 + 4 * T].rearrange("p (a s b) -> p a s b", a=4, s=BL)
        wglu = at(9216, 4, HALF)
        LAX = at(14784, 4, T)
        Yf_tok = at(0, 4, T)
        sgl = at(2304, 4, T)
        x0st, x0sw = (dring[:, o_:o_ + 256].rearrange("p (g j) -> p g j", g=SG) for o_ in (4608, 4864))
        SO = dring[:, 5120:5408].rearrange("p (g j) -> p g j", g=SG)
        st1, st2 = (at(2304 + 256 * k, SG, DEC_BATCH) for k in range(2))
        tab = sqf[:, 0:768].rearrange("p (k g) -> p k g", g=SG)
        UC, US = (at(17408 + 2048 * k, SG, NBP) for k in range(2))
        TA = XX[:, :, 0:NBP]
        TB = hflat[:, 4 * T:4 * T + SG * NBP].rearrange("p (g b) -> p g b", g=SG)
        (l_re, l_im, l_st, t_a, t_b, t_er, t_s, t_c, t_n, lr, li, lis, wr, wi, wis, t_d,
         lr8, li8) = (tab[:, k, :] for k in range(18))
        lis8 = tab[:, 18, :]
        t_e, t_f = tab[:, 20, :], tab[:, 21, :]
        u_scr = nc.dram_tensor("u_scratch", (4 * P, BL, NB), F32, kind="Internal").ap()
        y_scr = nc.dram_tensor("y_scratch", (4 * P, BL, NB), F32, kind="Internal").ap()

        def odd_sp(sp, stream, out):
            sp.wait_ge(S("proj_done"), USE["down0"] + 8)
            sp.dma_start(wad, d["w_ad"]).then_inc(S("o_small_in"), 16)
            sp.dma_start(aup, d["a_up"]).then_inc(S("o_small_in"), 16)
            sp.wait_ge(S("h_lo"), 32)
            sp.dma_start(tab[:, 0:3, :], d["s5_lam"]).then_inc(S("s5_lam_in"), 16)
            stream("o_in")
            sp.wait_ge(S("gl_x"), 14)
            sp.wait_ge(S("gl_qk"), 2)
            sp.dma_start(BC4, d["s5_bc"]).then_inc(S("s5_bx_in"), 16)
            for k, x in enumerate((x0st, x0sw)):
                sp.dma_start(x, d["s5_x0"][:, k]).then_inc(S("s5_bx_in"), 16)
            sp.wait_ge(S("proj_done"), USE["o_in"] + O_TILES)
            sp.dma_start(SSg, d["gS"]).then_inc(S("gS_in"), 16)
            sp.wait_ge(S("s5_up"), 1)
            sp.dma_start(u_scr.rearrange("(a p) s b -> p a (s b)", p=P),
                         up.rearrange("p a s b -> p a (s b)")).then_inc(S("u_scratched"), 16)
            sp.wait_ge(S("gl_st"), NCH + 1)
            out("pG", Sg)
            sp.wait_ge(S("gs_st"), 2)
            sp.dma_start(o["sG"], SSg).then_inc(S("sG_written"), 16)
            sp.wait_ge(S("out_written"), 16 * 6)
            sp.wait_ge(S("u_scratched"), 16)
            sp.wait_ge(S("ycat"), 12)
            uv = u_scr.rearrange("(g c) s b -> s c g b", c=SC)
            for s in range(BL):
                sp.dma_start(Ub[SC * s:SC * s + SC], uv[s]).then_inc(S("U_in"), 16)
            sp.wait_ge(S("s5_g"), 2)
            sp.wait_ge(S("s5_kc"), 8)
            for s in range(BL):
                sp.dma_start(Mt[SC * s:SC * s + SC, :, SC * s:P], Kb[:, :, 0:P - SC * s]).then_inc(S("M_in"), 16)
            sp.wait_ge(S("s5_zc"), 8)
            sp.dma_start(wglu, d["w_glu"]).then_inc(S("glu_in"), 16)
            for r in range(2):
                sp.dma_start(ZZ[64 * r:64 * r + 64, 1], ZZ[64 - 64 * r:128 - 64 * r, 0]).then_inc(S("zsw_in"), 16)
            sp.wait_ge(S("s5_yc"), len(Y_BANKS))
            yv = y_scr.rearrange("(g c) t b -> t c g b", c=SC)
            for t in range(BL):
                sp.dma_start(yv[t], Yb[SC * t:SC * t + SC]).then_inc(S("y_scratched"), 16)
            sp.wait_ge(S("y_scratched"), 16 * BL)
            sp.dma_start(Yf.rearrange("p a s b -> p a (s b)"),
                         y_scr.rearrange("(a p) s b -> p a (s b)", p=P)).then_inc(S("Y_in"), 16)
            sp.wait_ge(S("s5_scan"), 1)
            out("s5", SO)
            stream("o_out")
            sp.wait_ge(S("proj_done"), USE["ffn1"])
            sp.wait_ge(S("out_written"), 16 * 7)
            sp.dma_start(convin, d["conv_state"][1]).then_inc(S("convin_in"), 16)
            stream("ffn1")
            stream("down1")
            for s in range(2):
                sp.wait_ge(S(f"ext_free{s}"), 1 + 7 + 2 * FT)
            out("conv1", convout)
            sp.wait_ge(S("h_ready"), 40)
            out("y", hT[:])

        FSPLIT = 11

        def input_matrices(E, chain, cs, tmp, done, k0, k1):
            n, tmp = cs.stop - cs.start, tmp[:, :, cs]
            for k in range(k0, k1):
                s = BL - 1 - k
                new, nsw = FZ[:, :, s, cs], fsw[:, k % 2, :, cs]
                if k == 0:
                    x, sw, r, i = BC4[:, 0, :, cs], BC4[:, 1, :, cs], wr, wis
                else:
                    x, sw, r, i = FZ[:, :, s + 1, cs], fsw[:, (k + 1) % 2, :, cs], lr, lis
                r, i = bc(r, 2, n), bc(i, 2, n)
                tt(E, new, x, r, ALU.mult)
                chain(tt(E, tmp, sw, i, ALU.mult))
                last = tt(E, new, new, tmp, ALU.add)
                if k == BL - 1:
                    last.then_inc(done, 1)
                    return
                chain(last)
                tt(E, nsw, sw, r, ALU.mult)
                chain(tt(E, tmp, x, i, ALU.mult))
                chain(tt(E, nsw, nsw, tmp, ALU.subtract))

        def output_matrices(E, chain, cs, done):
            n = cs.stop - cs.start
            tmp = gt[:, :, cs]
            chain(E.tensor_scalar(Gy[:, :, 0, cs], BC4[:, 2, :, cs], v_("sgn"), -1.0, ALU.mult, ALU.mult))
            chain(E.tensor_scalar(gsw[:, 0, :, cs], BC4[:, 3, :, cs], v_("sgn"), None, ALU.mult))
            r, i = bc(lr, 2, n), bc(lis, 2, n)
            for k in range(BL):
                g, new = Gy[:, :, k, cs], Gy[:, :, k + 1, cs]
                sw, nsw = gsw[:, k % 2, :, cs], gsw[:, (k + 1) % 2, :, cs]
                tt(E, new, g, r, ALU.mult)
                chain(tt(E, tmp, sw, i, ALU.mult))
                last = tt(E, new, new, tmp, ALU.subtract)
                if k == BL - 1:
                    last.then_inc(done, 1)
                    return
                chain(last)
                chain(tt(E, nsw, sw, r, ALU.mult))
                chain(tt(E, tmp, g, i, ALU.mult))
                chain(tt(E, nsw, nsw, tmp, ALU.add))

        def odd_pool(pool, chain):
            pool.wait_ge(S("s5_lam"), 1)
            pool.wait_ge(S("s5_bx_in"), 48)
            pool.wait_ge(S("proj_done"), USE["o_in"] + O_TILES)
            output_matrices(nc.gpsimd, chain, slice(0, SC), S("s5_g"))
            pool.wait_ge(S("s5_g"), 1)
            pool.wait_ge(S("gs_st"), 2)
            input_matrices(nc.gpsimd, chain, slice(FSPLIT, SC), gt, S("s5_f"), 0, BL)
            pool.wait_ge(S("ycat"), 12)
            nc.gpsimd.memset(Mt.rearrange("p a b -> p (a b)"), 0.0).then_inc(S("s5_g"), 1)

        def odd_pe(pe, norm, project, head_norm):
            norm(2)
            pe.wait_ge(S("h_lo"), 32)
            pe.wait_ge(S("small_split"), 2)
            for a in range(2):
                h = slice(a * TH, (a + 1) * TH)
                for k in range(KT):
                    last = mm3(PP[2][0:GRANK, a, 0:TH], wad_hi[:, k, :], wad_lo[:, k, :],
                               H_HI["o_in"][k][:, h], hT_r[:, k, h], k == 0, k == KT - 1)
            last.then_inc(S("gates_done"), 1)
            pe.wait_ge(S("ad_copied"), 1)
            for t in range(2):
                for a in range(2):
                    last = mm(PP[2 + t][:, a, 0:TH], aup[:, t * P:(t + 1) * P], adown[:, a * TH:(a + 1) * TH])
                last.then_inc(S("gl_up"), 1)
            project("o_in")
            pe.wait_ge(S("gl_qk"), 2)
            pe.wait_ge(S("gl_x"), 14)
            all_free(pe, "o_in", O_TILES)
            for c in range(NCH + 1):
                n, c0 = (L, L * c) if c < NCH else (NSAMP, SEQ)
                cols = slice(c0, c0 + n)
                if c:
                    pe.wait_ge(S("gl_tokc"), c)
                    pe.wait_ge(S("gl_st"), c + 1)
                for h in range(GH):
                    nc.tensor.transpose(bank(4)[0:n, h * P:(h + 1) * P], zo[:, 4 + h, cols], ident)
                for t in range(2):
                    last = nc.tensor.transpose(bank(5)[0:n, t * P:(t + 1) * P], KG[:, t, cols], ident)
                last.then_inc(S("gl_tok"), 1)
                for h in range(GH):
                    t, r = h // 2, slice(64 * (h % 2), 64 * (h % 2) + 64)
                    if 4 * c + h >= 2:
                        pe.wait_ge(S("gl_am"), 4 * c + h - 1)
                    lev = range(8) if c < NCH else range(4, 8)
                    for e, v in enumerate(lev):
                        out = PP[h % 2][0:n, (e * n) // 512, (e * n) % 512:(e * n) % 512 + n]
                        lhs, rhs = ((XL[r, t, v, cols], XL[r, t, v, cols]) if v < 7
                                    else (zo[r, 2 + t, cols], zo[r, t, cols]))
                        last = mm(out, lhs, rhs)
                    last.then_inc(S("gl_sc"), 1)
                pe.wait_ge(S("gl_tokc"), c + 1)
                pe.wait_ge(S("gl_st"), c + 1)
                if c == NCH:
                    pe.wait_ge(S("gS_in"), 16)
                if c:
                    pe.wait_ge(S("gl_oc"), c)
                for h in range(GH):
                    t, r = h // 2, slice(64 * (h % 2), 64 * (h % 2) + 64)
                    out = bank(6 + h % 2)[:, t * n:(t + 1) * n]
                    pe.wait_ge(S("gl_at"), 4 * c + h + 1)
                    mm(out, vt[:, h, :], attg[:, h, 0:n], True, False)
                    if c < NCH:
                        last = mm(out, Sg[r, t, :], QG[r, t, cols], False, True)
                    else:
                        for j in range(8):
                            last = mm(out[:, 8 * j:8 * j + 8], SSg[r, t, j, :], QG[r, t, c0 + 8 * j:c0 + 8 * j + 8],
                                      False, j == 7)
                last.then_inc(S("gl_o"), 1)
                if c < NCH:
                    for h in range(GH):
                        t, r = h // 2, slice(64 * (h % 2), 64 * (h % 2) + 64)
                        last = mm(bank(5)[r, 256 + t * P:256 + (t + 1) * P], kgt[0:n, t, r], vt[0:n, h, :])
                    last.then_inc(S("gl_s"), 1)
                else:
                    pe.wait_ge(S("gs_vm"), 1)
                    pe.wait_ge(S("gl_am"), 20)
                    for t in range(2):
                        for h in (2 * t, 2 * t + 1):
                            r = slice(64 * (h % 2), 64 * (h % 2) + 64)
                            for a in range(2):
                                last = mm(PP[t][r, a, :], kgt[0:n, t, r], Vm[:, h, 4 * a:4 * a + 4, :])
                        last.then_inc(S("gs_s"), 1)
            pe.wait_ge(S("gs_st"), 2)
            head_norm("gn", zo[:, 0:4, :], LAX, ones, mean=False)

            pe.wait_ge(S("ycat"), 12)
            pe.wait_ge(S("s5_f"), 2)
            for b in range(8):
                if b >= 2:
                    pe.wait_ge(S("s5_ftc"), b - 1)
                for e in range(4):
                    last = nc.tensor.transpose(bank(b % 2)[:, e * P:(e + 1) * P],
                                               FZ[:, 4 * b + e, :, :].rearrange("p s c -> p (s c)"), ident)
                last.then_inc(S("s5_ft"), 1)
            pe.wait_ge(S("s5_g"), 1)
            for b in range(8):
                if b >= 2:
                    pe.wait_ge(S("s5_kc"), b - 1)
                for e in range(4):
                    g = 4 * b + e
                    last = mm(bank(2 + b % 2)[0:SC, e * P:(e + 1) * P], FZ[:, g, BL - 1, :],
                              Gy[:, g, 0:BL, :].rearrange("p s c -> p (s c)"))
                last.then_inc(S("s5_k"), 1)
            pe.wait_ge(S("U_in"), 16 * BL)
            pe.wait_ge(S("s5_ftc"), 8)
            for b in range(8):
                if b >= 2:
                    pe.wait_ge(S("s5_zc"), b - 1)
                for e in range(4):
                    last = mm(bank(4 + b % 2)[:, e * NB:(e + 1) * NB], FZT[:, 4 * b + e, :], Ub[:, 4 * b + e, :])
                last.then_inc(S("s5_z"), 1)
            pe.wait_ge(S("M_in"), 16 * BL)
            pe.wait_ge(S("s5_kc"), 8)
            for own in (True, False):
                if not own:
                    pe.wait_ge(S("s5_scan"), 2)
                for b, (g0, g1) in zip(Y_BANKS, Y_GROUPS):
                    for g in range(g0, g1):
                        out = bank(b)[:, (g - g0) * NB:(g - g0 + 1) * NB]
                        if own:
                            mm(out, Mt[:, g, :], Ub[:, g, :], g == g0, False)
                        else:
                            last = mm(out, Gy[:, g, 1:BL + 1, :].rearrange("p s c -> p (s c)"), XX[:, g, 0:NB],
                                      False, g == g1 - 1)
                    if not own:
                        last.then_inc(S("s5_y"), 1)
            pe.wait_ge(S("s5_gelu"), 4)
            pe.wait_ge(S("glu_in"), 16)
            for m in range(4):
                for a in range(2):
                    for k in range(4):
                        last = mm(PP[m][:, a, 0:TH], wglu[:, k, m * P:(m + 1) * P], Yf_tok[:, k, a * TH:(a + 1) * TH],
                                  k == 0, k == 3)
                last.then_inc(S("s5_glu"), 1)
            project("o_out")

        def odd_act(act, A, chain, norm, evac, head_norm, split_h):
            norm(2)
            split_h("o_in")
            act.wait_ge(S("gates_done"), 2)
            A(halves(adown), PP[2][0:GRANK, :, 0:TH], ACT.Copy).then_inc(S("ad_copied"), 1)
            for t in range(2):
                act.wait_ge(S("gl_up"), t + 1)
                chain(A(halves(LA[:, t, :]), pair(2 + t), ACT.Identity, bias=v_("a_b", t)))
                chain(A(BC[:, t, :], LA[:, t, :], ACT.Abs))
            for t in range(2):
                chain(A(BC[:, t, :], BC[:, t, :], ACT.Exp, scale=-1.0))
                A(BC[:, t, :], BC[:, t, :], ACT.Ln, bias=1.0).then_inc(S("gl_sp"), 1)
            evac("o_in", 0, 2, ACT.Copy, zo[:, 0:2, :], GDK ** -0.5)
            evac("o_in", 2, 2, ACT.Copy, zo[:, 2:4, :])
            for t in range(2):
                act.wait_ge(S("gl_kd"), t + 1)
                A(E1[:, t, :], BC[:, t, :], ACT.Exp)
                A(KG[:, t, :], KG[:, t, :], ACT.Exp).then_inc(S("gl_e1"), 1)

            def level_exps(k0, k1):
                for k in range(k0, k1):
                    t, v = k // 7, k % 7
                    n = SEQ if v < 4 else T
                    act.wait_ge(S("gl_d"), k + 1)
                    A(XL[:, t, v, 0:n], XL[:, t, v, 0:n], ACT.Exp).then_inc(S("gl_e"), 1)

            act.wait_ge(S("s5_lam_in"), 16)
            A(t_s, l_st, ACT.Exp).then_inc(S("s5_trig"), 1)
            level_exps(0, 3)
            for j in (4, 6):
                evac("o_in", j, 2, ACT.Copy, zo[:, j:j + 2, :])
                level_exps(j - 1, j + 1)
            act.wait_ge(S("s5_ab"), 1)
            A(t_er, t_a, ACT.Exp)
            A(t_s, t_s, ACT.Sin)
            A(t_c, t_c, ACT.Sin).then_inc(S("s5_trig"), 1)
            evac("o_in", 8, 4, ACT.Silu, zo[:, 8:12, :])
            level_exps(7, 10)
            for j in (12, 14):
                evac("o_in", j, 2, ACT.Copy, zo[:, j:j + 2, :])
                level_exps(j - 2, j)
            for c in range(NCH + 1):
                n, c0 = (L, L * c) if c < NCH else (NSAMP, SEQ)
                act.wait_ge(S("gl_tok"), c + 1)
                A(vt[0:n].rearrange("p a b -> p (a b)"), bank(4)[0:n, :], ACT.Copy)
                A(kgt[0:n].rearrange("p a b -> p (a b)"), bank(5)[0:n, 0:256], ACT.Copy).then_inc(S("gl_tokc"), 1)
                act.wait_ge(S("gl_o"), c + 1)
                for a in range(2):
                    last = A(zo[:, a:4:2, c0:c0 + n], bank(6 + a)[:, 0:2 * n].rearrange("p (h n) -> p h n", h=2),
                             ACT.Copy)
                last.then_inc(S("gl_oc"), 1)
            act.wait_ge(S("gl_oc"), NCH + 1)
            for h in range(4):
                act.sem_inc(S("hn_src"), 1)
            head_norm("gn", zo[:, 0:4, :], LAX, GDV, EPS, mean=False)

            act.wait_ge(S("s5_g"), 1)
            for b in range(8):
                act.wait_ge(S("s5_ft"), b + 1)
                A(FZT[:, 4 * b:4 * b + 4, :].rearrange("p a b -> p (a b)"), bank(b % 2), ACT.Copy).then_inc(
                    S("s5_ftc"), 1)
            for b in range(8):
                act.wait_ge(S("s5_k"), b + 1)
                A(Kb[:, 4 * b:4 * b + 4, :].rearrange("p a b -> p (a b)"), bank(2 + b % 2)[0:SC, :],
                  ACT.Copy).then_inc(S("s5_kc"), 1)
            act.wait_ge(S("M_in"), 16 * BL)
            for b in range(8):
                act.wait_ge(S("s5_z"), b + 1)
                A(ZZ[:, 0, 4 * b:4 * b + 4, :].rearrange("p a b -> p (a b)"), bank(4 + b % 2)[:, 0:4 * NB],
                  ACT.Copy).then_inc(S("s5_zc"), 1)
            for e, (b, (g0, g1)) in enumerate(zip(Y_BANKS, Y_GROUPS)):
                act.wait_ge(S("s5_y"), e + 1)
                A(Yb[:, g0:g1, :].rearrange("p a b -> p (a b)"), bank(b)[:, 0:(g1 - g0) * NB],
                  ACT.Copy).then_inc(S("s5_yc"), 1)
            for k in range(4):
                act.wait_ge(S("s5_ys"), k + 1)
                A(Yf_tok[:, k, :], Yf_tok[:, k, :], ACT.Gelu_apprx_tanh).then_inc(S("s5_gelu"), 1)
            for m in range(4):
                act.wait_ge(S("s5_glu"), m + 1)
                A(halves(sgl[:, m, :]), pair(m), ACT.Sigmoid).then_inc(S("s5_sig"), 1)
            split_h("o_out")

        def odd_dve(dve, V, chain, norm_split, residual, head_norm, split_h):
            norm_split(2, "norm_mix", 8, "o_in")
            dve.wait_ge(S("out_written"), 16 * 5)
            for t in range(2):
                dve.wait_ge(S("gl_sp"), t + 1)
                la, b_ = LA[:, t, :], BC[:, t, :]
                chain(stt(la, la, 0.0, b_, ALU.min, ALU.subtract))
                chain(V.tensor_scalar(la, la, 1.0 / GLA_TAU, None, ALU.mult))
                chain(V.tensor_tensor_scan(b_, c_("scan128", T), la, 0.0, ALU.mult, ALU.add))
                kd = KG[:, t, :]
                for c0, m, n in ((0, NCH, L), (SEQ, 8, 8)):
                    b3, k3 = (x[:, c0:c0 + m * n].rearrange("p (c n) -> p c n", n=n) for x in (b_, kd))
                    last = tt(V, k3, bc(b3[:, :, n - 1], 2, n), b3, ALU.subtract)
                last.then_inc(S("gl_kd"), 1)
            for t in range(2):
                dve.wait_ge(S("gl_e1"), t + 1)
                e1 = E1[:, t, :]
                V.tensor_copy(ebl[:, t, 0:4], e1[:, 0:SEQ].rearrange("p (c n) -> p c n", n=L)[:, :, L - 1])
                V.tensor_copy(ebl[:, t, 4:12], e1[:, SEQ:T].rearrange("p (c n) -> p c n", n=8)[:, :, 7])
                tt(V, QG[:, t, :], zo[:, t, :], e1, ALU.mult)
                tt(V, KG[:, t, :], zo[:, 2 + t, :], KG[:, t, :], ALU.mult).then_inc(S("gl_qk"), 1)

            def parts(x, v):
                h = 64 >> v
                n = SEQ if v < 4 else T
                b = x[:, 0:n].rearrange("p (b a h) -> p b a h", a=2, h=h)
                return b[:, :, 0, :], b[:, :, 1, :], h

            def diffs(k):
                t, v = k // 7, k % 7
                low, high, h = parts(XL[:, t, v, :], v)
                bl, bh, _ = parts(BC[:, t, :], v)
                ref = bc(bl[:, :, h - 1], 2, h)
                tt(V, low, ref, bl, ALU.subtract)
                tt(V, high, bh, ref, ALU.subtract).then_inc(S("gl_d"), 1)

            def scales(k):
                t, v = k // 7, k % 7
                dve.wait_ge(S("gl_e"), k + 1)
                low, high, _ = parts(XL[:, t, v, :], v)
                kl, _, _ = parts(zo[:, 2 + t, :], v)
                _, qh_, _ = parts(zo[:, t, :], v)
                tt(V, low, low, kl, ALU.mult)
                tt(V, high, high, qh_, ALU.mult).then_inc(S("gl_x"), 1)

            dve.wait_ge(S("s5_trig"), 1)
            chain(tt(V, t_a, l_re, t_s, ALU.mult))
            chain(tt(V, t_b, l_im, t_s, ALU.mult))
            for out, shift in ((t_s, 0.0), (t_c, np.pi / 2)):
                chain(V.tensor_scalar(t_n, t_b, 1.0 / TWO_PI, shift / TWO_PI, ALU.mult, ALU.add))
                chain(V.tensor_scalar(t_n, t_n, ROUND, None, ALU.add))
                chain(V.tensor_scalar(t_n, t_n, -ROUND, None, ALU.add))
                chain(stt(out, t_n, -6.28125, t_b, ALU.mult, ALU.add))
                chain(stt(out, t_n, -(TWO_PI - 6.28125), out, ALU.mult, ALU.add))
                chain(V.tensor_scalar(out, out, float(shift), 3.1415925, ALU.add, ALU.min))
                ins = V.tensor_scalar(out, out, -3.1415925, None, ALU.max)
                if shift:
                    ins.then_inc(S("s5_ab"), 1)
                else:
                    chain(ins)
            diffs(0)
            diffs(1)
            for k in range(7):
                diffs(k + 2)
                scales(k)
            dve.wait_ge(S("s5_trig"), 2)
            chain(tt(V, lr, t_er, t_c, ALU.mult))
            chain(tt(V, li, t_er, t_s, ALU.mult))
            V.tensor_scalar(lis, li, v_("sgn"), None, ALU.mult).then_inc(S("s5_lam"), 1)
            dve.wait_ge(S("s5_lam"), 1)
            chain(tt(V, t_d, l_re, l_re, ALU.mult))
            chain(tt(V, t_e, l_im, l_im, ALU.mult))
            chain(tt(V, t_d, t_d, t_e, ALU.add))
            chain(V.reciprocal(t_d, t_d))
            chain(V.tensor_scalar(t_f, lr, -1.0, None, ALU.add))
            for out, x, y, op in ((wr, l_re, l_im, ALU.add), (wi, l_im, l_re, ALU.subtract)):
                chain(tt(V, out, t_f, x, ALU.mult))
                chain(tt(V, t_e, li, y, ALU.mult))
                if op == ALU.add:
                    chain(tt(V, out, out, t_e, ALU.add))
                else:
                    chain(tt(V, out, t_e, out, ALU.subtract))
                chain(tt(V, out, out, t_d, ALU.mult))
            chain(V.tensor_scalar(wis, wi, v_("sgn"), None, ALU.mult))

            chain(V.tensor_copy(lr8, lr))
            chain(V.tensor_copy(li8, li))
            for _ in range(3):
                chain(tt(V, t_d, lr8, lr8, ALU.mult))
                chain(tt(V, t_e, li8, li8, ALU.mult))
                chain(tt(V, li8, lr8, li8, ALU.mult))
                chain(V.tensor_scalar(li8, li8, 2.0, None, ALU.mult))
                chain(tt(V, lr8, t_d, t_e, ALU.subtract))
            chain(V.tensor_scalar(lis8, li8, v_("sgn"), None, ALU.mult))
            uc, us, r8 = t_a, t_b, t_er
            for _ in range(3):
                chain(tt(V, r8, r8, r8, ALU.mult))
            chain(V.tensor_copy(uc, t_c))
            chain(V.tensor_scalar(us, t_s, v_("sgn"), None, ALU.mult))

            def unit():
                tt(V, t_d, uc, uc, ALU.mult)
                chain(tt(V, t_e, us, us, ALU.mult))
                chain(tt(V, t_d, t_d, t_e, ALU.add))
                chain(V.tensor_scalar(t_d, t_d, -0.5, 1.5, ALU.mult, ALU.add))
                tt(V, uc, uc, t_d, ALU.mult)
                chain(tt(V, us, us, t_d, ALU.mult))

            def square():
                tt(V, t_d, uc, uc, ALU.mult)
                tt(V, t_e, us, us, ALU.mult)
                chain(stt(us, uc, 2.0, us, ALU.mult, ALU.mult))
                chain(tt(V, uc, t_d, t_e, ALU.subtract))
                unit()

            unit()
            for _ in range(3):
                square()
            for k in range(7, 14):
                if k < 12:
                    diffs(k + 2)
                scales(k)
            dve.wait_ge(S("proj_done"), USE["o_in"] + O_TILES)
            V.memset(Sg, 0.0).then_inc(S("gl_st"), 1)
            all_free(dve, "o_in", O_TILES)
            for k in range(4):
                last = V.tensor_copy(up[:, k], zo[:, 12 + k, :].rearrange("p (b s) -> p s b", s=BL))
            last.then_inc(S("s5_up"), 1)
            for c in range(NCH + 1):
                n = L if c < NCH else NSAMP
                nl = 8 if c < NCH else 4
                m = c_("gla", 1024) if c < NCH else c_("gla_s", 256, 64)
                for h in range(GH):
                    w = attw[0:n, h % 2, 0:nl * n]
                    dve.wait_ge(S("gl_sc"), 4 * c + h + 1)
                    if c == NCH and h == 0:
                        V.memset(attg[NSAMP:P, :, 0:NSAMP], 0.0)
                    if c < NCH:
                        tt(V, w.rearrange("p (a b) -> p a b", a=2), PP[h % 2][:, :, :],
                           m.rearrange("p (a b) -> p a b", a=2), ALU.mult).then_inc(S("gl_am"), 1)
                    else:
                        tt(V, w, PP[h % 2][0:n, 0, 0:256], m, ALU.mult).then_inc(S("gl_am"), 1)
                    dve.wait_ge(S("gl_am"), 4 * c + h + 1)
                    V.tensor_reduce(attg[0:n, h, 0:n], w.rearrange("p (v n) -> p n v", v=nl), AX.X,
                                    ALU.add).then_inc(S("gl_at"), 1)
                if c < NCH:
                    dve.wait_ge(S("gl_s"), c + 1)
                    for t in range(2):
                        last = stt(Sg[:, t, :], Sg[:, t, :], ebl[:, t, c:c + 1], bank(5)[:, 256 + t * P:256 + (t + 1) * P],
                                   ALU.mult, ALU.add)
                    last.then_inc(S("gl_st"), 1)
                    dve.wait_ge(S("gl_st"), c + 2)
            dve.wait_ge(S("gl_tokc"), NCH + 1)
            for h in range(GH):
                last = tt(V, Vm[:, h], bc(vt[0:64, h, :], 1, 8), bc(seqmask[0:64, :], 2, P), ALU.mult)
            last.then_inc(S("gs_vm"), 1)
            dve.wait_ge(S("gl_o"), NCH + 1)
            dve.wait_ge(S("gS_in"), 16)
            for t in range(2):
                chain(tt(V, SSg[:, t], SSg[:, t], bc(ebl[:, t, 4:12], 2, P), ALU.mult))
                dve.wait_ge(S("gs_s"), t + 1)
                s4 = SSg[:, t].rearrange("p (a j) n -> p a (j n)", a=2)
                tt(V, s4, s4, PP[t][:, :, :], ALU.add).then_inc(S("gs_st"), 1)

            def gla_out():
                head_norm("gn", zo[:, 0:4, :], LAX, GDV, mean=False)
                dve.wait_ge(S("sG_written"), 16)
                for h in range(4):
                    stt(hT[:, h, :], zo[:, h, :], v_("o_ln_g", h), zo[:, 8 + h, :], ALU.mult,
                        ALU.mult).then_inc(S("ycat"), 1)

            dve.wait_ge(S("gs_st"), 2)
            dve.wait_ge(S("s5_bx_in"), 48)
            cs = slice(0, FSPLIT)
            input_matrices(V, chain, cs, ft, S("s5_f"), 0, 3)
            dve.wait_ge(S("u_scratched"), 16)
            gla_out()
            input_matrices(V, chain, cs, ft, S("s5_f"), 3, BL)
            dve.wait_ge(S("s5_k"), 8)
            V.memset(UC[:, :, 0:1], 1.0)
            chain(V.memset(US[:, :, 0:1], 0.0))
            n = 1
            while n < NBP:
                c0, s0, c1, s1 = UC[:, :, 0:n], US[:, :, 0:n], UC[:, :, n:2 * n], US[:, :, n:2 * n]
                cn, sn = bc(uc, 2, n), bc(us, 2, n)
                ta, tb = TA[:, :, 0:n], TB[:, :, 0:n]
                tt(V, c1, c0, cn, ALU.mult)
                tt(V, s1, s0, cn, ALU.mult)
                tt(V, ta, s0, sn, ALU.mult)
                chain(tt(V, tb, c0, sn, ALU.mult))
                tt(V, c1, c1, ta, ALU.subtract)
                chain(tt(V, s1, s1, tb, ALU.add))
                n *= 2
                if n < NBP:
                    square()
            dve.wait_ge(S("s5_kc"), 8)
            dve.wait_ge(S("zsw_in"), 32)
            z, zs = (ZZ[:, k, :, 0:NBP] for k in range(2))
            tt(V, TA, zs, US, ALU.mult)
            tt(V, TB, z, US, ALU.mult)
            tt(V, z, z, UC, ALU.mult)
            chain(tt(V, zs, zs, UC, ALU.mult))
            tt(V, z, z, TA, ALU.subtract)
            chain(tt(V, zs, zs, TB, ALU.add))
            for g in range(SG):
                for w in (z, zs):
                    last = V.tensor_tensor_scan(w[:, g, :], r8[:, g:g + 1].to_broadcast([P, NBP]), w[:, g, :], 0.0,
                                                ALU.mult, ALU.add)
            chain(last)
            tt(V, zs, zs, US, ALU.mult)
            tt(V, z, z, UC, ALU.mult)
            chain(V.memset(XX[:, :, 0:1], 0.0))
            chain(tt(V, XX[:, :, 1:NBP + 1], z, zs, ALU.add))
            chain(V.tensor_copy(SO[:, :, 0], XX[:, :, NBP]))
            x0 = x0st
            tt(V, st1, x0, bc(lr8, 2, 8), ALU.mult)
            chain(tt(V, st2, x0sw, bc(lis8, 2, 8), ALU.mult))
            chain(tt(V, st1, st1, st2, ALU.add))
            tt(V, SO[:, :, 1:9], st1, ZZ[:, 0, :, NBP:NB], ALU.add).then_inc(S("s5_scan"), 1)
            V.tensor_copy(XX[:, :, NBP:NB], x0).then_inc(S("s5_scan"), 1)
            dve.wait_ge(S("Y_in"), 16)
            dve.wait_ge(S("s5_y"), len(Y_BANKS))
            for k in range(4):
                stt(Yf_tok[:, k, :].rearrange("p (b s) -> p b s", s=BL),
                    zo[:, 12 + k, :].rearrange("p (b s) -> p b s", s=BL), v_("o_d", k),
                    Yf[:, k].rearrange("p s b -> p b s"), ALU.mult, ALU.add).then_inc(S("s5_ys"), 1)
            for m in range(4):
                dve.wait_ge(S("s5_sig"), m + 1)
                tt(V, hT[:, 4 + m, :], Yf_tok[:, m, :], sgl[:, m, :], ALU.mult).then_inc(S("ycat"), 1)
            split_h("o_out")
            residual("o_out")

        @block.sync
        def _(sp):
            def stream(name):
                c0 = CHUNK0[name]
                if name in RUNS:
                    t0, n = RUNS[name]
                    with sp.Fori(0, (n - 2) // 2) as i:
                        for s in range(2):
                            sp.wait_ge(S("w_split"), 2 * i + (c0 + s + 1))
                            sp.dma_start(w_ring[:, s, :], d["w"][bass.ds(2 * i + (t0 + 2 + s), 1)].rearrange(
                                "a p n -> p (a n)")).then_inc(WL[s], 16)
                    done = c0 + n
                else:
                    l = int(name[4:])

                    def load(e, i):
                        tile, j = e // 3, e % 3
                        k0, nk = DCH[j]
                        if i is None:
                            sp.wait_ge(S("w_split"), c0 + e - 1)
                            src = d["w_down"][8 * l + tile, :, k0 * P:(k0 + nk) * P]
                        else:
                            sp.wait_ge(S("w_split"), 6 * i + (c0 + e - 1))
                            src = d["w_down"][bass.ds(2 * i + (8 * l + tile), 1), :, k0 * P:(k0 + nk) * P].rearrange(
                                "a p n -> p (a n)")
                        sp.dma_start(w_ring[:, e % 2, 0:nk * P], src).then_inc(WL[e % 2], 16)

                    with sp.Fori(0, 3) as i:
                        for e in range(2, 8):
                            load(e, i)
                    for e in range(20, 24):
                        load(e, None)
                    done = c0 + 24
                nxt = NEXT[name]
                if nxt is None:
                    return
                for s in range(2):
                    sp.wait_ge(S("w_split"), done + s - 1)
                    if nxt in RUNS:
                        sp.dma_start(w_ring[:, s, :], d["w"][RUNS[nxt][0] + s]).then_inc(WL[s], 16)
                    else:
                        k0, nk = DCH[s]
                        sp.dma_start(w_ring[:, s, 0:nk * P], d["w_down"][8 * int(nxt[4:]), :, k0 * P:(k0 + nk) * P]
                                     ).then_inc(WL[s], 16)

            nout = [0]

            def out(name, src):
                nout[0] += 16
                sp.dma_start(o[name], src).then_inc(S("out_written"), 16)

            sp.dma_start(cst[:, 0:256], d["consts"][:, 0:256]).then_inc(S("ones_in"), 16)
            for k in range(2):
                h = slice(k * KT // 2, (k + 1) * KT // 2)
                sp.dma_start(xT[:, h, :], d["x"][:, h, :]).then_inc(S(f"x_in{k}"), 16)
            sp.dma_start(vec[:], d["vec"]).then_inc(S("x_in1"), 16)
            sp.dma_start(wif, d["w_if"]).then_inc(S("e_small_in"), 16)
            for s in range(2):
                sp.dma_start(w_ring[:, s, :], d["w"][s]).then_inc(WL[s], 16)
            sp.dma_start(cst[:, 256:], d["consts"][:, 256:]).then_inc(S("consts_in"), 16)
            sp.dma_start(shin, d["shift"]).then_inc(S("e_small_in"), 16)
            sp.dma_start(lora, d["lora"]).then_inc(S("e_small_in"), 16)
            sp.dma_start(r_m0[:, 0:8], d["m0"]).then_inc(S("e_small_in"), 16)
            sp.dma_start(convp[:], d["convp"]).then_inc(S("e_small_in"), 16)
            stream("e_in")
            sp.wait_ge(S("proj_done"), E_TILES)
            sp.dma_start(Csf, d["C"]).then_inc(S("C_in"), 16)
            for s in range(2):
                sp.wait_ge(S(f"ext_free{s}"), 1 + 7)
            out("shift", shout)
            sp.wait_ge(S("ml_rows"), 2)
            out("m", r_mo[:, 0:NSEQ])
            sp.wait_ge(S("ml_state"), 4)
            out("pC", Cst)
            sp.wait_ge(S("ml_sst"), 11)
            sp.dma_start(o["sC"], Csf).then_inc(S("sC_written"), 16)
            sp.wait_ge(S("rw_prep"), 4)
            sp.wait_ge(S("rw_pool"), 4)
            sp.dma_start(SS, d["rS"]).then_inc(S("rS_in"), 16)
            sp.wait_ge(S("rk_st"), NCR + 1)
            out("pS", Sr)
            sp.wait_ge(S("rs_st"), 1)
            sp.dma_start(o["sS"], SS).then_inc(S("sS_written"), 16)
            stream("e_out")
            sp.wait_ge(S("sS_written"), 16)
            sp.wait_ge(S("proj_done"), USE["ffn0"])
            sp.dma_start(convin, d["conv_state"][0]).then_inc(S("convin_in"), 16)
            stream("ffn0")
            stream("down0")
            for s in range(2):
                sp.wait_ge(S(f"ext_free{s}"), 1 + 7 + FT)
            out("conv0", convout)
            odd_sp(sp, stream, out)
            for n in ("sC_written", "sS_written", "sG_written"):
                sp.wait_ge(S(n), 16)
            sp.wait_ge(S("out_written"), nout[0])

        @block.gpsimd
        def _(pool):
            G = nc.gpsimd
            chain = Chain(pool, S("pool_chain"))

            def split(w, hi, lo, sem):
                one = (bc(ones[:, 0:w.shape[1]], 2, w.shape[2]) if len(w.shape) == 3
                       else ones[:, 0:1].to_broadcast(list(w.shape)))
                chain(tt(G, hi, w, one, ALU.mult))
                tt(G, lo, w, hi, ALU.subtract).then_inc(sem, 1)

            def chunk(s, n=KT * P):
                split(w_ring[:, s, 0:n], w_hi[:, s, 0:n], w_lo[:, s, 0:n], S("w_split"))

            def project(name, first=0):
                with pool.Fori(first, RUNS[name][1] // 2) as i:
                    chain.loop(i, 2, first)
                    for s in range(2):
                        pool.wait_ge(WL[s], 16 * i + 16 * (CHUNK0[name] // 2 + 1))
                        pool.wait_ge(S("proj_done"), 2 * i + (USE[name] + s - 1))
                        chunk(s)
                    chain.end_loop(RUNS[name][1] // 2 - first)

            def down(l):
                pool.wait_ge(S("proj_done"), USE[f"down{l}"] - 1)
                with pool.Fori(0, 4) as i:
                    chain.loop(i, 6)
                    for e in range(6):
                        tile, j = e // 3, e % 3
                        pool.wait_ge(WL[e % 2], 48 * i + 16 * (CHUNK0[f"down{l}"] // 2 + e // 2 + 1))
                        if j == 1:
                            pool.wait_ge(S("proj_done"), 2 * i + (USE[f"down{l}"] + tile))
                        else:
                            pool.wait_ge(S("chunk_used"), 4 * i + (16 * l + 2 * tile + (j == 2) + 1))
                        chunk(e % 2, DCH[j][1] * P)
                    chain.end_loop(4)

            pool.sem_inc(S("chunk_used"), 1)
            pool.wait_ge(S("ones_in"), 16)
            pool.wait_ge(S("e_small_in"), 16 * 5)
            split(wif, wif_hi, wif_lo, S("small_split"))
            for s in range(2):
                pool.wait_ge(WL[s], 16)
                chunk(s)
            project("e_in", 1)
            for p in range(RP):
                a, cum, em = (prep[:, k, p % 2, :] for k in (1, 2, 4))
                pool.wait_ge(S("rw_exp"), p + 1)
                pool.wait_ge(S("rw_k"), p + 1)
                tt(G, BK[:, p, 0, :], BK[:, p, 0, :], em, ALU.mult)
                tt(G, BK[:, p, 1, :], a, em, ALU.mult)
                tt(G, AR[:, p, 1, :], zr[:, p, :], cum, ALU.mult).then_inc(S("rw_pool"), 1)
            pool.wait_ge(S("rs_st"), 1)
            project("e_out")
            project("ffn0")
            down(0)
            pool.wait_ge(S("chunk_used"), 17)
            pool.wait_ge(S("o_small_in"), 32)
            split(wad, wad_hi, wad_lo, S("small_split"))
            project("o_in")
            odd_pool(pool, chain)
            pool.wait_ge(S("s5_y"), len(Y_BANKS))
            project("o_out")
            project("ffn1")
            down(1)

        @block.tensor
        def _(pe):
            def norm(n):
                for k in range(KT):
                    pe.wait_ge(S("sq_ready"), 8 * n + k + 1)
                    for a in range(2):
                        last = mm(PP[3][:, a, 0:TH], ones, sq[:, k % 2, a * TH:(a + 1) * TH], k == 0, k == KT - 1)
                    last.then_inc(S("sq_used"), 1)

            def project(name):
                n = RUNS[name][1]
                for s in range(2):
                    pe.wait_ge(S("w_split"), CHUNK0[name] + s + 1)
                    pe.wait_ge(FREE[s], USE[name] // 2 + 1)
                    for k in range(KT):
                        if s == 0:
                            pe.wait_ge(S("h_lo"), 8 * SPLIT[name] + k + 1)
                        c = slice(k * P, (k + 1) * P)
                        for a in range(2):
                            h = slice(a * TH, (a + 1) * TH)
                            last = mm3(PP[s][:, a, 0:TH], w_hi[:, s, c], w_lo[:, s, c],
                                       H_HI[name][k][:, h], hT_r[:, k, h], k == 0, k == KT - 1)
                    last.then_inc(S("proj_done"), 1)
                with pe.Fori(1, n // 2) as i:
                    for s in range(2):
                        pe.wait_ge(S("w_split"), 2 * i + (CHUNK0[name] + s + 1))
                        pe.wait_ge(FREE[s], i + (USE[name] // 2 + 1))
                        for a in range(2):
                            h = slice(a * TH, (a + 1) * TH)
                            for k in range(KT):
                                c = slice(k * P, (k + 1) * P)
                                last = mm3(PP[s][:, a, 0:TH], w_hi[:, s, c], w_lo[:, s, c],
                                           H_HI[name][k][:, h], hT_r[:, k, h], k == 0, k == KT - 1)
                        last.then_inc(S("proj_done"), 1)

            def down(l):
                c0 = CHUNK0[f"down{l}"]
                with pe.Fori(0, 4) as i:
                    for s in range(2):
                        pe.wait_ge(FREE[s], i + (USE[f"down{l}"] // 2 + 1))
                        for j, (k0, nk) in enumerate(DCH):
                            c = (3 * s + j) % 2
                            pe.wait_ge(S("w_split"), 6 * i + (c0 + 3 * s + j + 1))
                            pe.wait_ge(S("act_lo"), FT * l + (AHEAD if k0 + nk <= AHEAD else FT if k0 + nk == FT
                                                              else k0 + nk))
                            for a in range(2):
                                h = slice(a * TH, (a + 1) * TH)
                                for k in range(k0, k0 + nk):
                                    b = slice((k - k0) * P, (k - k0 + 1) * P)
                                    last = mm3(PP[s][:, a, 0:TH], w_hi[:, c, b], w_lo[:, c, b],
                                               act_hi[:, (k + KT) % FT, h], act_lo[:, k, h], k == 0,
                                               k == FT - 1)
                            last.then_inc(S("proj_done" if j == 2 else "chunk_used"), 1)

            def head_norm(nm, src, sqs, avg, mean=True):
                if mean:
                    for h in range(4):
                        pe.wait_ge(S("hn_src"), HN[nm] + h + 1)
                        for a in range(2):
                            last = mm(PP[h][:, a, 0:TH], avg, src[:, h, a * TH:(a + 1) * TH])
                        last.then_inc(S("hn_mean"), 1)
                for h in range(4):
                    pe.wait_ge(S("hn_sq"), HN[nm] + h + 1)
                    for a in range(2):
                        last = mm(PP[h][:, a, 0:TH], avg, sqs[:, h, a * TH:(a + 1) * TH])
                    last.then_inc(S("hn_var"), 1)

            def mlstm():
                pe.wait_ge(S("consts_in"), 16)
                pe.wait_ge(S("ml_exps"), 4)
                pe.wait_ge(FREE[0], USE["e_out"] // 2 + 1)
                pe.wait_ge(FREE[1], USE["e_out"] // 2 + 1)
                for h in range(MH):
                    if h >= 2:
                        pe.wait_ge(S("ml_qh"), h - 1)
                    for a in range(2):
                        last = mm(PP[h % 2][:, a, 0:TH], sel[:, h, :], r_s[:, a * TH:(a + 1) * TH])
                    last.then_inc(S("ml_bcast"), 1)
                for h in range(MH):
                    mm(bank(4)[:, 12 * h:12 * h + 12], sel[:, h, :], r_dec[:, 0:12])
                for c in range(NCH + 1):
                    n = L if c < NCH else NSAMP
                    last = mm(bank(4)[0:n, 48 + 4 * c:52 + 4 * c], r_w[:, L * c:L * c + n], ident[0:4, 0:4])
                last.then_inc(S("ml_small"), 1)
                pe.wait_ge(S("ml_qh"), 4)
                for c in range(NCH + 1):
                    n, c0 = (L, L * c) if c < NCH else (NSAMP, SEQ)
                    cols = slice(c0, c0 + n)
                    if c:
                        pe.wait_ge(S("ml_att"), c)
                    for h in range(MH):
                        mm(bank(0)[0:n, h * n:(h + 1) * n], zm[:, 4 + h, cols], zm[:, h, cols])
                    for h in range(MH):
                        mm(bank(1)[0:n, h * n:(h + 1) * n], sel[:, h, 0:n], r_a[:, cols], True, False)
                        last = mm(bank(1)[0:n, h * n:(h + 1) * n], r_i[:, cols], sel[:, h, 0:n], False, True)
                    last.then_inc(S("ml_scores"), 1)
                    if c:
                        pe.wait_ge(S("ml_tokc"), c)
                    for h in range(MH):
                        nc.tensor.transpose(bank(2)[0:n, h * P:(h + 1) * P], zm[:, 8 + h, cols], ident)
                    for h in range(MH):
                        last = nc.tensor.transpose(bank(3)[0:n, h * P:(h + 1) * P], zm[:, 4 + h, cols], ident)
                    last.then_inc(S("ml_tok"), 1)
                    pe.wait_ge(S("ml_att"), c + 1)
                    pe.wait_ge(S("ml_tokc"), c + 1)
                    pe.wait_ge(S("ml_qn"), c + 1)
                    if c:
                        pe.wait_ge(S("ml_outc"), c)
                    for h in range(MH):
                        num = bank(4)[:, h * n:(h + 1) * n]
                        den = bank(5)[0:4, 0:n]
                        mm(num, vaug[0:n, h, 0:P], att[0:n, h, 0:n], True, False)
                        if c < NCH:
                            mm(num, Cst[:, h, 0:P], qh[:, h, cols], False, True)
                        else:
                            if h == 0:
                                pe.wait_ge(S("C_in"), 16)
                            for j in range(8):
                                mm(num[:, 8 * j:8 * j + 8], Cs[:, h, j, 0:P], qh[:, h, c0 + 8 * j:c0 + 8 * j + 8],
                                   False, j == 7)
                        mm(den, col4(h, n), att[0:n, h, 0:n], h == 0, False)
                        last = mm(den, col4(h, P), qn[:, h, 0:n], False, h == MH - 1)
                    last.then_inc(S("ml_nd"), 1)
                    if c < NCH:
                        for h in range(MH):
                            last = mm(bank(6 + h // 2)[:, 129 * (h % 2):129 * (h % 2) + 129], ktok[:, h, :],
                                      vaug[:, h, :])
                        last.then_inc(S("ml_upd"), 1)
                    else:
                        pe.wait_ge(S("ml_km"), 1)
                        for g in range(11):
                            if g >= 2:
                                pe.wait_ge(S("ml_sst"), g - 1)
                            for e in range(3 * g, min(3 * g + 3, 32)):
                                last = mm(bank(6 + g % 2)[:, 129 * (e - 3 * g):129 * (e - 3 * g) + 129],
                                          Km[:, e // 8, e % 8, :], vaug[0:64, e // 8, :])
                            last.then_inc(S("ml_supd"), 1)
                pe.wait_ge(S("ml_den"), 1)
                pe.wait_ge(S("ml_sst"), 11)
                for h in range(MH):
                    for a in range(2):
                        last = mm(PP[h][:, a, 0:TH], sel[:, h, :], r_s[:, a * TH:(a + 1) * TH])
                    last.then_inc(S("ml_emt"), 1)
                head_norm("mn", zm[:, 4:8, :], zm[:, 8:12, :], ones)

            def rwkv():
                for p in range(RP):
                    pe.wait_ge(S("rw_kksq"), p + 1)
                    for a in range(2):
                        last = mm(PP[0][64:72, a, 0:TH], col8(p), AR[:, p, 1, a * TH:(a + 1) * TH], p == 0,
                                  p == RP - 1)
                last.then_inc(S("rw_kkn"), 1)
                pe.wait_ge(S("rw_lora"), 2)
                for p in (1, 2, 3, 0):
                    if p == 0:
                        pe.wait_ge(S("rw_kkrow"), 1)
                    for a in range(2):
                        last = mm(PP[p][:, a, 0:TH], lora[:, 1, p * P:(p + 1) * P], zr[:, 13, a * TH:(a + 1) * TH])
                    last.then_inc(S("rw_gate"), 1)
                pe.wait_ge(S("rw_kkrow"), 2)
                for p in range(RP):
                    pe.wait_ge(S("rw_gatec"), 4)
                    for a in range(2):
                        last = mm(PP[p][:, a, 0:TH], headrow[:, p, :], kkrow[:, a * TH:(a + 1) * TH])
                    last.then_inc(S("rw_kkn"), 1)
                for p in range(RP):
                    if p < 2:
                        pe.wait_ge(S("rw_kkrow"), 2 * p + 4)
                    if p >= 2:
                        pe.wait_ge(S("rw_sig"), 2 * (p - 1))
                    for q, r in ((0, 0), (1, 64)):
                        for a in range(2):
                            last = mm(PP[2 * (p % 2) + q][:, a, 0:TH], lora[r:r + 64, 0, p * P:(p + 1) * P],
                                      zr[r:r + 64, 12, a * TH:(a + 1) * TH])
                    last.then_inc(S("rw_up"), 1)
                pe.wait_ge(S("rw_sig"), 8)

                def rows2():
                    return [(slice(64 * h, 64 * h + 64)) for h in range(2)]

                def scores(c):
                    cols = slice(LR * c, LR * c + LR)
                    for p in range(RP):
                        pe.wait_ge(S("rw_prep"), p + 1)
                        pe.wait_ge(S("rw_pool"), p + 1)
                        if 4 * c + p >= 2:
                            pe.wait_ge(S("rk_g"), 4 * c + p - 1)
                        b = bank(p % 2)
                        for r in rows2():
                            mm(b[r, 0:128], BK[r, p, 0, cols], AR[r, p, :, cols])
                            mm(b[r, 128:256], BK[r, p, 1, cols], AR[r, p, :, cols])
                            last = mm(b[r, 256:320], AR[r, p, 0, cols], BK[r, p, 0, cols])
                        last.then_inc(S("rk_sc"), 1)

                def tokens(c):
                    cols = slice(LR * c, LR * c + LR)
                    for q in range(2):
                        if 2 * c + q >= 1:
                            pe.wait_ge(S("rk_tokc"), 2 * c + q)
                        for p in (2 * q, 2 * q + 1):
                            for r in rows2():
                                for k, src in enumerate((BK[r, p, 0, cols], BK[r, p, 1, cols], zr[r, 8 + p, cols])):
                                    e = 192 * (p % 2) + 64 * k
                                    last = mm(bank(4)[r, e:e + 64], src, ident[r, r])
                        last.then_inc(S("rk_tok"), 1)

                def level(c, k):
                    top = 5 if c < NCR else 2
                    for q in range(2):
                        if k == 0:
                            pe.wait_ge(S("rk_g"), 4 * c + 2 * q + 2)
                            if c:
                                pe.wait_ge(S(f"rk_lc{q}"), 6 * c)
                        else:
                            pe.wait_ge(S(f"rk_lc{q}"), 6 * c + k)
                        for pp in range(2):
                            p = 2 * q + pp
                            b = PP[1][:, q, 192 * pp:192 * pp + 192]
                            for r in rows2():
                                if k == 0:
                                    mm(b[r, 0:64], Gs[r, c % 2, p, 256:320], Gs[r, c % 2, p, 0:64])
                                    last = mm(b[r, 128:192], Gs[r, c % 2, p, 0:64], Gs[r, c % 2, p, 256:320])
                                    continue
                                v = XPA[r, q, k % 2, pp, :, :]
                                if k < top:
                                    mm(b[r, 0:128], v[:, 2, :], v[:, 0:2, :])
                                    last = mm(b[r, 128:192], v[:, 0, :], v[:, 2, :])
                                else:
                                    last = mm(b[r, 64:128], v[:, 2, :], v[:, 1, :])
                        last.then_inc(S(f"rk_lv{q}"), 1)

                def seq_r1(c):
                    g = c % 2
                    pe.wait_ge(S("rk_tokc"), 2 * c + 2)
                    pe.wait_ge(S("rk_st"), c + 1 if c < NCR else NCR + 1)
                    if c == NCR:
                        pe.wait_ge(S("rS_in"), 16)
                        pe.wait_ge(S("rk_uc"), c)
                        for p in range(RP):
                            for r in rows2():
                                for j in range(8):
                                    e = SEQ + 8 * j
                                    last = mm(bank(5)[r, 64 * p + 8 * j:64 * p + 8 * j + 8], SS[r, p, j, :],
                                              AR[r, p, 0, e:e + 8])
                        last.then_inc(S("rs_qt"), 1)
                        pe.wait_ge(S("rk_r1c"), NCR + 1)
                    elif c:
                        pe.wait_ge(S("rk_uc"), c)
                    for p in range(RP):
                        for r in rows2():
                            out = bank(5)[r, 64 * p:64 * p + 64]
                            if c < NCR:
                                mm(out, AR[r, p, 0, LR * c:LR * c + LR], Sr[r, p, :], True, False)
                            else:
                                mm(out, QT[r, p, :], ident[r, r], True, False)
                            last = mm(out, Gs[r, g, p, 128:192], tok[r, g, p, 2, :], False, True)
                    last.then_inc(S("rk_r1"), 1)

                def seq_u(c):
                    pe.wait_ge(S("rk_r1c"), c + 1 if c < NCR else NCR + 2)
                    for q in range(2):
                        pe.wait_ge(S(f"rk_lc{q}"), 6 * c + (6 if c < NCR else 3))
                    for p in range(RP):
                        for r in rows2():
                            last = mm(bank(5)[r, 256 + 64 * p:320 + 64 * p], PF[r, c % 2, p, :], R1[r, p, :])
                    last.then_inc(S("rk_u"), 1)

                def seq_ys(c):
                    g = c % 2
                    pe.wait_ge(S("rk_uc"), c + 1)
                    if c:
                        pe.wait_ge(S("rk_yc"), c)
                    for p in range(RP):
                        for r in rows2():
                            out = bank(6)[r, 64 * p:64 * p + 64]
                            mm(out, U[r, p, :], Gs[r, g, p, 64:128], True, False)
                            mm(out, tok[r, g, p, 2, :], Gs[r, g, p, 192:256], False, False)
                            if c < NCR:
                                last = mm(out, Sr[r, p, :], AR[r, p, 1, LR * c:LR * c + LR], False, True)
                            else:
                                for j in range(8):
                                    e = SEQ + 8 * j
                                    last = mm(out[:, 8 * j:8 * j + 8], SS[r, p, j, :], AR[r, p, 1, e:e + 8],
                                              False, j == 7)
                    last.then_inc(S("rk_y"), 1)
                    if c < NCR:
                        for p in range(RP):
                            for r in rows2():
                                out = bank(7)[r, 64 * p:64 * p + 64]
                                mm(out, tok[r, g, p, 0, :], U[r, p, :], True, False)
                                last = mm(out, tok[r, g, p, 1, :], tok[r, g, p, 2, :], False, True)
                        last.then_inc(S("rk_s"), 1)
                        return
                    pe.wait_ge(S("rs_uvm"), 1)
                    for p in range(RP):
                        if p >= 2:
                            pe.wait_ge(S("rs_sc"), p - 1)
                        for r in rows2():
                            mm(bank(p % 2)[r, :], tok[r, g, p, 0, :], UVm[r, 0, p, :, :], True, False)
                            last = mm(bank(p % 2)[r, :], tok[r, g, p, 1, :], UVm[r, 1, p, :, :], False, True)
                        last.then_inc(S("rs_s"), 1)

                for c in range(NCR + 1):
                    scores(c)
                    tokens(c)
                    level(c, 0)
                    if c:
                        seq_r1(c - 1)
                    level(c, 1)
                    if c:
                        seq_u(c - 1)
                    level(c, 2)
                    if c:
                        seq_ys(c - 1)
                    if c < NCR:
                        for k in (3, 4, 5):
                            level(c, k)
                seq_r1(NCR)
                seq_u(NCR)
                seq_ys(NCR)
                pe.wait_ge(S("rk_yc"), NCR + 1)
                for p, b in enumerate(BONUS_PAIR):
                    if p == 3:
                        pe.wait_ge(S("rw_bonusc"), 1)
                    for a in range(2):
                        last = mm(PP[b][:, a, 0:TH], headones, rkp[:, p, a * TH:(a + 1) * TH])
                    last.then_inc(S("rw_bonus"), 1)
                pe.wait_ge(S("rs_sc"), 4)
                pe.wait_ge(S("rw_bonusc"), 4)
                head_norm("rn", yr, AR[:, :, 0, :], headones)

            pe.wait_ge(S("ones_in"), 16)
            norm(0)
            pe.wait_ge(S("h_lo"), 8)
            pe.wait_ge(S("small_split"), 1)
            for a in range(2):
                h = slice(a * TH, (a + 1) * TH)
                for k in range(KT):
                    last = mm3(PP[2][0:36, a, 0:TH], wif_hi[:, k, :], wif_lo[:, k, :],
                               H_HI["e_in"][k][:, h], hT_r[:, k, h], k == 0, k == KT - 1)
            last.then_inc(S("gates_done"), 1)
            project("e_in")
            mlstm()
            rwkv()
            project("e_out")
            norm(1)
            project("ffn0")
            down(0)
            odd_pe(pe, norm, project, head_norm)
            norm(3)
            project("ffn1")
            down(1)
            norm(4)

        @block.scalar
        def _(act):
            A = nc.scalar.activation
            chain = Chain(act, S("act_chain"))

            def norm(n):
                for k in range(KT):
                    if n == 0:
                        act.wait_ge(S(f"x_in{k // 4}"), 16 * (1 + k // 4))
                    else:
                        act.wait_ge(FREE[k % 2], USE[ADDS[n - 1]] // 2 + k // 2 + 2)
                    if 8 * n + k >= 2:
                        act.wait_ge(S("sq_used"), 8 * n + k - 1)
                    A(sq[:, k % 2, :], xT[:, k, :], ACT.Square).then_inc(S("sq_ready"), 1)
                act.wait_ge(S("sq_used"), 8 * n + 8)
                chain(A(halves(rstd[:, :]), pair(3), ACT.Ln, scale=1.0 / D_MODEL, bias=EPS))
                A(rstd[:, :], rstd[:, :], ACT.Exp, scale=-0.5).then_inc(S("rstd_ready"), 1)

            def split_h(name):
                q = SPLIT[name]
                for k in range(KT):
                    if name[1:] == "_out":
                        act.wait_ge(S("ycat"), (0 if name == "e_out" else 8) + k + 1)
                    else:
                        act.wait_ge(S("h_ready"), 8 * {"e_in": 0, "ffn0": 1, "o_in": 2, "ffn1": 3}[name] + k + 1)
                    A(H_HI[name][k], hT[:, k, :], ACT.Copy).then_inc(S("h_hi"), 1)

            def evac(name, j0, n, func, dst, scale=1.0):
                with act.Fori(0, n // 2) as i:
                    for s in range(2):
                        act.wait_ge(S("proj_done"), 2 * i + (USE[name] + j0 + s + 1))
                        out = dst[:, bass.ds(2 * i + s, 1), :].rearrange("p a n -> p (a n)")
                        A(halves(out), pair(s), func, scale=scale).then_inc(FREE[s], 1)

            def to_ext(s, lead):
                e = ext[:, s, :]
                A(e[:, lead:lead + TH], PP[s][:, 0, 0:TH], ACT.Copy)
                A(e[:, lead + TH:lead + SEQ], PP[s][:, 1, 0:SEQ - TH], ACT.Copy)
                samp = e[:, lead + SEQ:lead + SEQ + (8 + lead) * 8].rearrange("p (j n) -> p j n", j=8)
                return A(samp[:, :, lead:lead + 8],
                         PP[s][:, 1, SEQ - TH:TH].rearrange("p (j n) -> p j n", j=8), ACT.Copy)

            def head_norm(nm, src, sqs, n, eps, mean=True):
                for h in range(4):
                    act.wait_ge(S("hn_xc" if mean else "hn_src"), HN[nm] + h + 1)
                    A(sqs[:, h, :], src[:, h, :], ACT.Square).then_inc(S("hn_sq"), 1)
                for h in range(4):
                    act.wait_ge(S("hn_var"), HN[nm] + h + 1)
                    ins = A(halves(sqs[:, h, :]), pair(h), ACT.Ln, scale=1.0 / n, bias=eps)
                chain(ins)
                for h in range(4):
                    A(sqs[:, h, :], sqs[:, h, :], ACT.Exp, scale=-0.5).then_inc(S("hn_std"), 1)

            def ffn(l):
                base = USE[f"ffn{l}"]
                for first, end in ((0, AHEAD), (AHEAD, FT)):
                    with act.Fori(first, end) as i:
                        for s in range(2):
                            act.wait_ge(S("proj_done"), 2 * i + (base + s + 1))
                            act.wait_ge(S(f"ext_free{s}"), i + (1 + 7 + FT * l))
                            to_ext(s, 2).then_inc(FREE[s], 1)
                        act.wait_ge(S("gate_conv"), i + (1 + FT * l))
                        A(cv[:, 2, :], cv[:, 1, :], ACT.Silu).then_inc(S("silu_done"), 1)
                        if end == AHEAD:
                            act.wait_ge(S("act_ready"), i + (1 + FT * l))
                            src, dst = (v[:, bass.ds(i + o, 1), :].rearrange("p a n -> p (a n)")
                                        for v, o in ((actv, 0), (act_hi, KT)))
                            A(dst, src, ACT.Copy).then_inc(S("act_hi"), 1)
                act.wait_ge(S("proj_done"), base + 2 * FT)
                for k in range(AHEAD, FT):
                    act.wait_ge(S("act_ready"), k + 1 + FT * l)
                    A(act_hi[:, k - AHEAD, :], actv[:, k, :], ACT.Copy).then_inc(S("act_hi"), 1)

            norm(0)
            split_h("e_in")
            act.wait_ge(S("x_in1"), 32)
            act.wait_ge(S("gates_done"), 1)
            A(halves(r_i), PP[2][0:4, :, 0:TH], ACT.Identity, bias=v_("b_if", rows=4))
            chain(A(halves(r_f), PP[2][32:36, :, 0:TH], ACT.Identity, bias=v_("b_if", rows=4, r0=32)))
            chain(A(r_B, r_f, ACT.Abs))
            chain(A(r_B, r_B, ACT.Exp, scale=-1.0))
            A(r_B, r_B, ACT.Ln, bias=1.0).then_inc(S("ml_softplus"), 1)
            evac("e_in", 0, 4, ACT.Copy, zm[:, 0:4, :])
            evac("e_in", 4, 4, ACT.Copy, zm[:, 4:8, :], MHD ** -0.5)
            evac("e_in", 8, 4, ACT.Copy, zm[:, 8:12, :])
            evac("e_in", 12, 4, ACT.Sigmoid, zm[:, 12:16, :])
            with act.Fori(0, 7) as i:
                for s in range(2):
                    act.wait_ge(S("proj_done"), 2 * i + (16 + s + 1))
                    act.wait_ge(S(f"ext_free{s}"), i + 1)
                    to_ext(s, 1).then_inc(FREE[s], 1)
            act.wait_ge(S("ml_rows"), 1)
            for r in (r_s, r_w, r_dec[:, 0:12]):
                A(r, r, ACT.Exp).then_inc(S("ml_exps"), 1)
            A(r_e, r_m, ACT.Exp, scale=-1.0).then_inc(S("ml_exps"), 1)
            for c in range(NCH + 1):
                n, c0 = (L, L * c) if c < NCH else (NSAMP, SEQ)
                act.wait_ge(S("ml_dm"), c + 1)
                dm = Dm[0:n, :, :].rearrange("p a b -> p (a b)")[:, 0:4 * n]
                A(dm, dm, ACT.Exp).then_inc(S("ml_w"), 1)
                act.wait_ge(S("ml_nd"), c + 1)
                A(zm[:, 4:8, c0:c0 + n], bank(4)[:, 0:4 * n].rearrange("p (h n) -> p h n", h=4), ACT.Copy)
                A(r_s[:, c0:c0 + n], bank(5)[0:4, 0:n], ACT.Abs).then_inc(S("ml_outc"), 1)
            head_norm("mn", zm[:, 4:8, :], zm[:, 8:12, :], MHD, EPS)
            act.wait_ge(S("shifted"), 14)
            A(zr[0:64, 12, :], zr[0:64, 12, :], ACT.Tanh).then_inc(S("rw_lora"), 1)
            A(zr[:, 13, :], zr[:, 13, :], ACT.Sigmoid).then_inc(S("rw_lora"), 1)
            for p in range(RP):
                act.wait_ge(S("rw_kk"), p + 1)
                A(AR[:, p, 1, :], AR[:, p, 0, :], ACT.Square).then_inc(S("rw_kksq"), 1)
            act.wait_ge(S("rw_kkrow"), 1)
            A(kkrow, kkrow, ACT.Sqrt).then_inc(S("rw_kksqrt"), 1)
            act.wait_ge(S("sC_written"), 16)
            for q, p in enumerate((1, 2, 3, 0)):
                act.wait_ge(S("rw_gate"), q + 1)
                A(halves(hT[:, 4 + p, :]), pair(p), ACT.Copy).then_inc(S("rw_gatec"), 1)
            for p in range(RP):
                act.wait_ge(S("rw_up"), p + 1)
                if p == 0:
                    act.wait_ge(S("ycat"), 4)
                if p >= 2:
                    act.wait_ge(S("rw_prep"), p - 1)
                    act.wait_ge(S("rw_pool"), p - 1)
                for q, b in ((0, "w0"), (1, "a0")):
                    A(halves(prep[:, q, p % 2, :]), pair(2 * (p % 2) + q), ACT.Sigmoid,
                      bias=v_(b, p)).then_inc(S("rw_sig"), 1)
                act.wait_ge(S("rw_cum"), p + 1)
                A(prep[:, 4, p % 2, :], prep[:, 2, p % 2, :], ACT.Exp, scale=-1.0)
                A(prep[:, 2, p % 2, :], prep[:, 2, p % 2, :], ACT.Exp)
                A(prep[:, 3, p % 2, :], prep[:, 3, p % 2, :], ACT.Exp).then_inc(S("rw_exp"), 1)

            def r1_copy(c):
                if c == NCR:
                    act.wait_ge(S("rs_qt"), 1)
                    A(QT, bank(5)[:, 0:256].rearrange("p (a b) -> p a b", a=4), ACT.Copy).then_inc(S("rk_r1c"), 1)
                act.wait_ge(S("rk_r1"), c + 1)
                A(R1, bank(5)[:, 0:256].rearrange("p (a b) -> p a b", a=4), ACT.Copy).then_inc(S("rk_r1c"), 1)

            def u_copy(c):
                act.wait_ge(S("rk_u"), c + 1)
                A(U, bank(5)[:, 256:512].rearrange("p (a b) -> p a b", a=4), ACT.Copy).then_inc(S("rk_uc"), 1)

            def y_copy(c):
                act.wait_ge(S("rk_y"), c + 1)
                A(yr[:, :, LR * c:LR * c + LR], bank(6)[:, 0:256].rearrange("p (a b) -> p a b", a=4),
                  ACT.Copy).then_inc(S("rk_yc"), 1)

            act.wait_ge(S("rw_prep"), 4)
            act.wait_ge(S("rw_pool"), 4)
            for c in range(NCR + 1):
                if c >= 2:
                    act.wait_ge(S("rk_s"), c - 1)
                for q in range(2):
                    act.wait_ge(S("rk_tok"), 2 * c + q + 1)
                    A(tok[:, c % 2, 2 * q:2 * q + 2, :, :].rearrange("p a b c -> p (a b c)"), bank(4)[:, 0:384],
                      ACT.Copy).then_inc(S("rk_tokc"), 1)
                if c:
                    r1_copy(c - 1)
                    u_copy(c - 1)
                    y_copy(c - 1)
            r1_copy(NCR)
            u_copy(NCR)
            y_copy(NCR)
            head_norm("rn", yr, AR[:, :, 0, :], RHD, RWKV_EPS)
            split_h("e_out")
            norm(1)
            act.wait_ge(S("out_written"), 16 * 4)
            split_h("ffn0")
            ffn(0)
            odd_act(act, A, chain, norm, evac, head_norm, split_h)
            norm(3)
            split_h("ffn1")
            ffn(1)
            norm(4)

        @block.vector
        def _(dve):
            V = nc.vector
            chain = Chain(dve, S("dve_chain"))

            def norm(n, vname, k0):
                dve.wait_ge(S("rstd_ready"), n + 1)
                for k in range(KT):
                    normed(n, vname, k0, k)

            def normed(n, vname, k0, k):
                stt(hT[:, k, :], xT[:, k, :], v_(vname, k0 + k), rstd[:, :], ALU.mult,
                    ALU.mult).then_inc(S("h_ready"), 1)

            def low(name, k):
                dve.wait_ge(S("h_hi"), 8 * SPLIT[name] + k + 1)
                tt(V, hT_r[:, k, :], hT[:, k, :], H_HI[name][k], ALU.subtract).then_inc(S("h_lo"), 1)

            def norm_split(n, vname, k0, name):
                dve.wait_ge(S("rstd_ready"), n + 1)
                for k in range(KT + 1):
                    if k < KT:
                        normed(n, vname, k0, k)
                    if k:
                        low(name, k - 1)

            def split_h(name):
                for k in range(KT):
                    low(name, k)

            def residual(name):
                with dve.Fori(0, 4) as i:
                    for s in range(2):
                        dve.wait_ge(S("proj_done"), 2 * i + (USE[name] + s + 1))
                        x = xT[:, bass.ds(2 * i + s, 1), :].rearrange("p a n -> p (a n)")
                        tt(V, halves(x), pair(s), halves(x), ALU.add).then_inc(FREE[s], 1)

            def head_norm(nm, src, sqs, n, mean=True):
                if mean:
                    for h in range(4):
                        dve.wait_ge(S("hn_mean"), HN[nm] + h + 1)
                        stt(halves(src[:, h, :]), pair(h), -1.0 / n, halves(src[:, h, :]), ALU.mult,
                            ALU.add).then_inc(S("hn_xc"), 1)
                for h in range(4):
                    dve.wait_ge(S("hn_std"), HN[nm] + h + 1)
                    chain(tt(V, src[:, h, :], src[:, h, :], sqs[:, h, :], ALU.mult))

            def conv_pair(l, i):
                base = USE[f"ffn{l}"] // 2
                for s in range(2):
                    dve.wait_ge(FREE[s], i + (base + 2))
                    e = ext[:, s, :]
                    samp = e[:, 2 + SEQ:2 + SEQ + 80].rearrange("p (j n) -> p j n", j=8)
                    par = convp[:, l, :].rearrange("p (t s k) -> p t s k", s=2, k=4)[
                        :, bass.ds(i, 1), s, :].rearrange("p a k -> p (a k)")
                    cin = convin.rearrange("p (t s) k -> p t s k", s=2)[:, bass.ds(i, 1), s, :].rearrange(
                        "p a k -> p (a k)").rearrange("p (j n) -> p j n", j=8)
                    cout = convout.rearrange("p (t s) k -> p t s k", s=2)[:, bass.ds(i, 1), s, :].rearrange(
                        "p a k -> p (a k)")
                    chain(V.tensor_copy(samp[:, :, 0:2], cin))
                    c = cv[:, s, :]
                    cs = c[:, SEQ:T].rearrange("p (j n) -> p j n", j=8)
                    V.tensor_scalar(c[:, 0:SEQ], e[:, 0:SEQ], par[:, 0:1], par[:, 3:4], ALU.mult, ALU.add)
                    chain(V.tensor_scalar(cs, samp[:, :, 0:8], par[:, 0:1], par[:, 3:4], ALU.mult, ALU.add))
                    for k in (1, 2):
                        stt(c[:, 0:SEQ], e[:, k:k + SEQ], par[:, k:k + 1], c[:, 0:SEQ], ALU.mult, ALU.add)
                        ins = stt(cs, samp[:, :, k:k + 8], par[:, k:k + 1], cs, ALU.mult, ALU.add)
                        if k == 1 or s == 0:
                            chain(ins)
                        else:
                            ins.then_inc(S("gate_conv"), 1)
                    V.tensor_copy(cout[:, 0:2], e[:, SEQ:SEQ + 2])
                    V.tensor_copy(cout[:, 2:18].rearrange("p (j n) -> p j n", j=8),
                                  samp[:, :, 8:10]).then_inc(S(f"ext_free{s}"), 1)
                dve.wait_ge(S("silu_done"), i + (1 + FT * l))
                out = actv[:, bass.ds(i, 1), :].rearrange("p a n -> p (a n)")
                tt(V, out, cv[:, 0, :], cv[:, 2, :], ALU.mult).then_inc(S("act_ready"), 1)

            def ffn(l):
                chain(V.memset(ext[:, :, 0:2], 0.0))
                dve.wait_ge(S("convin_in"), 16 * (l + 1))
                for first, end in ((0, AHEAD), (AHEAD, FT)):
                    with dve.Fori(first, end) as i:
                        chain.loop(i, 7, first)
                        conv_pair(l, i)
                        if end == AHEAD:
                            dve.wait_ge(S("act_hi"), i + (1 + FT * l))
                            lo, x, hi = (v[:, bass.ds(i + o, 1), :].rearrange("p a n -> p (a n)")
                                         for v, o in ((act_lo, 0), (actv, 0), (act_hi, KT)))
                            tt(V, lo, x, hi, ALU.subtract).then_inc(S("act_lo"), 1)
                        chain.end_loop(end - first)
                for k in range(AHEAD, FT):
                    dve.wait_ge(S("act_hi"), k + 1 + FT * l)
                    tt(V, act_lo[:, k, :], actv[:, k, :], act_hi[:, k - AHEAD, :],
                       ALU.subtract).then_inc(S("act_lo"), 1)

            def mlstm_rows():
                dve.wait_ge(S("consts_in"), 16)
                dve.wait_ge(S("ml_softplus"), 1)
                chain(stt(r_f, r_f, 0.0, r_B, ALU.min, ALU.subtract))
                chain(V.tensor_tensor_scan(r_B, c_("scan128", T, 4), r_f, 0.0, ALU.mult, ALU.add))
                dve.wait_ge(S("e_small_in"), 80)
                sf, si = r_a[:, 0:64], r_s[:, 0:64]
                chain(V.tensor_copy(sf, r_f[:, SEQ:T]))
                chain(V.tensor_copy(si, r_i[:, SEQ:T]))
                f8, i8 = (x.rearrange("p (j n) -> p j n", j=8)[:, :, 0] for x in (sf, si))
                chain(tt(V, f8, f8, r_m0[:, 0:8], ALU.add))
                chain(tt(V, i8, i8, f8, ALU.max))
                chain(V.memset(f8, NEG))
                chain(V.tensor_tensor_scan(r_m[:, 0:SEQ], r_f[:, 0:SEQ], r_i[:, 0:SEQ], M_INIT, ALU.add, ALU.max))
                chain(V.tensor_tensor_scan(r_m[:, SEQ:T], sf, si, NEG, ALU.add, ALU.max))
                chain(tt(V, r_i, r_i, r_B, ALU.subtract))
                chain(tt(V, r_a, r_B, r_m, ALU.subtract))
                m_s = r_m[:, SEQ:T].rearrange("p (j n) -> p j n", j=8)[:, :, 7]
                chain(V.memset(r_mp[:, 0:1], M_INIT))
                m_p = r_m[:, 0:SEQ].rearrange("p (c n) -> p c n", n=L)[:, :, L - 1]
                chain(V.tensor_copy(r_mp[:, 1:NCH], m_p[:, 0:NCH - 1]))
                chain(V.tensor_copy(r_mp[:, NCH:NCH + 8], r_m0[:, 0:8]))
                chain(V.tensor_copy(r_rl[:, 0:NCH], r_a[:, 0:SEQ].rearrange("p (c n) -> p c n", n=L)[:, :, L - 1]))
                chain(V.tensor_copy(r_rl[:, NCH:NCH + 8],
                                    r_a[:, SEQ:T].rearrange("p (j n) -> p j n", j=8)[:, :, 7]))
                for dst, src, add in ((r_s, r_a, r_mp), (r_w, r_i, r_rl)):
                    tt(V, dst[:, 0:SEQ].rearrange("p (c n) -> p c n", n=L), src[:, 0:SEQ].rearrange(
                        "p (c n) -> p c n", n=L), bc(add[:, 0:NCH], 2, L), ALU.add)
                    tt(V, dst[:, SEQ:T].rearrange("p (j n) -> p j n", j=8), src[:, SEQ:T].rearrange(
                        "p (j n) -> p j n", j=8), bc(add[:, NCH:NCH + 8], 2, 8), ALU.add)
                tt(V, r_dec[:, 0:12], r_rl[:, 0:12], r_mp[:, 0:12], ALU.add).then_inc(S("ml_rows"), 1)
                V.tensor_copy(r_mo[:, 0:1], r_m[:, SEQ - 1:SEQ])
                V.tensor_copy(r_mo[:, 1:9], m_s).then_inc(S("ml_rows"), 1)

            def token_shift():
                dve.wait_ge(S("e_small_in"), 80)
                chain(V.memset(ext[:, :, 0:1], 0.0))
                for s in range(2):
                    dve.sem_inc(S(f"ext_free{s}"), 1)
                tmp = sq
                with dve.Fori(0, 7) as i:
                    chain.loop(i, 4)
                    for s in range(2):
                        dve.wait_ge(FREE[s], i + (8 + 2))
                        e = ext[:, s, :]
                        samp = e[:, 1 + SEQ:1 + SEQ + 72].rearrange("p (j n) -> p j n", j=8)
                        k = 2 * i + s
                        sin = shin[:, bass.ds(k, 1), :].rearrange("p a n -> p (a n)")
                        so = shout[:, bass.ds(k, 1), :].rearrange("p a n -> p (a n)")
                        mu = vec[:, bass.ds(k + VEC["mu"], 1)]
                        z = zr[:, bass.ds(k, 1), :].rearrange("p a n -> p (a n)")
                        chain(V.tensor_copy(samp[:, :, 0], sin))
                        d1 = tmp[:, s, :]
                        tt(V, d1[:, 0:SEQ], e[:, 0:SEQ], e[:, 1:SEQ + 1], ALU.subtract)
                        chain(tt(V, d1[:, SEQ:T].rearrange("p (j n) -> p j n", j=8), samp[:, :, 0:8],
                                 samp[:, :, 1:9], ALU.subtract))
                        stt(z[:, 0:SEQ], d1[:, 0:SEQ], mu, e[:, 1:SEQ + 1], ALU.mult, ALU.add)
                        stt(z[:, SEQ:T].rearrange("p (j n) -> p j n", j=8),
                            d1[:, SEQ:T].rearrange("p (j n) -> p j n", j=8), mu, samp[:, :, 1:9], ALU.mult,
                            ALU.add).then_inc(S("shifted"), 1)
                        V.tensor_copy(so[:, 0:1], e[:, SEQ:SEQ + 1])
                        V.tensor_copy(so[:, 1:9], samp[:, :, 8]).then_inc(S(f"ext_free{s}"), 1)
                    chain.end_loop(7)

            def mlstm():
                for h in range(MH):
                    dve.wait_ge(S("ml_bcast"), h + 1)
                    tt(V, halves(qh[:, h, :]), halves(zm[:, h, :]), pair(h % 2), ALU.mult).then_inc(S("ml_qh"), 1)
                dve.wait_ge(S("ml_qh"), 4)
                dve.wait_ge(S("ml_small"), 1)
                V.tensor_copy(decb.rearrange("p a b -> p (a b)"), bank(4)[:, 0:48])
                V.tensor_copy(wlc[:, 0:NCH, :].rearrange("p a b -> p (a b)"), bank(4)[:, 48:48 + 4 * NCH])
                V.tensor_copy(wlc[0:64, NCH, :], bank(4)[0:64, 48 + 4 * NCH:52 + 4 * NCH])
                V.memset(vaug[:, :, 128:129], 1.0)
                chain(V.memset(Cst, 0.0))
                for c in range(NCH + 1):
                    n, c0 = (L, L * c) if c < NCH else (NSAMP, SEQ)
                    dm, at_ = (x[0:n, :, :].rearrange("p a b -> p (a b)")[:, 0:4 * n].rearrange(
                        "p (h n) -> p h n", h=4) for x in (Dm, att))
                    if c == NCH:
                        at_ = att[0:n, :, 0:n]
                    neg = c_("mneg", 128) if c < NCH else c_("mneg_s", 64, 64)
                    dve.wait_ge(S("ml_scores"), c + 1)
                    tt(V, dm, bank(1)[0:n, 0:4 * n].rearrange("p (h n) -> p h n", h=4), bc(neg, 1, 4),
                       ALU.add).then_inc(S("ml_dm"), 1)
                    q = qh[:, :, c0:c0 + n]
                    if c < NCH:
                        tt(V, qn, q, bc(Cst[:, :, 128], 2, L), ALU.mult).then_inc(S("ml_qn"), 1)
                    else:
                        dve.wait_ge(S("C_in"), 16)
                        tt(V, qn[:, :, 0:n].rearrange("p h (j n) -> p h j n", j=8),
                           q.rearrange("p h (j n) -> p h j n", j=8), bc(Cs[:, :, :, 128], 3, 8),
                           ALU.mult).then_inc(S("ml_qn"), 1)
                    dve.wait_ge(S("ml_w"), c + 1)
                    tt(V, at_, bank(0)[0:n, 0:4 * n].rearrange("p (h n) -> p h n", h=4), dm,
                       ALU.mult).then_inc(S("ml_att"), 1)
                    dve.wait_ge(S("ml_tok"), c + 1)
                    vt = V.tensor_copy(vaug[0:n, :, 0:128], bank(2)[0:n, :].rearrange("p (h n) -> p h n", h=4))
                    kp = bank(3)[0:n, :].rearrange("p (h n) -> p h n", h=4)
                    if c < NCH:
                        tt(V, ktok, kp, bc(wlc[:, c, :], 2, 128), ALU.mult).then_inc(S("ml_tokc"), 1)
                        dve.wait_ge(S("ml_upd"), c + 1)
                        for h in range(MH):
                            last = stt(Cst[:, h, :], Cst[:, h, :], decb[:, h, c:c + 1],
                                       bank(6 + h // 2)[:, 129 * (h % 2):129 * (h % 2) + 129], ALU.mult, ALU.add)
                        last.then_inc(S("ml_state"), 1)
                        dve.wait_ge(S("ml_state"), c + 1)
                    else:
                        vt.then_inc(S("ml_tokc"), 1)
                        chain(tt(V, wlm[0:64], bc(wlc[0:64, c, :], 2, 8), bc(seqmask[0:64, :], 1, 4), ALU.mult))
                        for h in range(MH):
                            last = tt(V, Km[:, h], bc(kp[:, h, :], 1, 8), bc(wlm[0:64, h, :], 2, 128), ALU.mult)
                        last.then_inc(S("ml_km"), 1)
                        dve.wait_ge(S("ml_outc"), NCH + 1)
                        chain(tt(V, r_s, r_s, r_e, ALU.max))
                        V.reciprocal(r_s, r_s).then_inc(S("ml_den"), 1)
                        chain(tt(V, Cs, Cs, bc(decb[:, :, NCH:NCH + 8], 3, 129), ALU.mult))
                        for g in range(11):
                            e0, e1 = 3 * g, min(3 * g + 3, 32)
                            dve.wait_ge(S("ml_supd"), g + 1)
                            tt(V, Csf[:, e0:e1, :], Csf[:, e0:e1, :], bank(6 + g % 2)[:, 0:129 * (e1 - e0)].rearrange(
                                "p (a b) -> p a b", b=129), ALU.add).then_inc(S("ml_sst"), 1)
                for h in range(MH):
                    dve.wait_ge(S("ml_emt"), h + 1)
                    tt(V, halves(zm[:, 4 + h, :]), halves(zm[:, 4 + h, :]), pair(h),
                       ALU.mult).then_inc(S("hn_src"), 1)
                dve.wait_ge(S("hn_src"), 4)
                head_norm("mn", zm[:, 4:8, :], zm[:, 8:12, :], MHD)
                dve.wait_ge(S("sC_written"), 16)
                for h in range(MH):
                    stt(hT[:, h, :], zm[:, 4 + h, :], v_("ln_m_g", h), zm[:, 12 + h, :], ALU.mult,
                        ALU.mult).then_inc(S("ycat"), 1)

            def rwkv_prep():
                chain(V.tensor_scalar(omka, vec[:, VEC["k_a"]:VEC["k_a"] + 4], -1.0, 1.0, ALU.mult, ALU.add))
                dve.wait_ge(S("ycat"), 4)
                for p in range(RP):
                    V.tensor_scalar(AR[:, p, 0, :], zr[:, 4 + p, :], v_("k_k", p), None,
                                    ALU.mult).then_inc(S("rw_kk"), 1)
                dve.wait_ge(S("rw_kkn"), 1)
                V.tensor_scalar(halves(kkrow), PP[0][64:72, :, 0:TH], 1e-24, None, ALU.max).then_inc(
                    S("rw_kkrow"), 1)
                dve.wait_ge(S("rw_kksqrt"), 1)
                V.reciprocal(kkrow, kkrow).then_inc(S("rw_kkrow"), 1)
                for p in range(RP):
                    dve.wait_ge(S("rw_kkn"), p + 2)
                    tt(V, halves(AR[:, p, 0, :]), halves(AR[:, p, 0, :]), pair(p), ALU.mult).then_inc(
                        S("rw_kkrow"), 1)
                dve.wait_ge(S("rw_kkrow"), 6)
                for p in range(RP):
                    ld, a, cum, ex, em = (prep[:, k, p % 2, :] for k in range(5))
                    dve.wait_ge(S("rw_sig"), 2 * p + 2)
                    chain(V.tensor_scalar(ld, ld, -float(np.exp(-0.5)), None, ALU.mult))
                    chain(V.tensor_tensor_scan(cum, c_("scan64", T), ld, 0.0, ALU.mult, ALU.add))
                    tt(V, ex, cum, ld, ALU.subtract).then_inc(S("rw_cum"), 1)
                    kk, r, kr = AR[:, p, 0, :], zr[:, p, :], zr[:, 4 + p, :]
                    chain(tt(V, BK[:, p, 0, :], kk, a, ALU.mult))
                    chain(V.tensor_scalar(a, a, v_("k_a", p), omka[:, p:p + 1], ALU.mult, ALU.add))
                    chain(tt(V, a, a, kr, ALU.mult))
                    chain(stt(rkp[:, p, :], r, v_("r_k", p), a, ALU.mult, ALU.mult))
                    dve.sem_inc(S("rw_k"), 1)
                    dve.wait_ge(S("rw_exp"), p + 1)
                    chain(V.tensor_copy(PL[:, p, 0:8], cum[:, 0:SEQ].rearrange("p (c n) -> p c n", n=LR)[:, :, LR - 1]))
                    chain(V.tensor_copy(PL[:, p, 8:16], cum[:, SEQ:T].rearrange("p (c n) -> p c n", n=8)[:, :, 7]))
                    stt(kk, kk, -1.0, ex, ALU.mult, ALU.mult).then_inc(S("rw_prep"), 1)

            def rwkv():
                V.memset(Sr, 0.0).then_inc(S("rk_st"), 1)

                def gate(c):
                    if c >= 2:
                        dve.wait_ge(S("rk_y"), c - 1)
                    m = c_("rk" if c < NCR else "rk_s", 320)
                    for p in range(RP):
                        dve.wait_ge(S("rk_sc"), 4 * c + p + 1)
                        tt(V, Gs[:, c % 2, p, :], bank(p % 2)[:, 0:320], m, ALU.mult).then_inc(S("rk_g"), 1)
                    dve.wait_ge(S("rk_g"), 4 * c + 4)

                def level(c, k):
                    top = 5 if c < NCR else 2
                    for q in range(2):
                        b = PP[1][:, q, 0:384].rearrange("p (a k n) -> p a k n", a=2, k=3)
                        new = XPA[:, q, (k + 1) % 2]
                        dve.wait_ge(S(f"rk_lv{q}"), 6 * c + k + 1)
                        if k == 0:
                            tt(V, new[:, :, 1, :], Gs[:, c % 2, 2 * q:2 * q + 2, 0:64],
                               bc(c_("idpair", 64), 1, 2), ALU.add)
                        else:
                            dst = new[:, :, 1, :] if k < top else PF[:, c % 2, 2 * q:2 * q + 2, :]
                            last = tt(V, dst, XPA[:, q, k % 2, :, 1, :], b[:, :, 1, :], ALU.add)
                        if k < top:
                            last = V.tensor_copy(new[:, :, 0:3:2, :], b[:, :, 0:3:2, :])
                        last.then_inc(S(f"rk_lc{q}"), 1)
                        dve.wait_ge(S(f"rk_lc{q}"), 6 * c + k + 1)

                def state(c):
                    dve.wait_ge(S("rk_s"), c + 1)
                    chain(tt(V, Sr, Sr, bank(7)[:, 0:256].rearrange("p (a b) -> p a b", a=4), ALU.add))
                    tt(V, Sr, Sr, bc(PL[:, :, c], 2, 64), ALU.mult).then_inc(S("rk_st"), 1)
                    dve.wait_ge(S("rk_st"), c + 2)

                for c in range(NCR + 1):
                    gate(c)
                    for k in range(3):
                        level(c, k)
                    if c:
                        state(c - 1)
                    if c < NCR:
                        for k in (3, 4, 5):
                            level(c, k)
                dve.wait_ge(S("rk_uc"), NCR + 1)
                for p in range(RP):
                    tt(V, UVm[:, 0, p], bc(U[:, p, :], 1, 8), bc(seqmask, 2, 64), ALU.mult)
                    last = tt(V, UVm[:, 1, p], bc(tok[:, NCR % 2, p, 2, :], 1, 8), bc(seqmask, 2, 64), ALU.mult)
                last.then_inc(S("rs_uvm"), 1)
                for p in range(RP):
                    dve.wait_ge(S("rs_s"), p + 1)
                    tt(V, SS[:, p], SS[:, p], bank(p % 2).rearrange("p (j n) -> p j n", j=8),
                       ALU.add).then_inc(S("rs_sc"), 1)
                for p, b in enumerate(BONUS_PAIR):
                    dve.wait_ge(S("rw_bonus"), p + 1)
                    tt(V, halves(rkp[:, p, :]), pair(b), halves(zr[:, 8 + p, :]), ALU.mult).then_inc(S("rw_bonusc"), 1)
                dve.wait_ge(S("rs_sc"), 4)
                tt(V, SS, SS, bc(PL[:, :, 8:16], 3, 64), ALU.mult).then_inc(S("rs_st"), 1)
                for p in range(RP):
                    chain(V.tensor_scalar(rkp[:, p, :], rkp[:, p, :], v_("ln_r_b", p), None, ALU.add))
                dve.wait_ge(S("rk_yc"), NCR + 1)
                dve.sem_inc(S("hn_src"), 4)
                head_norm("rn", yr, AR[:, :, 0, :], RHD)
                for p in range(RP):
                    chain(stt(yr[:, p, :], yr[:, p, :], v_("ln_r_g", p), rkp[:, p, :], ALU.mult, ALU.add))
                    tt(V, hT[:, 4 + p, :], hT[:, 4 + p, :], yr[:, p, :], ALU.mult).then_inc(S("ycat"), 1)

            for s in range(2):
                dve.sem_inc(FREE[s], 1)
            dve.wait_ge(S("x_in1"), 32)
            dve.wait_ge(S("x_in0"), 16)
            dve.wait_ge(S("x_in1"), 32)
            norm_split(0, "norm_mix", 0, "e_in")
            mlstm_rows()
            token_shift()
            mlstm()
            rwkv_prep()
            rwkv()
            split_h("e_out")
            residual("e_out")
            norm_split(1, "norm_ffn", 0, "ffn0")
            ffn(0)
            residual("down0")
            odd_dve(dve, V, chain, norm_split, residual, head_norm, split_h)
            norm_split(3, "norm_ffn", 8, "ffn1")
            ffn(1)
            residual("down1")
            norm(4, "norm_final", 0)


def _tiles(w):
    k, n = w.shape
    return w.reshape(k // P, P, n // P, P).transpose(2, 1, 0, 3).reshape(n // P, P, k)


def _cols(v):
    return v.reshape(-1, P).T


def _pairs(w):
    return w.reshape(w.shape[0], 2, FT, P).transpose(0, 2, 1, 3).reshape(w.shape[0], -1)


def host_arrays(x_prompt, x_sample, state_mlstm_C, state_mlstm_n, state_mlstm_m, state_rwkv_S, state_rwkv_shift,
                state_gla_S, state_s5_re, state_s5_im, state_ffn_conv, norm_mix, norm_ffn, norm_final,
                e_w_in, e_b_if, e_mu, e_w0, e_w_up, e_a0, e_a_up, e_g_up, e_k_k, e_k_a, e_r_k,
                e_ln_m_g, e_ln_r_g, e_ln_r_b, e_w_out, o_w_in, o_a_up, o_a_b, o_ln_g, o_lam_re, o_lam_im,
                o_log_step, o_b_re, o_b_im, o_c_re, o_c_im, o_d, o_w_glu, o_w_out,
                f_w_up, f_conv_w, f_conv_b, f_w_down):
    d = {}
    x = np.concatenate([x_prompt.reshape(SEQ, D_MODEL), x_sample.reshape(NSAMP, D_MODEL)])
    d["x"] = x.T.reshape(KT, P, T).transpose(1, 0, 2)
    d["consts"] = shape_constants()
    w = e_w_in[0]
    m4 = 4 * HALF
    wo = o_w_in[0]
    w_list = [np.concatenate([w[:, :m4], w[:, m4 + 8:]], 1), e_w_out[0], _pairs(f_w_up[0]),
              np.concatenate([wo[:, :1536], wo[:, 1552:]], 1), o_w_out[0], _pairs(f_w_up[1])]
    d["w"] = np.concatenate([_tiles(a) for a in w_list])
    wif = np.zeros((D_MODEL, 36), np.float32)
    wif[:, 0:4], wif[:, 32:36] = w[:, m4:m4 + 4], w[:, m4 + 4:m4 + 8]
    d["w_if"] = wif.reshape(KT, P, 36).transpose(1, 0, 2)
    d["w_down"] = np.concatenate([_tiles(a) for a in f_w_down])
    vec = np.zeros((P, NVEC), np.float32)

    def put(name, v):
        v = _cols(v)
        vec[:, VEC[name]:VEC[name] + v.shape[1]] = v

    for name, v in (("norm_mix", norm_mix.reshape(-1)), ("norm_ffn", norm_ffn.reshape(-1)), ("norm_final", norm_final),
                    ("mu", e_mu[0]), ("w0", e_w0[0]), ("a0", e_a0[0]), ("k_k", e_k_k[0]), ("k_a", e_k_a[0]),
                    ("r_k", e_r_k[0]), ("ln_m_g", e_ln_m_g[0]), ("ln_r_g", e_ln_r_g[0]), ("ln_r_b", e_ln_r_b[0]),
                    ("a_b", o_a_b[0]), ("o_ln_g", o_ln_g[0]), ("o_d", o_d[0])):
        put(name, v)
    vec[0:4, VEC["b_if"]], vec[32:36, VEC["b_if"]] = e_b_if[0, 0:4], e_b_if[0, 4:8]
    vec[0:64, VEC["sgn"]], vec[64:128, VEC["sgn"]] = -1.0, 1.0
    d["vec"] = vec
    cp = np.concatenate([_pairs(f_conv_w[k]).reshape(3, 2 * FT, P) for k in range(2)]).reshape(2, 3, 2 * FT, P)
    cb = _pairs(f_conv_b).reshape(2, 1, 2 * FT, P)
    d["convp"] = np.concatenate([cp, cb], 1).transpose(3, 0, 2, 1).reshape(P, 2, CONVC)
    cs = np.stack([_pairs(state_ffn_conv[k].reshape(16, -1)) for k in range(2)])
    d["conv_state"] = cs.reshape(2, 16, 2 * FT, P).transpose(0, 3, 2, 1)
    d["shift"] = state_rwkv_shift[0].reshape(8, 14, P).transpose(2, 1, 0)
    d["lora"] = np.stack([np.concatenate([e_w_up[0], e_a_up[0]]), e_g_up[0]], 1)
    d["m0"] = state_mlstm_m[0].T
    C = state_mlstm_C[0].transpose(3, 1, 0, 2)
    n = state_mlstm_n[0].transpose(2, 1, 0)[..., None]
    d["C"] = np.concatenate([C, n], 3).reshape(P, 32, 129)
    d["rS"] = state_rwkv_S[0].reshape(8, 4, 2, 64, 64).transpose(2, 4, 1, 0, 3).reshape(P, 4, 8, 64)
    d["w_ad"] = wo[:, 1536:1552].reshape(KT, P, GRANK).transpose(1, 0, 2)
    d["a_up"] = o_a_up[0]
    d["gS"] = state_gla_S[0].reshape(8, 2, 2, GDK, GDV).transpose(2, 3, 1, 0, 4).reshape(P, 2, 8, GDV)
    lam = [np.concatenate([a.T, a.T]) for a in (o_lam_re[0], o_lam_im[0])]
    d["s5_lam"] = np.stack(lam + [np.broadcast_to(o_log_step[0], (P, SG))], 1)
    b = [a[0].transpose(1, 0, 2) for a in (o_b_re, o_b_im)]
    c = [a[0].transpose(2, 0, 1) for a in (o_c_re, o_c_im)]
    d["s5_bc"] = np.stack([np.concatenate(x) for x in (b, b[::-1], c, c[::-1])], 1)
    x0 = [a[0].transpose(2, 1, 0) for a in (state_s5_re, state_s5_im)]
    d["s5_x0"] = np.stack([np.concatenate(x0), np.concatenate(x0[::-1])], 1)
    d["w_glu"] = o_w_glu[0].reshape(4, P, HALF).transpose(1, 0, 2)
    return {k: np.ascontiguousarray(v, dtype=np.float32) for k, v in d.items()}


OUT = {"shift": (P, 14, NSEQ), "m": (4, NSEQ), "pC": (P, 4, 129), "sC": (P, 32, 129), "pS": (P, 4, 64),
       "sS": (P, 4, 8, 64), "conv0": (P, 2 * FT, 18), "y": (P, KT, T),
       "pG": (P, 2, GDV), "sG": (P, 2, 8, GDV), "s5": (P, SG, NSEQ), "conv1": (P, 2 * FT, 18)}


def _tokens(y):
    y = y.transpose(1, 0, 2).reshape(D_MODEL, T).T
    return y[:SEQ].reshape(1, SEQ, D_MODEL), y[SEQ:].reshape(DEC_BATCH, DEC_SEQ, D_MODEL)


def _even_states(r):
    pC, sC = r["pC"], r["sC"].reshape(P, 4, 8, 129)
    sh = r["shift"].transpose(2, 1, 0).reshape(NSEQ, -1)
    m = r["m"].T
    pS = r["pS"].reshape(2, 64, 4, 64).transpose(2, 0, 3, 1).reshape(1, 1, 8, 64, 64)
    sS = r["sS"].reshape(2, 64, 4, 8, 64).transpose(3, 2, 0, 4, 1).reshape(1, 8, 8, 64, 64)
    p = (pC[:, :, :128].transpose(1, 2, 0)[None, None], pC[:, :, 128].T[None, None], m[0][None, None], pS,
         sh[0][None, None])
    s = (sC[:, :, :, :128].transpose(2, 1, 3, 0)[None], sC[:, :, :, 128].transpose(2, 1, 0)[None], m[1:][None], sS,
         sh[1:][None])
    return p, s


def _conv(c):
    return c.reshape(P, FT, 2, NSEQ, 2).transpose(3, 4, 2, 1, 0).reshape(NSEQ, 2, 2 * D_FF)


def kernel(**inputs):
    import concourse.bacc as bacc
    from concourse.bass_utils import run_bass_kernel_spmd as run

    ins = host_arrays(**{k: np.asarray(v) for k, v in inputs.items()})
    nc = bacc.Bacc("TRN2", target_bir_lowering=False, num_devices=1)
    d = {k: nc.dram_tensor(f"in_{k}", v.shape, F32, kind="ExternalInput").ap() for k, v in ins.items()}
    o = {k: nc.dram_tensor(f"out_{k}", v, F32, kind="ExternalOutput").ap() for k, v in OUT.items()}
    program(nc, d, o)
    r = run(nc, [{f"in_{k}": v for k, v in ins.items()}], core_ids=[0]).results[0]
    r = {k: r[f"out_{k}"] for k in OUT}
    p, s = _even_states(r)
    pG = r["pG"].reshape(2, GDK, 2, GDV).transpose(2, 0, 1, 3).reshape(1, 1, GH, GDK, GDV)
    sG = r["sG"].reshape(2, GDK, 2, 8, GDV).transpose(3, 2, 0, 1, 4).reshape(1, 8, GH, GDK, GDV)
    x5 = r["s5"].transpose(2, 1, 0)
    re, im = x5[None, :, :, :SP], x5[None, :, :, SP:]
    conv = np.stack([_conv(r["conv0"]), _conv(r["conv1"])])
    out = (*_tokens(r["y"]), *p, pG, re[:, :1], im[:, :1], conv[:, :1], *s, sG, re[:, 1:], im[:, 1:], conv[:, 1:])
    return tuple(np.ascontiguousarray(a) for a in out)
```
